# Optimizing a Trainium2 kernel written in Bass

```python
import math
import jax, jax.numpy as jnp
from jax import lax
import numpy as np

D_MODEL = 1024
BATCH = 1
SEQ = 512
DEPTH = 1

CHUNK = 64
LOOKBACK_CHUNKS = 8
Q_BLOCK = 128
HEAD_DIM = 64
N_HEADS_A = 8
N_HEADS_B = 8
WIDTH_A = N_HEADS_A * HEAD_DIM
WIDTH_B = N_HEADS_B * HEAD_DIM
REL_CLIP = 128
N_IN = 3 * WIDTH_A + 3 * WIDTH_B + N_HEADS_B + 2 * D_MODEL
_SPLITS = list(np.cumsum([WIDTH_A, WIDTH_A, WIDTH_A, WIDTH_B, WIDTH_B, WIDTH_B,
                          N_HEADS_B, D_MODEL])[:].astype(int))
N_EXPERTS = 64
TOP_K = 8
N_GROUPS = 8
TOPK_GROUPS = 4
EXPERT_FF = 256
SHARED_FF = 256
ROUTED_SCALE = 2.5
EXPERT_BLOCK = 256
EPS = 1e-6
NEG_INF = -1e30

kernel_name = "hybrid_chunked_fox_moe_adaln_trunk"

def rms_norm(x, g):
    xf = x.astype(jnp.float32)
    y = xf * lax.rsqrt(jnp.mean(xf * xf, axis=-1, keepdims=True) + EPS)
    return (y * g.astype(jnp.float32)).astype(x.dtype)

def modulate(h, shift, scale):
    return h * (1.0 + scale[:, None, :]) + shift[:, None, :]

def chunk_band_attention(q, k, v, rel_table):
    B, H, S, dh = q.shape
    n_chunks = S // CHUNK
    pad = LOOKBACK_CHUNKS * CHUNK
    band = pad + CHUNK
    k_pad = jnp.pad(k, ((0, 0), (0, 0), (pad, 0), (0, 0)))
    v_pad = jnp.pad(v, ((0, 0), (0, 0), (pad, 0), (0, 0)))
    qi = jnp.arange(CHUNK)[:, None]
    kj = jnp.arange(band)[None, :]
    rel = qi + pad - kj
    bias = rel_table[:, jnp.clip(rel, -REL_CLIP, REL_CLIP) + REL_CLIP]
    bias = bias.astype(jnp.float32)
    scale = 1.0 / math.sqrt(dh)

    def one_chunk(n):
        start = n * CHUNK
        qn = lax.dynamic_slice_in_dim(q, start, CHUNK, axis=2)
        kn = lax.dynamic_slice_in_dim(k_pad, start, band, axis=2)
        vn = lax.dynamic_slice_in_dim(v_pad, start, band, axis=2)
        s = jnp.einsum('bhqd,bhkd->bhqk', qn, kn).astype(jnp.float32) * scale + bias
        valid = (start - pad + kj) >= 0
        p = jax.nn.softmax(jnp.where(valid, s, NEG_INF), axis=-1)
        return jnp.einsum('bhqk,bhkd->bhqd', p.astype(vn.dtype), vn)

    out = lax.map(one_chunk, jnp.arange(n_chunks))
    return out.transpose(1, 2, 0, 3, 4).reshape(B, H, S, dh)

def forgetting_attention(q, k, v, log_f):
    B, H, S, dh = q.shape
    cum = jnp.cumsum(log_f, axis=-1)
    scale = 1.0 / math.sqrt(dh)
    kpos = jnp.arange(S)[None, :]

    def one_block(i):
        start = i * Q_BLOCK
        qb = lax.dynamic_slice_in_dim(q, start, Q_BLOCK, axis=2)
        cq = lax.dynamic_slice_in_dim(cum, start, Q_BLOCK, axis=2)
        s = jnp.einsum('bhqd,bhkd->bhqk', qb, k).astype(jnp.float32) * scale
        s = s + cq[..., :, None] - cum[..., None, :]
        causal = kpos <= (start + jnp.arange(Q_BLOCK))[:, None]
        p = jax.nn.softmax(jnp.where(causal, s, NEG_INF), axis=-1)
        return jnp.einsum('bhqk,bhkd->bhqd', p.astype(v.dtype), v)

    out = lax.map(one_block, jnp.arange(S // Q_BLOCK))
    return out.transpose(1, 2, 0, 3, 4).reshape(B, H, S, dh)

def hybrid_mixer(h, w_in, b_fgate, qn_a, kn_a, qn_b, kn_b, rel_table, w_proj_a, w_proj_b, w_out):
    B, S, _ = h.shape
    z = h @ w_in
    qa, ka, va, qb, kb, vb, f_raw, ga, gb = jnp.split(z, _SPLITS, axis=-1)

    def heads(u):
        return u.reshape(B, S, -1, HEAD_DIM)

    def to_bhsd(u):
        return u.transpose(0, 2, 1, 3)

    qa = to_bhsd(rms_norm(heads(qa), qn_a))
    ka = to_bhsd(rms_norm(heads(ka), kn_a))
    qb = to_bhsd(rms_norm(heads(qb), qn_b))
    kb = to_bhsd(rms_norm(heads(kb), kn_b))
    ya = chunk_band_attention(qa, ka, to_bhsd(heads(va)), rel_table)
    log_f = jax.nn.log_sigmoid((f_raw + b_fgate).astype(jnp.float32)).transpose(0, 2, 1)
    yb = forgetting_attention(qb, kb, to_bhsd(heads(vb)), log_f)

    def merge_heads(y):
        return y.transpose(0, 2, 1, 3).reshape(B, S, -1)

    ua = merge_heads(ya) @ w_proj_a
    ub = merge_heads(yb) @ w_proj_b
    m = jax.nn.sigmoid(ga) * ua + jax.nn.sigmoid(gb) * ub
    return m @ w_out

def swiglu(t, wg, wu, wd):
    return (jax.nn.silu(t @ wg) * (t @ wu)) @ wd

def routed_experts(t, idx, w, wg, wu, wd):
    T, D = t.shape
    K = idx.shape[1]
    E = wg.shape[0]
    A = T * K
    G = EXPERT_BLOCK
    n_blocks = (A + G - 1) // G + E
    P = n_blocks * G
    flat_e = idx.reshape(-1)
    flat_tok = jnp.repeat(jnp.arange(T, dtype=jnp.int32), K)
    flat_w = w.reshape(-1)
    order = jnp.argsort(flat_e)
    se, stok, sw = flat_e[order], flat_tok[order], flat_w[order]
    counts = jnp.bincount(flat_e, length=E)
    starts = jnp.cumsum(counts) - counts
    padded = ((counts + G - 1) // G) * G
    pends = jnp.cumsum(padded)
    pstarts = pends - padded
    dest = pstarts[se] + (jnp.arange(A) - starts[se])
    buf_tok = jnp.full((P,), T, jnp.int32).at[dest].set(stok)
    buf_w = jnp.zeros((P,), flat_w.dtype).at[dest].set(sw)
    block_e = jnp.minimum(jnp.searchsorted(pends, jnp.arange(n_blocks) * G, side='right'), E - 1)
    t_pad = jnp.concatenate([t, jnp.zeros((1, D), t.dtype)], axis=0)

    def one_block(args):
        tok, e = args
        xb = t_pad[tok]
        return swiglu(xb, wg[e], wu[e], wd[e])

    out = lax.map(one_block, (buf_tok.reshape(n_blocks, G), block_e)).reshape(P, D)
    out = out * buf_w[:, None].astype(out.dtype)
    y = jnp.zeros((T + 1, D), out.dtype).at[buf_tok].add(out)[:T]
    return y.astype(t.dtype)

def moe_ffn(h, w_router, router_bias, wg, wu, wd, wgs, wus, wds):
    B, S, D = h.shape
    t = h.reshape(-1, D)
    T = t.shape[0]
    scores = jax.nn.sigmoid((t @ w_router).astype(jnp.float32))
    biased = scores + router_bias.astype(jnp.float32)
    per_group = N_EXPERTS // N_GROUPS
    grp = lax.top_k(biased.reshape(T, N_GROUPS, per_group), 2)[0].sum(-1)
    gidx = lax.top_k(grp, TOPK_GROUPS)[1]
    gmask = jnp.any(jnp.arange(N_GROUPS)[None, None, :] == gidx[:, :, None], axis=1)
    emask = jnp.repeat(gmask, per_group, axis=1)
    _, idx = lax.top_k(jnp.where(emask, biased, -jnp.inf), TOP_K)
    wsel = jnp.take_along_axis(scores, idx, axis=-1)
    wsel = wsel / jnp.sum(wsel, axis=-1, keepdims=True) * ROUTED_SCALE
    routed = routed_experts(t, idx, wsel, wg, wu, wd)
    shared = swiglu(t, wgs, wus, wds)
    return (routed + shared).reshape(B, S, D)

def setup_inputs(seed: int = 0) -> dict:
    key = jax.random.key(seed)
    ks = jax.random.split(key, 24)
    f32 = jnp.float32

    def nrm(k, shape, scale):
        return jax.random.normal(k, shape, f32) * scale

    L, D = DEPTH, D_MODEL
    return {
        "x": nrm(ks[0], (BATCH, SEQ, D), 1.0),
        "c": nrm(ks[1], (BATCH, D), 1.0),
        "ada_w": nrm(ks[2], (L, D, 6 * D), 0.5 * D ** -0.5),
        "ada_b": nrm(ks[3], (L, 6 * D), 0.02),
        "mix_norm_g": 1.0 + nrm(ks[4], (L, D), 0.05),
        "w_in": nrm(ks[5], (L, D, N_IN), D ** -0.5),
        "b_fgate": jax.random.uniform(ks[6], (L, N_HEADS_B), f32, 1.0, 4.0),
        "qn_a": 1.0 + nrm(ks[7], (L, HEAD_DIM), 0.05),
        "kn_a": 1.0 + nrm(ks[8], (L, HEAD_DIM), 0.05),
        "qn_b": 1.0 + nrm(ks[9], (L, HEAD_DIM), 0.05),
        "kn_b": 1.0 + nrm(ks[10], (L, HEAD_DIM), 0.05),
        "rel_bias": nrm(ks[11], (L, N_HEADS_A, 2 * REL_CLIP + 1), 0.5),
        "w_proj_a": nrm(ks[12], (L, WIDTH_A, D), WIDTH_A ** -0.5),
        "w_proj_b": nrm(ks[13], (L, WIDTH_B, D), WIDTH_B ** -0.5),
        "w_out": nrm(ks[14], (L, D, D), D ** -0.5),
        "ffn_norm_g": 1.0 + nrm(ks[15], (L, D), 0.05),
        "w_router": nrm(ks[16], (L, D, N_EXPERTS), D ** -0.5),
        "router_bias": nrm(ks[17], (L, N_EXPERTS), 0.01),
        "w_gate_e": nrm(ks[18], (L, N_EXPERTS, D, EXPERT_FF), D ** -0.5),
        "w_up_e": nrm(ks[19], (L, N_EXPERTS, D, EXPERT_FF), D ** -0.5),
        "w_down_e": nrm(ks[20], (L, N_EXPERTS, EXPERT_FF, D), EXPERT_FF ** -0.5),
        "w_gate_s": nrm(ks[21], (L, D, SHARED_FF), D ** -0.5),
        "w_up_s": nrm(ks[22], (L, D, SHARED_FF), D ** -0.5),
        "w_down_s": nrm(ks[23], (L, SHARED_FF, D), SHARED_FF ** -0.5),
    }

def reference(x, c, ada_w, ada_b, mix_norm_g, w_in, b_fgate, qn_a, kn_a, qn_b, kn_b, rel_bias,
              w_proj_a, w_proj_b, w_out, ffn_norm_g, w_router, router_bias,
              w_gate_e, w_up_e, w_down_e, w_gate_s, w_up_s, w_down_s):
    c_act = jax.nn.silu(c)
    for l in range(DEPTH):
        mod = c_act @ ada_w[l] + ada_b[l]
        sh1, sc1, g1, sh2, sc2, g2 = jnp.split(mod, 6, axis=-1)
        h = modulate(rms_norm(x, mix_norm_g[l]), sh1, sc1)
        x = x + g1[:, None, :] * hybrid_mixer(h, w_in[l], b_fgate[l], qn_a[l], kn_a[l], qn_b[l],
                                              kn_b[l], rel_bias[l], w_proj_a[l], w_proj_b[l],
                                              w_out[l])
        h = modulate(rms_norm(x, ffn_norm_g[l]), sh2, sc2)
        x = x + g2[:, None, :] * moe_ffn(h, w_router[l], router_bias[l], w_gate_e[l], w_up_e[l],
                                         w_down_e[l], w_gate_s[l], w_up_s[l], w_down_s[l])
    return x


_drawn_inputs = setup_inputs


def setup_inputs(seed=0):
    import zlib

    import numpy as np

    out = dict(_drawn_inputs(seed))
    spreads = {}
    factors = {'mix_norm_g': 3.594,
     'qn_a': 7.682,
     'kn_a': 8.0,
     'qn_b': 7.954,
     'kn_b': 6.779,
     'rel_bias': 2.778}
    for name, (base, spread) in spreads.items():
        noise = np.random.default_rng([zlib.crc32(name.encode()), seed]).standard_normal(out[name].shape)
        drawn = base * np.exp(spread * noise) if base else spread * noise
        out[name] = __import__('jax').numpy.asarray(drawn.astype(out[name].dtype))
    for name, factor in factors.items():
        out[name] = (out[name] * factor).astype(out[name].dtype)
    return out
```

```python
import contextlib

import numpy as np

import concourse.bass as bass
from concourse import mybir

P = 128
D = 1024
S = 512
DH = 64
HA = 8
NH = 16
NT = S // P
KD = D // P
E = 64
NG = 8
TOPG = 4
TOPK = 8
F = 256
EPS = 1e-6
ROUTED_SCALE = 2.5
REL = 128
NTAB = 2 * REL + 1
EXT = 640
N_ADA = 6 * D
HC = 256
SEG = 512
DA = DH + 2
NBLK = 64 + 36
NEXT = NBLK - E
MAXPAIRS = 48
NEG = -1e30
NOROW = 8192.0
NOTOK = 1024.0

C_ID, C_TEX, C_TIN, C_ONE, C_SLOT = 0, 128, 256, 384, 512
C_TOKG, C_TOKR, C_M, C_E, C_LOW, C_SC, C_NEG1 = 640, 644, 648, 684, 685, 749, 757
C_N = 757 + 128


def constants():
    c = np.zeros((P, C_N), np.float32)
    p = np.arange(P)[:, None]
    f = np.arange(P)[None, :]
    c[:, C_ID:C_ID + P] = p == f
    c[:, C_TEX:C_TEX + P] = p < f
    c[:, C_TIN:C_TIN + P] = p <= f
    c[:, C_ONE:C_ONE + P] = 1.0
    c[:, C_SLOT:C_SLOT + P] = f + 1
    c[:, C_TOKG:C_TOKG + NT] = p + P * np.arange(NT)[None] - NOTOK
    c[:, C_TOKR:C_TOKR + NT] = (p + P * np.arange(NT)[None]) * TOPK - NOROW
    c[:, C_M:C_M + NEXT] = np.arange(NEXT)[None]
    c[:, C_E:C_E + 1] = p
    c[:, C_LOW:C_LOW + 64] = (np.arange(8)[None, :] < np.arange(8)[:, None]).reshape(1, 64)
    c[:, C_SC:C_SC + 3] = [EPS, DH * EPS, 1.0]
    c[:, C_NEG1:C_NEG1 + P] = -1.0
    causal = np.zeros((P, S), np.float32)
    causal[:, S - P:] = np.where(f > p, NEG, 0.0)
    etab = np.zeros((1, NBLK), np.int32)
    etab[0, :E] = np.arange(E)
    return c, causal, etab


def build(nc, a):
    f32, i32 = mybir.dt.float32, mybir.dt.int32
    ALU, ACT, AX = mybir.AluOpType, mybir.ActivationFunctionType, mybir.AxisListType

    st = contextlib.ExitStack()
    with st:
        def sb(name, shape, dt=f32):
            return st.enter_context(nc.sbuf_tensor(name, shape, dt))

        def sem(name):
            return st.enter_context(nc.semaphore(name))

        h2_dram = nc.dram_tensor("h2_rows", (S, D), f32).ap()
        routed_dram = nc.dram_tensor("routed_rows", (S * TOPK, D), f32).ap()
        ext_dram = nc.dram_tensor("bias_rows", (HA, P, EXT), f32).ap()

        cst = sb("cst", [P, C_N])
        X = sb("X", [P, NT, D])
        MOD = sb("MOD", [P, 4, D])
        R_HT = sb("R_HT", [P, 4096])
        R_Z = sb("R_Z", [P, 12288])
        R_G = sb("R_G", [P, 8192])
        R_W = sb("R_W", [P, 8192])
        R_T = sb("R_T", [P, 4608])
        R_S = sb("R_S", [P, 3616])
        R_A = sb("R_A", [P, 1024])

        HT = R_HT[:, :].rearrange("p (k s) -> p k s", k=KD)
        Z = R_Z[:, :].rearrange("p (r t n) -> p r t n", r=3, t=NT)
        G = R_G[:, :].rearrange("p (r t n) -> p r t n", r=2, t=NT)
        WR = R_W[:, :].rearrange("p (b k n) -> p b k n", b=2, k=KD)
        AD = R_T[:, 0:4096].rearrange("p (b k n) -> p b k n", b=2, k=KD)
        CB = R_A[:, :].rearrange("p (k m) -> p k m", k=KD)
        ACC = R_A[:, :].rearrange("p (b n) -> p b n", b=4)
        HROW = R_S[:, 0:2048].rearrange("p (b n) -> p b n", b=2)
        JUNK = R_S[:, 2048:3072]
        SQT = R_S[:, 0:2048].rearrange("p (t n) -> p t n", t=NT)
        GN = R_G[:, 0:2048].rearrange("p (b n) -> p b n", b=2)
        QKT = R_HT[0:DA, 0:2048].rearrange("p (b r s) -> p b r s", b=2, r=2)
        PTS = R_HT[:, 2048:3328]
        TB = R_A[:, :].rearrange("p (b s) -> p b s", b=2)
        T4 = R_T[:, :].rearrange("p (h s) -> p h s", h=9)
        PB = R_S[:, 0:2560].rearrange("p (b s) -> p b s", b=2)
        QS = R_S[:, 2560:3616].rearrange("p (b r t d) -> p b r t d", b=2, r=2, t=NT)
        YT = R_T[:, 0:4096].rearrange("p (k s) -> p k s", k=KD)
        WPA = R_W[:, 0:4096].rearrange("p (k n) -> p k n", k=4)
        WPB = R_W[:, 4096:8192].rearrange("p (k n) -> p k n", k=4)
        MT = HT
        WO = R_Z[:, 0:8192].rearrange("p (k n) -> p k n", k=KD)
        H2T = YT
        WSGU = R_W[:, 0:4096].rearrange("p (k n) -> p k n", k=KD)
        WSD = R_W[:, 4096:6144].rearrange("p (k n) -> p k n", k=2)
        WRT = R_W[:, 6144:6656].rearrange("p (k n) -> p k n", k=KD)
        SILS = R_S[:, 1024:2048].rearrange("p (t n) -> p t n", t=NT)
        ACTS = R_S[:, 2048:3072].rearrange("p (t n) -> p t n", t=NT)
        RX = R_HT[:, 0:1200].rearrange("p (j t c) -> p j t c", j=NBLK, t=NT)
        PM = R_HT[:, 1200:1600].rearrange("p (j t) -> p j t", j=NBLK)

        def tab(at):
            return R_HT[:, at:at + 256].rearrange("p (t e) -> p t e", t=NT)
        SC, BI, MB, RP, SEL, WT, Q1, RV = (tab(1600 + 256 * n) for n in range(8))
        M8 = R_HT[:, 3648:3904].rearrange("p (g v) -> p g v", g=32)
        GT = R_HT[:, 3136:3392].rearrange("p (t g u) -> p t g u", t=NT, g=NG)
        GE = R_HT[:, 3392:3648].rearrange("p (t g u) -> p t g u", t=NT, g=NG)
        Q1T, WTT, RVT = R_A[0:E, 0:512], R_A[0:E, 512:1024], R_S[0:E, 3072:3584]
        WX = R_Z[:, :].rearrange("p (b n) -> p b n", b=2)
        WGU = [WX[:, b, 0:4096].rearrange("p (k n) -> p k n", k=KD) for b in range(2)]
        WDN = [WX[:, b, 4096:6144].rearrange("p (k n) -> p k n", k=2) for b in range(2)]
        XG = R_G[:, 0:2048].rearrange("p (b n) -> p b n", b=2)
        XT = R_G[:, 2048:4096].rearrange("p (b k s) -> p b k s", b=2, k=KD)
        SIL = R_G[:, 4096:4608].rearrange("p (b n) -> p b n", b=2)
        AR = R_G[:, 4608:5120].rearrange("p (b n) -> p b n", b=2)
        AT = R_G[:, 5120:5632].rearrange("p (b k s) -> p b k s", b=2, k=2)
        OB = R_G[:, 5632:7680].rearrange("p (b n) -> p b n", b=2)
        AH = R_S[:, 0:1024].rearrange("p (b t s) -> p b t s", b=2, t=NT)
        FB = [R_W[:, :], R_Z[:, 0:8192], R_G[:, :], R_W[:, :]]

        cact = sb("cact", [P, KD])
        craw = sb("craw", [P, KD])
        ssx = sb("ssx", [P, 12])
        QKG = sb("QKG", [P, 2, 2, DH])
        RQ = sb("RQ", [P, 2, NT, NH])
        bfg = sb("bfg", [P, HA])
        rbias = sb("rbias", [P, E])
        tabr = R_Z[0:HA, 11000:11000 + NTAB]
        extr = R_Z[0:HA, 11300:11300 + EXT]
        WF = sb("WF", [P, KD, HA])
        FZ = sb("FZ", [P, 4, NT, HA])
        CUM = sb("CUM", [P, 2, NT, NH])
        mx = sb("mx", [P, 2, 2, NT])
        sm = sb("sm", [P, 2, 2, NT])
        gs = sb("gs", [P, 5, 32])
        ws = sb("ws", [P, 2, NT])
        V8 = sb("V8", [P, NT, 8])
        ob = sb("ob", [E, 8])
        OH = sb("OH", [E, 3, NEXT])
        etab = sb("etab_sb", [1, NBLK], i32)
        nover = sb("nover", [1, 1], i32)
        slx = sb("slx", [P, 8, 3])
        gidx = [sb(f"gidx{b}", [P, 1], i32) for b in range(2)]
        ridx = [sb(f"ridx{b}", [P, 1], i32) for b in range(2)]
        PS = st.enter_context(nc.psum_tensor("PS", [P, 8, 512], f32))

        ident = cst[:, C_ID:C_ID + P]
        ones = cst[:, C_ONE:C_ONE + P]

        s_cst, s_c, s_x, s_gn, s_qkg, s_small, s_tab, s_modb = map(sem, (
            "cst_loaded", "c_loaded", "x_loaded", "gains_loaded", "qk_gains_loaded", "small_loaded",
            "table_loaded", "mod_bias_loaded"))
        s_modb2, s_wf, s_ext, s_extw, s_t4, s_t4c = map(sem, (
            "mod_bias2_loaded", "wf_loaded", "ext_built", "ext_written", "bias_tiles_loaded", "causal_loaded"))
        s_ada = [sem(f"ada_loaded{b}") for b in range(2)]
        s_w = [sem(f"w_in_loaded{b}") for b in range(2)]
        s_cb = sem("c_spread")
        s_cact, s_acc, s_ones, s_madd, s_mod1, s_mod2 = map(sem, (
            "c_act_ready", "ada_sums_ready", "ada_spread", "mod_added", "mod1_ready", "mod2_ready"))
        s_ssx, s_hrow, s_xpose, s_ht = map(sem, ("x_root_ready", "h_row_ready", "h_transposed", "ht_ready"))
        s_f, s_e, s_lf, s_cum, s_cumr = map(sem, ("f_done", "softplus_part", "log_f_ready", "cum_done", "cum_ready"))
        s_proj, s_zfree, s_ss, s_root, s_norm = map(sem, (
            "proj_done", "proj_evacuated", "qk_squares_ready", "qk_roots_ready", "qk_normed"))
        s_t4m, s_stage, s_tb, s_tq, s_qkev, s_s, s_sred, s_nmx, s_exp = map(sem, (
            "bias_masked", "qk_staged", "bias_staged", "qk_transposed", "qkt_ready", "scores_done",
            "scores_taken", "negmax_ready", "probs_ready"))
        s_pt, s_ptd, s_pta, s_pv, s_y = map(sem, (
            "probs_transposed", "pt_ready_dve", "pt_ready_act", "pv_done", "y_ready"))
        s_yt, s_yted, s_ytea, s_wp, s_u, s_m, s_mt, s_mte, s_wo, s_o, s_x2 = map(sem, (
            "y_transposed", "yt_ready_dve", "yt_ready_act", "w_proj_loaded", "u_done", "m_ready",
            "m_transposed", "mt_ready", "w_out_loaded", "out_done", "x2_ready"))
        s_ss2, s_h2, s_h2t, s_h2te, s_ws, s_rt, s_sc = map(sem, (
            "x2_root_ready", "h2_row_ready", "h2_transposed", "h2t_ready", "shared_loaded",
            "router_done", "scores_ready"))
        s_hb = [sem(f"h2_written{b}") for b in range(2)]
        s_sgu, s_ssil, s_sact, s_sat, s_sate, s_sdn, s_sx = map(sem, (
            "shared_gu_done", "shared_silu_ready", "shared_act_ready", "shared_at_done",
            "shared_at_ready", "shared_down_done", "shared_added"))
        s_sel, s_pos, s_q1, s_ob, s_oend, s_oh1, s_tr, s_trd, s_xm, s_tabs = map(sem, (
            "selected", "positions_done", "slots_ready", "over_counts_ready", "over_ends_done",
            "over_onehot_ready", "tables_transposed", "tables_ready_t", "ext_tables_done", "tables_ready"))
        s_etab = sem("expert_table_loaded")
        s_xgi = sem("gather_buffers_set")
        s_wgu = [sem(f"gate_up_loaded{b}") for b in range(2)]
        s_wd = [sem(f"down_loaded{b}") for b in range(2)]
        s_gat = [sem(f"gathered{b}") for b in range(2)]
        s_scat = [sem(f"scattered{b}") for b in range(2)]
        s_ah, s_ohd, s_sl, s_xt, s_xtd, s_xta, s_gu, s_silu, s_act, s_at, s_ate, s_dn, s_oed, s_oea, s_ri = map(sem, (
            "onehot_ready", "slots_done", "slot_rows_ready", "x_transposed", "xt_ready_dve",
            "xt_ready_act", "gu_done", "silu_ready", "act_ready", "act_transposed", "at_ready",
            "down_done", "o_ready_dve", "o_ready_act", "row_index_ready"))
        s_routed, s_fin, s_out = map(sem, ("all_scattered", "out_ready", "out_written"))
        s_fb = [sem(f"final_loaded{b}") for b in range(3)]
        s_idle = sem("idle")
        s_dch, s_ach, s_pch = map(sem, ("dve_chain", "act_chain", "pool_chain"))

        block = st.enter_context(nc.Block())

        def need(eng, s, value):
            if isinstance(value, int) and value <= 0:
                return
            eng.wait_ge(s, value)

        class Chain:
            def __init__(self, eng, s):
                self.eng, self.s, self.base, self.n = eng, s, 0, 0

            def __call__(self, ins):
                self.n += 1
                ins.then_inc(self.s, 1)
                self.eng.wait_ge(self.s, self.base + self.n)

            def enter(self, i, first, per):
                if not isinstance(i, int):
                    self.saved = self.base + self.n
                    self.base, self.n = self.saved + (i - first) * per, 0
                    self.per = per
                else:
                    self.saved = None

            def leave(self, count):
                if self.saved is not None:
                    assert self.n == self.per, self.n
                    self.base, self.n = self.saved + count * self.per, 0

        w_in, ada_w = a["w_in"], a["ada_w"]
        ADA_COLS = ([HC * u for u in range(8)]
                    + [3 * D + HC * u for u in range(8)]
                    + [2 * D + HC * u for u in range(4)] + [5 * D + HC * u for u in range(4)])
        W_COLS = []
        for r in range(3):
            W_COLS += [(0 * 3 + r) * SEG, (1 * 3 + r) * SEG]
        W_COLS += [6 * SEG + HA + SEG * n for n in range(4)]

        def settle(eng):
            eng.sem_inc(s_idle, 1)

        def bc(ap, shape):
            return ap.to_broadcast(shape)

        @block.sync
        def _(sp):
            sp.dma_start(craw[:, :], a["c"].rearrange("o (k p) -> p (o k)", p=P),
                         allow_slow_non_contiguous=True).then_inc(s_c, 16)
            sp.dma_start(cst[:, :], a["consts"]).then_inc(s_cst, 16)

            def load_ada(u):
                if u >= 10:
                    sp.wait_ge(s_acc, u - 9)
                elif u >= 2:
                    sp.wait_ge(s_ones, u - 1)
                sp.dma_start(AD[:, u % 2], ada_w[:, ADA_COLS[u]:ADA_COLS[u] + HC].rearrange(
                    "(k p) n -> p k n", p=P)).then_inc(s_ada[u % 2], 16)

            def load_w(c):
                if c >= 2:
                    sp.wait_ge(s_proj, 4 * (c - 1))
                sp.dma_start(WR[:, c % 2], w_in[:, W_COLS[c]:W_COLS[c] + SEG].rearrange(
                    "(k p) n -> p k n", p=P)).then_inc(s_w[c % 2], 16)

            for u in range(8):
                load_ada(u)
            sp.dma_start(WF[:, :, :], w_in[:, 6 * SEG:6 * SEG + HA].rearrange(
                "(k p) n -> p k n", p=P)).then_inc(s_wf, 16)
            load_w(0)
            load_w(1)
            sp.wait_ge(s_mod1, 1)
            sp.dma_start(MOD[:, 0:2, :], a["ada_b"][3 * D:5 * D].rearrange("(o s d) -> o s d", o=1, s=2)
                         .to_broadcast([P, 2, D])).then_inc(s_modb2, 16)
            sp.dma_start(MOD[:, 2, :], a["ada_b"][2 * D:3 * D].rearrange("(o d) -> o d", o=1)
                         .to_broadcast([P, D])).then_inc(s_modb2, 16)
            sp.dma_start(MOD[:, 3, :], a["ada_b"][5 * D:6 * D].rearrange("(o d) -> o d", o=1)
                         .to_broadcast([P, D])).then_inc(s_modb2, 16)
            for g in range(4):
                for u in range(8 + 4 * g, 12 + 4 * g):
                    load_ada(u)
                load_w(2 + g)
            sp.wait_ge(s_acc, 16)
            sp.wait_ge(s_extw, 16)
            sp.dma_start(T4[:, 0:HA, :], bass.AP(ext_dram.tensor, P - 1, [[EXT - 1, P], [P * EXT, HA], [1, S]]))\
                .then_inc(s_t4, 16)
            sp.dma_start(T4[:, HA, :], a["causal"]).then_inc(s_t4c, 16)
            for c in range(6, 10):
                load_w(c)
            sp.wait_ge(s_proj, 36)
            sp.dma_start(WPA, a["w_proj_a"].rearrange("(k p) n -> p k n", p=P)).then_inc(s_wp, 16)
            sp.wait_ge(s_proj, 40)
            sp.dma_start(WPB, a["w_proj_b"].rearrange("(k p) n -> p k n", p=P)).then_inc(s_wp, 16)
            sp.wait_ge(s_yt, 8)
            sp.dma_start(WO, a["w_out"].rearrange("(k p) n -> p k n", p=P)).then_inc(s_wo, 16)
            sp.wait_ge(s_u, 8)
            sp.dma_start(WRT, a["w_router"].rearrange("(k p) n -> p k n", p=P)).then_inc(s_ws, 16)
            sp.dma_start(WSGU[:, :, 0:F], a["w_gate_s"].rearrange("(k p) n -> p k n", p=P)).then_inc(s_ws, 16)
            sp.dma_start(WSGU[:, :, F:2 * F], a["w_up_s"].rearrange("(k p) n -> p k n", p=P)).then_inc(s_ws, 16)
            sp.dma_start(WSD, a["w_down_s"].rearrange("(k p) n -> p k n", p=P)).then_inc(s_ws, 16)
            for t in range(NT):
                sp.wait_ge(s_h2, t + 1)
                sp.dma_start(h2_dram[P * t:P * (t + 1), :], HROW[:, t % 2]).then_inc(s_hb[t % 2], 16)

            def load_expert(j, b, e):
                need(sp, s_gu, j - 1)
                sp.dma_start(WGU[b][:, :, 0:F], a["w_gate_e"][bass.ds(e, 1)].rearrange(
                    "o (k p) n -> p (o k) n", p=P)).then_inc(s_wgu[b], 16)
                sp.dma_start(WGU[b][:, :, F:2 * F], a["w_up_e"][bass.ds(e, 1)].rearrange(
                    "o (k p) n -> p (o k) n", p=P)).then_inc(s_wgu[b], 16)
                need(sp, s_dn, 2 * (j - 1))
                sp.dma_start(WDN[b], a["w_down_e"][bass.ds(e, 1)].rearrange(
                    "o (k p) n -> p (o k) n", p=P)).then_inc(s_wd[b], 16)

            sp.wait_ge(s_o, 8)
            load_expert(0, 0, 0)
            load_expert(1, 1, 1)
            sp.wait_ge(s_tabs, 1)
            npairs = (sp.value_load(nover[0:1, 0:1], min_val=0, max_val=31) + (E + 1)) // 2
            with sp.Fori(1, MAXPAIRS) as i:
                with sp.If(i < npairs):
                    for b in range(2):
                        e = sp.value_load(etab[0:1, bass.ds(2 * i + b, 1)], min_val=0, max_val=E - 1)
                        load_expert(2 * i + b, b, e)
            sp.wait_ge(s_routed, 1)
            for t in range(NT):
                if t == 3:
                    sp.wait_ge(s_fin, 1)
                sp.dma_start(FB[t], routed_dram[P * TOPK * t:P * TOPK * (t + 1), :].rearrange(
                    "(p k) d -> p (k d)", k=TOPK)).then_inc(s_fb[t % 3], 16)
            for t in range(NT):
                sp.wait_ge(s_fin, t + 1)
                sp.dma_start(a["out"][P * t:P * (t + 1), :], X[:, t, :]).then_inc(s_out, 16)
            sp.wait_ge(s_out, 16 * NT)

        @block.gpsimd
        def _(pool):
            pool.memset(CUM[:, :, :, 0:HA], 0.0).then_inc(s_pch, 1)
            pool.memset(extr[:, :], 0.0).then_inc(s_pch, 1)
            pool.wait_ge(s_tab, 16)
            pool.wait_ge(s_pch, 2)
            pool.tensor_copy(extr[:, 383:383 + 2 * REL], tabr[:, NTAB - 1:0:-1]).then_inc(s_ext, 1)
            pool.tensor_copy(extr[:, 0:383], bc(tabr[:, NTAB - 1:NTAB], [HA, 383])).then_inc(s_ext, 1)
            pool.wait_ge(s_ext, 2)
            pool.dma_start(ext_dram, bc(extr[:, :].unsqueeze(1), [HA, P, EXT])).then_inc(s_extw, 16)
            pool.wait_ge(s_t4, 16)
            pool.memset(T4[0:DH, 0:HA, S - DH:S], NEG).then_inc(s_t4m, 1)
            pool.wait_ge(s_t4m, 1)
            pool.wait_ge(s_t4c, 16)
            pool.wait_ge(s_proj, 40)
            pool.wait_ge(s_norm, 4)
            pool.wait_ge(s_cumr, 2)
            pool.memset(QS[:, :, 0, :, DH + 1:DA], 1.0).then_inc(s_pch, 1)
            pool.memset(QS[:, :, 1, :, DH:DH + 1], 1.0).then_inc(s_pch, 1)
            pool.wait_ge(s_pch, 4)

            def stage(i, b, mixer):
                h = 2 * i + b
                need(pool, s_tq, 2 * h - 2)
                settle(pool)
                pool.tensor_copy(QS[:, b, 0, :, 0:DH], Z[:, 0, :, bass.ds(h * DH, DH)]).then_inc(s_stage, 1)
                pool.tensor_copy(QS[:, b, 1, :, 0:DH], Z[:, 1, :, bass.ds(h * DH, DH)]).then_inc(s_stage, 1)
                pool.tensor_copy(QS[:, b, 0, :, DH:DH + 1], CUM[:, 0, :, bass.ds(h, 1)]).then_inc(s_stage, 1)
                pool.tensor_copy(QS[:, b, 1, :, DH + 1:DA], CUM[:, 1, :, bass.ds(h, 1)]).then_inc(s_stage, 1)
                need(pool, s_sred, 3 * (h - 1))
                settle(pool)
                row = bass.ds(h, 1) if mixer == 0 else bass.ds(HA, 1)
                pool.tensor_copy(TB[:, b, :], T4[:, row, :].rearrange("p o s -> p (o s)")).then_inc(s_tb, 1)

            for b in range(2):
                stage(0, b, 0)
            with pool.Fori(1, HA // 2) as i:
                for b in range(2):
                    stage(i, b, 0)
            with pool.Fori(HA // 2, NH // 2) as i:
                for b in range(2):
                    stage(i, b, 1)

            pool.wait_ge(s_sdn, 8)
            pool.memset(XG[:, 0, :], 0.0).then_inc(s_xgi, 1)
            pool.memset(XG[:, 1, :], 0.0).then_inc(s_xgi, 1)
            pool.wait_ge(s_xgi, 2)
            pool.wait_ge(s_hb[0], 32)
            pool.wait_ge(s_hb[1], 32)

            def gather(j, b):
                pool.wait_ge(s_sl, 2 * j + 2)
                need(pool, s_xt, j - 1)
                settle(pool)
                pool.indirect_dma_start(
                    out=XG[:, b, :], out_offset=None, in_=h2_dram,
                    in_offset=bass.IndirectOffsetOnAxis(ap=gidx[b][:, 0:1], axis=0),
                    bounds_check=S - 1, oob_is_err=False).then_inc(s_gat[b], 16)

            def scatter(j, b):
                pool.wait_ge(s_oed, j + 1)
                pool.wait_ge(s_oea, j + 1)
                pool.wait_ge(s_ri, j + 1)
                settle(pool)
                pool.indirect_dma_start(
                    out=routed_dram, out_offset=bass.IndirectOffsetOnAxis(ap=ridx[b][:, 0:1], axis=0),
                    in_=OB[:, b, :], in_offset=None,
                    bounds_check=S * TOPK - 1, oob_is_err=False).then_inc(s_scat[b], 16)

            for j in range(4):
                gather(j, j % 2)
            npairs = (pool.value_load(nover[0:1, 0:1], min_val=0, max_val=31) + (E + 1)) // 2
            with pool.Fori(0, MAXPAIRS) as i:
                with pool.If(i < npairs):
                    for b in range(2):
                        j = 2 * i + b
                        scatter(j, b)
                        gather(j + 4, b)
            for b in range(2):
                pool.wait_ge(s_scat[b], 16 * npairs)
            for b in range(2):
                pool.wait_ge(s_gat[b], 16 * npairs + 32)
            pool.sem_inc(s_routed, 1)

        @block.scalar
        def _(act):
            link = Chain(act, s_ach)
            act.dma_start(MOD[:, 0:2, :], a["ada_b"][0:2 * D].rearrange("(o s d) -> o s d", o=1, s=2)
                          .to_broadcast([P, 2, D])).then_inc(s_modb, 16)
            act.dma_start(X[:, :, :], a["x"].rearrange("(t p) d -> p t d", p=P)).then_inc(s_x, 16)
            act.dma_start(tabr[:, :], a["rel_bias"]).then_inc(s_tab, 16)
            for n, g in enumerate(("mix_norm_g", "ffn_norm_g")):
                act.dma_start(GN[:, n, :], a[g].rearrange("(o d) -> o d", o=1).to_broadcast([P, D]))\
                    .then_inc(s_gn, 16)
            for n, g in enumerate(("qn_a", "qn_b", "kn_a", "kn_b")):
                act.dma_start(QKG[:, n // 2, n % 2, :], a[g].rearrange("(o d) -> o d", o=1).to_broadcast([P, DH]))\
                    .then_inc(s_qkg, 16)
            act.dma_start(bfg[:, :], a["b_fgate"].rearrange("(o d) -> o d", o=1).to_broadcast([P, HA]))\
                .then_inc(s_small, 16)
            act.dma_start(rbias[:, :], a["router_bias"].rearrange("(o d) -> o d", o=1).to_broadcast([P, E]))\
                .then_inc(s_small, 16)
            act.dma_start(etab[:, :], a["etab"]).then_inc(s_etab, 16)
            act.wait_ge(s_c, 16)
            act.activation(cact[:, :], craw[:, :], ACT.Silu).then_inc(s_cact, 1)
            act.wait_ge(s_x, 16)
            for t in range(NT):
                link(act.activation(JUNK, X[:, t, :], ACT.Square, accum_out=ssx[:, t:t + 1]))
            act.wait_ge(s_cst, 16)
            act.activation(ssx[:, 4:8], ssx[:, 0:4], ACT.Sqrt, scale=1.0 / D, bias=cst[:, C_SC:C_SC + 1])\
                .then_inc(s_ssx, 1)
            for n in range(8):
                act.wait_ge(s_xpose, n + 1)
                act.activation(HT[:, 4 * (n % 2):4 * (n % 2) + 4, P * (n // 2):P * (n // 2) + P],
                               PS[:, 6 + n % 2, :].rearrange("p (k s) -> p k s", k=4), ACT.Copy).then_inc(s_ht, 1)
            act.wait_ge(s_e, 1)
            link(act.activation(FZ[:, 2], FZ[:, 1], ACT.Exp))
            act.activation(FZ[:, 3], FZ[:, 2], ACT.Ln, bias=cst[:, C_SC + 2:C_SC + 3]).then_inc(s_e, 1)

            act.wait_ge(s_extw, 16)
            act.sem_inc(s_zfree, 4)

            def take_qkv(r, half):
                for t in range(NT):
                    act.wait_ge(s_proj, 8 * r + 4 * half + t + 1)
                    act.activation(Z[:, bass.ds(r, 1), t, SEG * half:SEG * (half + 1)].rearrange("p o n -> p (o n)"),
                                   PS[:, t, :], ACT.Copy).then_inc(s_zfree, 1)
            with act.Fori(0, 3) as r:
                for half in range(2):
                    take_qkv(r, half)
            act.wait_ge(s_ss, 4)
            act.activation(RQ[:, 0], RQ[:, 0], ACT.Sqrt, bias=cst[:, C_SC + 1:C_SC + 2]).then_inc(s_root, 1)
            act.activation(RQ[:, 1], RQ[:, 1], ACT.Sqrt, scale=1.0 / DH, bias=cst[:, C_SC:C_SC + 1]).then_inc(s_root, 1)
            act.wait_ge(s_mod2, 1)
            with act.Fori(0, 2) as r:
                for half in range(2):
                    for t in range(NT):
                        act.wait_ge(s_proj, 24 + 8 * r + 4 * half + t + 1)
                        act.activation(G[:, bass.ds(r, 1), t, SEG * half:SEG * (half + 1)].rearrange("p o n -> p (o n)"),
                                       PS[:, t, :], ACT.Sigmoid).then_inc(s_zfree, 1)

            def take_qkt(h, b):
                need(act, s_s, 3 * (h - 1))
                for r in range(2):
                    act.wait_ge(s_tq, 2 * h + 1 + r)
                    act.activation(QKT[:, b, r, :], PS[0:DA, 4 + r, :], ACT.Copy).then_inc(s_qkev, 1)

            def exps(h, b):
                act.wait_ge(s_nmx, h + 1)
                need(act, s_y, h - 1)
                for i in range(NT):
                    at = P * (i * (i + 1) // 2)
                    act.activation(PB[:, b, at:at + P * (i + 1)], PB[:, b, at:at + P * (i + 1)], ACT.Exp,
                                   bias=mx[:, b, 1, i:i + 1], accum_out=sm[:, b, 0, i:i + 1]).then_inc(s_exp, 1)

            def take_pt3(h):
                act.wait_ge(s_pt, 4 * h + 4)
                act.activation(PTS[:, 768:1280], PS[:, 7, :], ACT.Copy).then_inc(s_pta, 1)

            take_qkt(0, 0)
            take_qkt(1, 1)
            exps(0, 0)
            take_qkt(2, 0)
            exps(1, 1)
            take_pt3(0)

            def heads(i):
                for b in range(2):
                    h = 2 * i + 1 + b
                    take_qkt(h + 2, 1 - b)
                    exps(h + 1, b)
                    take_pt3(h)
            heads(0)
            with act.Fori(1, 6) as i:
                heads(i)
            take_qkt(15, 1)
            exps(14, 0)
            take_pt3(13)
            exps(15, 1)
            take_pt3(14)
            take_pt3(15)

            for t in range(NT):
                act.wait_ge(s_yt, 2 * t + 2)
                act.activation(YT[:, 4:8, P * t:P * t + P],
                               PS[:, 5 + 2 * (t % 2), :].rearrange("p (k s) -> p k s", k=4), ACT.Copy).then_inc(s_ytea, 1)
            for n in range(8):
                t = n // 2
                act.wait_ge(s_mt, n + 1)
                act.activation(MT[:, 4 * (n % 2):4 * (n % 2) + 4, P * t:P * t + P],
                               PS[:, 4 + n % 4, :].rearrange("p (k s) -> p k s", k=4), ACT.Copy).then_inc(s_mte, 1)

            def take_h2t(t):
                for n in range(2 * t, 2 * t + 2):
                    act.wait_ge(s_h2t, n + 1)
                    act.activation(H2T[:, 4 * (n % 2):4 * (n % 2) + 4, P * t:P * t + P],
                                   PS[:, 4 + n % 4, :].rearrange("p (k s) -> p k s", k=4), ACT.Copy).then_inc(s_h2te, 1)
            for t in range(NT):
                act.wait_ge(s_x2, 2 * t + 2)
                link(act.activation(G[:, 0, t, :], X[:, t, :], ACT.Square, accum_out=ssx[:, t:t + 1]))
                act.activation(ssx[:, 4 + t:5 + t], ssx[:, t:t + 1], ACT.Sqrt, scale=1.0 / D,
                               bias=cst[:, C_SC:C_SC + 1]).then_inc(s_ss2, 1)
                if t:
                    take_h2t(t - 1)
            take_h2t(NT - 1)
            act.wait_ge(s_rt, 1)
            act.activation(SC, PS[:, 4, 0:256].rearrange("p (t e) -> p t e", t=NT), ACT.Sigmoid).then_inc(s_sc, 1)
            for b in range(2):
                act.wait_ge(s_hb[b], 32)
            for t in range(NT):
                act.wait_ge(s_sgu, t + 1)
                act.activation(SILS[:, t, :], PS[:, t, 0:F], ACT.Silu).then_inc(s_ssil, 1)
            for t in range(NT):
                act.wait_ge(s_sat, t + 1)
                need(act, s_sdn, 2 * (t - 1))
                act.activation(AT[:, t % 2], PS[:, 5, 0:F].rearrange("p (k s) -> p k s", k=2), ACT.Copy)\
                    .then_inc(s_sate, 1)

            def take_xt(j, b):
                act.wait_ge(s_xt, j + 1)
                need(act, s_gu, j - 1)
                act.activation(XT[:, b, 4:8, :], PS[:, 5, :].rearrange("p (k s) -> p k s", k=4), ACT.Copy)\
                    .then_inc(s_xta, 1)

            def silu(j, b):
                act.wait_ge(s_gu, j + 1)
                need(act, s_act, j - 1)
                act.activation(SIL[:, b, :], PS[:, b, 0:F], ACT.Silu).then_inc(s_silu, 1)

            def take_at(j, b):
                act.wait_ge(s_at, j + 1)
                need(act, s_dn, 2 * (j - 1))
                act.activation(AT[:, b], PS[:, 6, 0:F].rearrange("p (k s) -> p k s", k=2), ACT.Copy)\
                    .then_inc(s_ate, 1)

            def take_o(i, j, b):
                act.wait_ge(s_dn, 2 * j + 2)
                need(act, s_scat[b], 16 * i)
                act.activation(OB[:, b, 512:1024], PS[:, 3, :], ACT.Copy,
                               scale=slx[:, bass.ds(j % 8, 1), 2:3].rearrange("p o c -> p (o c)")).then_inc(s_oea, 1)

            take_xt(0, 0)
            take_xt(1, 1)
            silu(0, 0)
            act.wait_ge(s_tabs, 1)
            npairs = (act.value_load(nover[0:1, 0:1], min_val=0, max_val=31) + (E + 1)) // 2

            def blocks(i):
                take_at(2 * i, 0)
                silu(2 * i + 1, 1)
                take_xt(2 * i + 2, 0)
                take_o(i, 2 * i, 0)
                take_at(2 * i + 1, 1)
                with act.If(i + 1 < npairs):
                    silu(2 * i + 2, 0)
                take_xt(2 * i + 3, 1)
                take_o(i, 2 * i + 1, 1)
            blocks(0)
            with act.Fori(1, MAXPAIRS) as i:
                with act.If(i < npairs):
                    blocks(i)

        @block.vector
        def _(dve):
            link = Chain(dve, s_dch)

            def ada_sum(u):
                b = u % 2
                dve.wait_ge(s_ada[b], 16 * (u // 2 + 1))
                dve.wait_ge(s_ones, max(8, u - 3))
                link(dve.tensor_tensor(AD[:, b], AD[:, b], bc(cact[:, :].unsqueeze(2), [P, KD, HC]), ALU.mult))
                dve.tensor_reduce(ACC[:, u % 4], AD[:, b].rearrange("p k n -> p n k"), AX.X, ALU.add).then_inc(s_acc, 1)

            def mod_add(u, at):
                dve.tensor_tensor(MOD[:, at // D, at % D:at % D + HC], MOD[:, at // D, at % D:at % D + HC],
                                  PS[:, 4 + (u % 4) // 2, HC * (u % 2):HC * (u % 2) + HC], ALU.add).then_inc(s_madd, 1)

            dve.wait_ge(s_cact, 1)
            dve.tensor_copy(CB, bc(cact[:, :].unsqueeze(2), [P, KD, P])).then_inc(s_cb, 1)
            dve.wait_ge(s_modb, 16)
            for i in range(4):
                dve.wait_ge(s_ones, 2 * i + 2)
                for b in range(2):
                    mod_add(2 * i + b, HC * (2 * i + b))
            dve.wait_ge(s_madd, 8)
            dve.wait_ge(s_gn, 32)
            dve.wait_ge(s_ssx, 1)
            link(dve.reciprocal(ssx[:, 8:12], ssx[:, 4:8]))
            link(dve.scalar_tensor_tensor(MOD[:, 1, :], MOD[:, 1, :], 1.0, GN[:, 0, :], ALU.add, ALU.mult))
            for t in range(NT):
                if t >= 2:
                    dve.wait_ge(s_xpose, 2 * t - 2)
                link(dve.scalar_tensor_tensor(HROW[:, t % 2], X[:, t, :], ssx[:, 8 + t:9 + t], MOD[:, 1, :],
                                              ALU.mult, ALU.mult))
                dve.tensor_tensor(HROW[:, t % 2], HROW[:, t % 2], MOD[:, 0, :], ALU.add).then_inc(s_hrow, 1)
            dve.wait_ge(s_hrow, NT)
            dve.sem_inc(s_mod1, 1)
            dve.wait_ge(s_f, 1)
            dve.wait_ge(s_small, 32)
            link(dve.tensor_tensor(FZ[:, 0], PS[:, 6, 0:32].rearrange("p (t h) -> p t h", t=NT),
                                   bc(bfg[:, :].unsqueeze(1), [P, NT, HA]), ALU.add))
            link(dve.tensor_scalar(FZ[:, 1], FZ[:, 0], -1.0, None, ALU.mult))
            dve.tensor_tensor(FZ[:, 1], FZ[:, 0], FZ[:, 1], ALU.min).then_inc(s_e, 1)
            dve.wait_ge(s_e, 2)
            link(dve.tensor_scalar(FZ[:, 0], FZ[:, 0], 0.0, None, ALU.min))
            dve.tensor_tensor(FZ[:, 0], FZ[:, 0], FZ[:, 3], ALU.subtract).then_inc(s_lf, 1)
            dve.wait_ge(s_modb2, 48)
            for g in range(4):
                for u in range(8 + 4 * g, 12 + 4 * g):
                    ada_sum(u)
                if g:
                    dve.wait_ge(s_ones, 8 + 4 * g)
                    for u in range(4 + 4 * g, 8 + 4 * g):
                        mod_add(u, HC * (u - 8))
            dve.wait_ge(s_ones, 24)
            for u in range(20, 24):
                mod_add(u, HC * (u - 8))
            dve.wait_ge(s_madd, 24)
            dve.scalar_tensor_tensor(MOD[:, 1, :], MOD[:, 1, :], 1.0, GN[:, 1, :], ALU.add, ALU.mult).then_inc(s_mod2, 1)
            dve.wait_ge(s_cum, 1)
            cps = PS[:, 7, 0:32].rearrange("p (t h) -> p t h", t=NT)
            dve.tensor_copy(CUM[:, 0, :, HA:NH], cps).then_inc(s_cumr, 1)
            dve.tensor_scalar(CUM[:, 1, :, HA:NH], cps, -1.0, None, ALU.mult).then_inc(s_cumr, 1)
            dve.wait_ge(s_qkg, 64)

            def qk(r, half):
                return Z[:, r, :, SEG * half:SEG * (half + 1)].rearrange("p t (h d) -> p t h d", h=HA)
            for r in range(2):
                for half in range(2):
                    dve.wait_ge(s_zfree, 4 + 8 * r + 4 * half + 4)
                    link(dve.tensor_tensor(SQT, Z[:, r, :, SEG * half:SEG * (half + 1)],
                                           Z[:, r, :, SEG * half:SEG * (half + 1)], ALU.mult))
                    link(dve.tensor_reduce(RQ[:, r, :, HA * half:HA * (half + 1)],
                                           SQT.rearrange("p t (h d) -> p t h d", h=HA), AX.X, ALU.add))
                    dve.sem_inc(s_ss, 1)
            dve.wait_ge(s_root, 2)
            link(dve.reciprocal(RQ[:, :, :, :].rearrange("p r t h -> p (r t h)"),
                                RQ[:, :, :, :].rearrange("p r t h -> p (r t h)")))
            for r in range(2):
                for half in range(2):
                    link(dve.tensor_tensor(qk(r, half), qk(r, half), bc(
                        RQ[:, r, :, HA * half:HA * (half + 1)].unsqueeze(3), [P, NT, HA, DH]), ALU.mult))
                    dve.tensor_tensor(qk(r, half), qk(r, half), bc(
                        QKG[:, r, half, :].unsqueeze(1).unsqueeze(1), [P, NT, HA, DH]), ALU.mult).then_inc(s_norm, 1)

            def take_scores(h, b):
                dve.wait_ge(s_tb, h + 1)
                need(dve, s_pt, 4 * (h - 1))
                for g, tiles in enumerate(((0, 2), (1,), (3,))):
                    dve.wait_ge(s_s, 3 * h + g + 1)
                    settle(dve)
                    for n, i in enumerate(tiles):
                        w, at = P * (i + 1), P * (i * (i + 1) // 2)
                        src = P if i == 2 else 0
                        ins = dve.tensor_tensor_reduce(
                            out=PB[:, b, at:at + w], in0=PS[:, g, src:src + w], in1=TB[:, b, S - w:S],
                            scale=1.0, scalar=-3e38, op0=ALU.add, op1=ALU.max, accum_out=mx[:, b, 0, i:i + 1])
                    ins.then_inc(s_sred, 1)
                dve.wait_ge(s_sred, 3 * h + 3)
                dve.tensor_scalar(mx[:, b, 1, :], mx[:, b, 0, :], -1.0, None, ALU.mult).then_inc(s_nmx, 1)

            def take_pt(h, i):
                dve.wait_ge(s_pt, 4 * h + i + 1)
                at = P * (i * (i + 1) // 2)
                dve.tensor_copy(PTS[:, at:at + P * (i + 1)], PS[:, 6 + i % 2, 0:P * (i + 1)]).then_inc(s_ptd, 1)

            def take_y(h, b):
                dve.wait_ge(s_exp, 4 * h + 4)
                link(dve.reciprocal(sm[:, b, 1, :], sm[:, b, 0, :]))
                dve.wait_ge(s_pv, 4 * h + 4)
                dve.tensor_tensor(Z[:, 0, :, bass.ds(h * DH, DH)],
                                  PS[:, 3, 0:256].rearrange("p (t d) -> p t d", t=NT),
                                  bc(sm[:, b, 1, :].unsqueeze(2), [P, NT, DH]), ALU.mult).then_inc(s_y, 1)

            take_scores(0, 0)
            take_scores(1, 1)
            for n in range(3):
                take_pt(0, n)

            def heads(i, first):
                link.enter(i, first, 2)
                for b in range(2):
                    h = 2 * i + 1 + b
                    take_scores(h + 1, b)
                    for n in range(3):
                        take_pt(h, n)
                    take_y(h - 1, b)
            heads(0, 0)
            with dve.Fori(1, 7) as i:
                heads(i, 1)
            link.leave(6)
            for n in range(3):
                take_pt(15, n)
            take_y(14, 0)
            take_y(15, 1)

            for t in range(NT):
                dve.wait_ge(s_yt, 2 * t + 1)
                dve.tensor_copy(YT[:, 0:4, P * t:P * t + P],
                                PS[:, 4 + 2 * (t % 2), :].rearrange("p (k s) -> p k s", k=4)).then_inc(s_yted, 1)
            for n in range(8):
                t, cols = n // 2, slice(512 * (n % 2), 512 * (n % 2) + 512)
                dve.wait_ge(s_u, n + 1)
                for r in range(2):
                    link(dve.tensor_tensor(G[:, r, t, cols], G[:, r, t, cols], PS[:, 2 * (n % 2) + r, :], ALU.mult))
                dve.tensor_tensor(G[:, 0, t, cols], G[:, 0, t, cols], G[:, 1, t, cols], ALU.add).then_inc(s_m, 1)

            def h2_rows(t):
                dve.wait_ge(s_ss2, t + 1)
                link(dve.reciprocal(ssx[:, 8 + t:9 + t], ssx[:, 4 + t:5 + t]))
                if t >= 2:
                    dve.wait_ge(s_h2t, 2 * t - 2)
                    dve.wait_ge(s_hb[t % 2], 16)
                link(dve.scalar_tensor_tensor(HROW[:, t % 2], X[:, t, :], ssx[:, 8 + t:9 + t], MOD[:, 1, :],
                                              ALU.mult, ALU.mult))
                dve.tensor_tensor(HROW[:, t % 2], HROW[:, t % 2], MOD[:, 0, :], ALU.add).then_inc(s_h2, 1)

            for n in range(8):
                t, cols = n // 2, slice(512 * (n % 2), 512 * (n % 2) + 512)
                dve.wait_ge(s_o, n + 1)
                link(dve.tensor_tensor(G[:, 1, t, cols], PS[:, n % 4, :], MOD[:, 2, cols], ALU.mult))
                dve.tensor_tensor(X[:, t, cols], X[:, t, cols], G[:, 1, t, cols], ALU.add).then_inc(s_x2, 1)
                if n % 2 and t:
                    h2_rows(t - 1)
            h2_rows(NT - 1)

            dve.wait_ge(s_sc, 1)
            gsum, cnt, gm, ng = (gs[:, n, :].rearrange("p (t g) -> p t g", t=NT) for n in range(4))
            link(dve.tensor_tensor(BI, SC, bc(rbias[:, :].unsqueeze(1), [P, NT, E]), ALU.add))
            for t in range(NT):
                for g in range(NG):
                    ins = dve.max(M8[:, NG * t + g, :], BI[:, t, 8 * g:8 * g + 8])
            link(ins)
            link(dve.tensor_tensor(gs[:, 0, :].unsqueeze(2), M8[:, :, 0:1], M8[:, :, 1:2], ALU.add))
            mine = bc(gsum.unsqueeze(3), [P, NT, NG, NG])
            other = bc(gsum.unsqueeze(2), [P, NT, NG, NG])
            low = bc(cst[:, C_LOW:C_LOW + 64].rearrange("p (g u) -> p g u", g=NG).unsqueeze(1), [P, NT, NG, NG])
            link(dve.tensor_tensor(GE, other, mine, ALU.is_equal))
            link(dve.tensor_tensor(GE, GE, low, ALU.mult))
            link(dve.tensor_tensor(GT, other, mine, ALU.is_gt))
            link(dve.tensor_tensor(GT, GT, GE, ALU.add))
            link(dve.tensor_reduce(cnt, GT, AX.X, ALU.add))
            link(dve.tensor_scalar(gm, cnt, float(TOPG) - 0.5, None, ALU.is_lt))
            link(dve.tensor_scalar(ng, gm, -NEG, NEG, ALU.mult, ALU.add))
            for t in range(NT):
                v = MB[:, t, :].rearrange("p (g u) -> p g u", g=NG)
                link(dve.tensor_tensor(v, BI[:, t, :].rearrange("p (g u) -> p g u", g=NG),
                                       bc(gm[:, t, :].unsqueeze(2), [P, NG, 8]), ALU.mult))
                link(dve.tensor_tensor(v, v, bc(ng[:, t, :].unsqueeze(2), [P, NG, 8]), ALU.add))
                link(dve.max(V8[:, t, :], MB[:, t, :]))
                link(dve.match_replace(RP[:, t, :], V8[:, t, :], MB[:, t, :], -3e38))
            dve.tensor_scalar(SEL, RP, -2e38, None, ALU.is_lt).then_inc(s_sel, 1)
            dve.wait_ge(s_sel, 1)
            link(dve.tensor_tensor(WT, SC, SEL, ALU.mult))
            link(dve.tensor_reduce(ws[:, 0, :], WT, AX.X, ALU.add))
            link(dve.reciprocal(ws[:, 1, :], ws[:, 0, :]))
            link(dve.tensor_tensor(WT, WT, bc(ws[:, 1, :].unsqueeze(2), [P, NT, E]), ALU.mult))
            link(dve.tensor_scalar(WT, WT, ROUTED_SCALE, None, ALU.mult))
            for t in range(NT):
                link(dve.tensor_tensor_scan(RV[:, t, :], cst[:, C_ONE:C_ONE + E], SEL[:, t, :], 0.0, ALU.mult, ALU.add))
            link(dve.tensor_tensor(RV, RV, SEL, ALU.subtract))
            link(dve.tensor_tensor(RV, RV, bc(cst[:, C_TOKR:C_TOKR + NT].unsqueeze(2), [P, NT, E]), ALU.add))
            dve.wait_ge(s_pos, 1)
            link(dve.scalar_tensor_tensor(Q1, PS[:, 4, 0:256].rearrange("p (t e) -> p t e", t=NT), 1.0, SEL,
                                          ALU.add, ALU.mult))
            dve.sem_inc(s_q1, 1)
            link(dve.tensor_scalar(ob[:, 0:1], PS[0:E, 4, 256:257], float(P) + 0.5, None, ALU.is_gt))
            link(dve.tensor_scalar(ob[:, 1:2], PS[0:E, 4, 256:257], 2.0 * P + 0.5, None, ALU.is_gt))
            link(dve.tensor_scalar(ob[:, 2:3], PS[0:E, 4, 256:257], 3.0 * P + 0.5, None, ALU.is_gt))
            link(dve.tensor_tensor(ob[:, 3:4], ob[:, 0:1], ob[:, 1:2], ALU.add))
            dve.tensor_tensor(ob[:, 3:4], ob[:, 3:4], ob[:, 2:3], ALU.add).then_inc(s_ob, 1)
            perm = "p t e -> p e t"
            link(dve.tensor_copy(PM[:, 0:E, :], Q1.rearrange(perm)))
            link(dve.tensor_copy(RX[:, 0:E, :, 1], RV.rearrange(perm)))
            link(dve.tensor_copy(RX[:, 0:E, :, 2], WT.rearrange(perm)))
            link(dve.tensor_copy(RX[:, :, :, 0], bc(cst[:, C_TOKG:C_TOKG + NT].unsqueeze(1), [P, NBLK, NT])))
            dve.wait_ge(s_oend, 1)
            m36 = cst[0:E, C_M:C_M + NEXT]
            link(dve.tensor_copy(ob[:, 4:5], PS[0:E, 4, 0:1]))
            link(dve.tensor_tensor(ob[:, 5:6], ob[:, 4:5], ob[:, 3:4], ALU.subtract))
            link(dve.tensor_scalar(OH[:, 0, :], m36, ob[:, 5:6], None, ALU.is_ge))
            link(dve.scalar_tensor_tensor(OH[:, 0, :], m36, ob[:, 4:5], OH[:, 0, :], ALU.is_lt, ALU.mult))
            link(dve.tensor_scalar(OH[:, 1, :], m36, ob[:, 5:6], 1.0, ALU.subtract, ALU.add))
            dve.scalar_tensor_tensor(OH[:, 1, :], OH[:, 1, :], float(P), OH[:, 0, :], ALU.mult, ALU.mult)\
                .then_inc(s_oh1, 1)
            for n, (dst, bank) in enumerate(((Q1T, 5), (WTT, 6), (RVT, 7))):
                dve.wait_ge(s_tr, n + 1)
                dve.tensor_copy(dst, PS[0:E, bank, :]).then_inc(s_trd, 1)
            dve.wait_ge(s_xm, 1)
            for col, dst in enumerate((PM[:, E:NBLK, :], RX[:, E:NBLK, :, 2], RX[:, E:NBLK, :, 1])):
                link(dve.tensor_copy(dst, PS[:, 4, 144 * col:144 * (col + 1)].rearrange("p (t m) -> p m t", t=NT)))
            dve.wait_ge(s_etab, 16)
            link(dve.tensor_copy(nover[:, :], PS[0:1, 4, 468:469]))
            dve.tensor_copy(etab[:, E:NBLK], PS[0:1, 4, 432:468]).then_inc(s_tabs, 1)

            for t in range(NT):
                dve.wait_ge(s_ssil, t + 1)
                dve.tensor_tensor(ACTS[:, t, :], SILS[:, t, :], PS[:, t, F:2 * F], ALU.mult).then_inc(s_sact, 1)
            for n in range(8):
                t, cols = n // 2, slice(512 * (n % 2), 512 * (n % 2) + 512)
                dve.wait_ge(s_sdn, n + 1)
                link(dve.tensor_tensor(G[:, 1, 3, cols], PS[:, 6 + n % 2, :], MOD[:, 3, cols], ALU.mult))
                link(dve.tensor_tensor(X[:, t, cols], X[:, t, cols], G[:, 1, 3, cols], ALU.add))
                dve.sem_inc(s_sx, 1)

            def onehot(j, b):
                need(dve, s_ohd, j - 1)
                dve.tensor_tensor(AH[:, b], bc(cst[:, C_SLOT:C_SLOT + P].unsqueeze(1), [P, NT, P]),
                                  bc(PM[:, bass.ds(j, 1), :].rearrange("p o t -> p (o t)").unsqueeze(2), [P, NT, P]),
                                  ALU.is_equal).then_inc(s_ah, 1)

            def slots(j, b):
                dve.wait_ge(s_ohd, j + 1)
                need(dve, s_xt, j - 1)
                dve.tensor_copy(slx[:, bass.ds(j % 8, 1), :].rearrange("p o c -> p (o c)"), PS[:, 7, 0:3])\
                    .then_inc(s_sl, 1)
                dve.tensor_scalar(gidx[b][:, :], PS[:, 7, 0:1], NOTOK, None, ALU.add).then_inc(s_sl, 1)

            def take_xt(j, b):
                dve.wait_ge(s_xt, j + 1)
                need(dve, s_gu, j - 1)
                dve.tensor_copy(XT[:, b, 0:4, :], PS[:, 4, :].rearrange("p (k s) -> p k s", k=4)).then_inc(s_xtd, 1)

            def mul(j, b):
                dve.wait_ge(s_silu, j + 1)
                need(dve, s_at, j - 1)
                dve.tensor_tensor(AR[:, b, :], SIL[:, b, :], PS[:, b, F:2 * F], ALU.mult).then_inc(s_act, 1)

            def take_o(i, j, b):
                need(dve, s_scat[b], 16 * i)
                dve.wait_ge(s_sl, 2 * j + 2)
                dve.tensor_scalar(ridx[b][:, :], slx[:, bass.ds(j % 8, 1), 1:2].rearrange("p o c -> p (o c)"),
                                  NOROW, None, ALU.add).then_inc(s_ri, 1)
                dve.wait_ge(s_dn, 2 * j + 1)
                dve.tensor_scalar(OB[:, b, 0:512], PS[:, 2, :],
                                  slx[:, bass.ds(j % 8, 1), 2:3].rearrange("p o c -> p (o c)"), None,
                                  ALU.mult).then_inc(s_oed, 1)

            dve.wait_ge(s_tabs, 1)
            npairs = (dve.value_load(nover[0:1, 0:1], min_val=0, max_val=31) + (E + 1)) // 2
            onehot(0, 0)
            onehot(1, 1)
            slots(0, 0)
            onehot(2, 0)
            slots(1, 1)
            onehot(3, 1)
            take_xt(0, 0)
            take_xt(1, 1)
            slots(2, 0)
            slots(3, 1)
            mul(0, 0)

            def blocks(i):
                onehot(2 * i + 4, 0)
                mul(2 * i + 1, 1)
                take_xt(2 * i + 2, 0)
                slots(2 * i + 4, 0)
                take_o(i, 2 * i, 0)
                onehot(2 * i + 5, 1)
                with dve.If(i + 1 < npairs):
                    mul(2 * i + 2, 0)
                take_xt(2 * i + 3, 1)
                slots(2 * i + 5, 1)
                take_o(i, 2 * i + 1, 1)
            blocks(0)
            with dve.Fori(1, MAXPAIRS) as i:
                with dve.If(i < npairs):
                    blocks(i)

            for t in range(NT):
                dve.wait_ge(s_fb[t % 3], 16 * (t // 3 + 1))
                for w in (4 * D, 2 * D, D):
                    link(dve.tensor_tensor(FB[t][:, 0:w], FB[t][:, 0:w], FB[t][:, w:2 * w], ALU.add))
                link(dve.tensor_tensor(FB[t][:, 0:D], FB[t][:, 0:D], MOD[:, 3, :], ALU.mult))
                dve.tensor_tensor(X[:, t, :], X[:, t, :], FB[t][:, 0:D], ALU.add).then_inc(s_fin, 1)

        @block.tensor
        def _(pe):
            mm = pe.matmul

            def spread(us):
                for u in us:
                    ins = mm(PS[:, 4 + (u % 4) // 2, HC * (u % 2):HC * (u % 2) + HC], ones, ACC[:, u % 4],
                             start=True, stop=True)
                ins.then_inc(s_ones, len(us))

            pe.wait_ge(s_cb, 1)
            for u in range(8):
                pe.wait_ge(s_ada[u % 2], 16 * (u // 2 + 1))
                need(pe, s_madd, u - u % 2 - 2)
                for k in range(KD):
                    ins = mm(PS[:, 4 + (u % 4) // 2, HC * (u % 2):HC * (u % 2) + HC], CB[:, k, :], AD[:, u % 2, k],
                             start=k == 0, stop=k == KD - 1)
                ins.then_inc(s_ones, 1)

            pe.wait_ge(s_cst, 16)

            def turn(dst_bank, src, ready):
                for k in range(4):
                    ins = pe.transpose(PS[:, dst_bank, P * k:P * k + P], src[:, P * k:P * k + P], ident)
                ins.then_inc(ready, 1)

            for t in range(NT):
                pe.wait_ge(s_hrow, t + 1)
                for half in range(2):
                    need(pe, s_ht, 2 * t - 1 + half)
                    turn(6 + half, HROW[:, t % 2, 512 * half:512 * half + 512], s_xpose)
            pe.wait_ge(s_ht, 8)
            pe.wait_ge(s_wf, 16)
            for t in range(NT):
                for k in range(KD):
                    ins = mm(PS[:, 6, HA * t:HA * t + HA], HT[:, k, P * t:P * t + P], WF[:, k, :],
                             start=k == 0, stop=k == KD - 1)
            ins.then_inc(s_f, 1)

            def project(i, b):
                pe.wait_ge(s_w[b], 16 * (i + 1))
                for t in range(NT):
                    pe.wait_ge(s_zfree, 8 * i + 4 * b + t + 1)
                    for k in range(KD):
                        ins = mm(PS[:, t, :], HT[:, k, P * t:P * t + P], WR[:, b, k, :],
                                 start=k == 0, stop=k == KD - 1)
                    ins.then_inc(s_proj, 1)

            for i in range(2):
                for b in range(2):
                    project(i, b)
                    pe.wait_ge(s_acc, 4 + 4 * (2 * i + b))
                    pe.wait_ge(s_madd, 8 + 4 * (2 * i + b))
                    spread(range(8 + 4 * (2 * i + b), 12 + 4 * (2 * i + b)))
            pe.wait_ge(s_lf, 1)
            for t in range(NT):
                for j in range(t + 1):
                    ins = mm(PS[:, 7, HA * t:HA * t + HA], cst[:, C_TIN:C_TIN + P] if j == t else ones,
                             FZ[:, 0, j, :], start=j == 0, stop=j == t)
            ins.then_inc(s_cum, 1)
            with pe.Fori(2, 5) as i:
                for b in range(2):
                    project(i, b)

            def turn_qk(h, b):
                pe.wait_ge(s_stage, 4 * h + 4)
                for r in range(2):
                    need(pe, s_qkev, 2 * h - 1 + r)
                    for t in range(NT):
                        ins = pe.transpose(PS[0:DA, 4 + r, P * t:P * t + P], QS[:, b, r, t, :], ident)
                    ins.then_inc(s_tq, 1)

            def scores(h, b):
                pe.wait_ge(s_qkev, 2 * h + 2)
                for g, tiles in enumerate(((0, 2), (1,), (3,))):
                    need(pe, s_sred, 3 * h - 2 + g)
                    for i in tiles:
                        at = P if i == 2 else 0
                        ins = mm(PS[:, g, at:at + P * (i + 1)], QKT[:, b, 0, P * i:P * i + P],
                                 QKT[:, b, 1, 0:P * (i + 1)], start=True, stop=True)
                    ins.then_inc(s_s, 1)

            def turn_p(h, b, i):
                at = P * (i * (i + 1) // 2)
                pe.wait_ge(s_exp, 4 * h + i + 1)
                if i == 1:
                    need(pe, s_pta, h)
                else:
                    need(pe, s_ptd, 3 * h + (0, 0, 1, 2)[i])
                for j in range(i + 1):
                    ins = pe.transpose(PS[:, 6 + i % 2, P * j:P * j + P], PB[:, b, at + P * j:at + P * j + P], ident)
                ins.then_inc(s_pt, 1)

            def pv(h, i):
                at = P * (i * (i + 1) // 2)
                if i == 3:
                    pe.wait_ge(s_pta, h + 1)
                else:
                    pe.wait_ge(s_ptd, 3 * h + i + 1)
                if i == 0:
                    need(pe, s_y, h)
                for j in range(i + 1):
                    ins = mm(PS[:, 3, DH * i:DH * i + DH], PTS[:, at + P * j:at + P * j + P],
                             Z[:, 2, j, bass.ds(h * DH, DH)], start=j == 0, stop=j == i)
                ins.then_inc(s_pv, 1)

            pe.wait_ge(s_zfree, 44)
            pe.wait_ge(s_cumr, 2)
            pe.wait_ge(s_madd, 24)
            turn_qk(0, 0)
            turn_qk(1, 1)
            scores(0, 0)
            scores(1, 1)
            turn_qk(2, 0)
            for n in range(4):
                turn_p(0, 0, n)

            def heads(i):
                for b in range(2):
                    h = 2 * i + 1 + b
                    scores(h + 1, b)
                    turn_qk(h + 2, 1 - b)
                    for n in range(4):
                        pv(h - 1, n)
                        turn_p(h, 1 - b, n)
            for i in range(1):
                heads(i)
            with pe.Fori(1, 6) as i:
                heads(i)
            scores(14, 0)
            turn_qk(15, 1)
            for n in range(4):
                pv(12, n)
                turn_p(13, 1, n)
            scores(15, 1)
            for h in (14, 15):
                for n in range(4):
                    pv(h - 1, n)
                    turn_p(h, h % 2, n)
            for n in range(4):
                pv(15, n)

            pe.wait_ge(s_y, 16)
            pe.wait_ge(s_qkev, 32)
            pe.wait_ge(s_ptd, 48)
            pe.wait_ge(s_pta, 16)
            for t in range(NT):
                for half in range(2):
                    need(pe, s_ytea if half else s_yted, t - 1)
                    turn(4 + 2 * (t % 2) + half, Z[:, 0, t, 512 * half:512 * half + 512], s_yt)
            pe.wait_ge(s_sred, 48)
            pe.wait_ge(s_yted, 4)
            pe.wait_ge(s_ytea, 4)
            pe.wait_ge(s_wp, 32)

            def merge(t):
                for half in range(2):
                    n = 2 * t + half
                    need(pe, s_m, n - 1)
                    for r, w in enumerate((WPA, WPB)):
                        for k in range(4):
                            ins = mm(PS[:, 2 * half + r, :], YT[:, 4 * r + k, P * t:P * t + P],
                                     w[:, k, 512 * half:512 * half + 512], start=k == 0, stop=k == 3)
                    ins.then_inc(s_u, 1)

            def turn_m(t):
                pe.wait_ge(s_m, 2 * t + 2)
                for half in range(2):
                    need(pe, s_mte, 2 * t + half - 3)
                    turn(4 + (2 * t + half) % 4, G[:, 0, t, 512 * half:512 * half + 512], s_mt)
            merge(0)
            for t in range(1, NT):
                merge(t)
                turn_m(t - 1)
            turn_m(NT - 1)
            pe.wait_ge(s_mte, 8)
            pe.wait_ge(s_wo, 16)

            def turn_h2(t):
                pe.wait_ge(s_h2, t + 1)
                for half in range(2):
                    need(pe, s_h2te, 2 * t + half - 3)
                    turn(4 + (2 * t + half) % 4, HROW[:, t % 2, 512 * half:512 * half + 512], s_h2t)
            for n in range(8):
                t, half = n // 2, n % 2
                need(pe, s_x2, n - 3)
                for k in range(KD):
                    ins = mm(PS[:, n % 4, :], MT[:, k, P * t:P * t + P], WO[:, k, 512 * half:512 * half + 512],
                             start=k == 0, stop=k == KD - 1)
                ins.then_inc(s_o, 1)
                if half and t >= 2:
                    turn_h2(t - 2)
            turn_h2(2)
            turn_h2(3)
            pe.wait_ge(s_h2te, 8)
            pe.wait_ge(s_ws, 64)
            for t in range(NT):
                for k in range(KD):
                    ins = mm(PS[:, 4, E * t:E * t + E], H2T[:, k, P * t:P * t + P], WRT[:, k, :],
                             start=k == 0, stop=k == KD - 1)
            ins.then_inc(s_rt, 1)
            pe.wait_ge(s_x2, 8)
            for t in range(NT):
                for k in range(KD):
                    ins = mm(PS[:, t, :], H2T[:, k, P * t:P * t + P], WSGU[:, k, :], start=k == 0, stop=k == KD - 1)
                ins.then_inc(s_sgu, 1)
            pe.wait_ge(s_sel, 1)
            pe.wait_ge(s_sc, 1)
            for t in range(NT):
                for j in range(t + 1):
                    mm(PS[:, 4, E * t:E * t + E], cst[:, C_TEX:C_TEX + P] if j == t else ones, SEL[:, j, :],
                       start=j == 0, stop=j == t)
            for j in range(NT):
                ins = mm(PS[0:E, 4, 256:257], SEL[:, j, :], ones[:, 0:1], start=j == 0, stop=j == NT - 1)
            ins.then_inc(s_pos, 1)
            pe.wait_ge(s_ob, 1)
            mm(PS[0:E, 4, 0:1], cst[0:E, C_TIN:C_TIN + E], ob[:, 3:4], start=True, stop=True).then_inc(s_oend, 1)
            pe.wait_ge(s_q1, 1)
            for bank, src in ((5, Q1), (6, WT), (7, RV)):
                for t in range(NT):
                    ins = pe.transpose(PS[0:E, bank, P * t:P * t + P], src[:, t, :], ident)
                ins.then_inc(s_tr, 1)
            pe.wait_ge(s_trd, 3)
            pe.wait_ge(s_oh1, 1)
            for t in range(NT):
                at = NEXT * t
                mm(PS[:, 4, at:at + NEXT], Q1T[:, P * t:P * t + P], OH[:, 0, :], start=True, stop=False)
                mm(PS[:, 4, at:at + NEXT], cst[0:E, C_NEG1:C_NEG1 + P], OH[:, 1, :], start=False, stop=True)
            for n, src in ((1, WTT), (2, RVT)):
                for t in range(NT):
                    at = 144 * n + NEXT * t
                    mm(PS[:, 4, at:at + NEXT], src[:, P * t:P * t + P], OH[:, 0, :], start=True, stop=True)
            mm(PS[0:1, 4, 432:468], cst[0:E, C_E:C_E + 1], OH[:, 0, :], start=True, stop=True)
            mm(PS[0:1, 4, 468:469], ob[:, 3:4], ones[0:E, 0:1], start=True, stop=True).then_inc(s_xm, 1)
            for t in range(NT):
                pe.wait_ge(s_sact, t + 1)
                need(pe, s_sate, t)
                for k in range(2):
                    ins = pe.transpose(PS[:, 5, P * k:P * k + P], ACTS[:, t, P * k:P * k + P], ident)
                ins.then_inc(s_sat, 1)
                pe.wait_ge(s_sate, t + 1)
                for half in range(2):
                    need(pe, s_sx, 2 * t + half - 1)
                    for k in range(2):
                        ins = mm(PS[:, 6 + half, :], AT[:, t % 2, k, :], WSD[:, k, 512 * half:512 * half + 512],
                                 start=k == 0, stop=k == 1)
                    ins.then_inc(s_sdn, 1)
            pe.wait_ge(s_sx, 8)
            pe.wait_ge(s_tabs, 1)

            def slot_rows(j, b):
                pe.wait_ge(s_ah, j + 1)
                need(pe, s_sl, 2 * j)
                for t in range(NT):
                    ins = mm(PS[:, 7, 0:3], AH[:, b, t, :], RX[:, bass.ds(j, 1), t, :].rearrange("p o c -> p (o c)"),
                             start=t == 0, stop=t == NT - 1)
                ins.then_inc(s_ohd, 1)

            def turn_x(i, j, b):
                pe.wait_ge(s_gat[b], 16 * (i + 1))
                need(pe, s_xtd, j)
                need(pe, s_xta, j)
                for half in range(2):
                    for k in range(4):
                        ins = pe.transpose(PS[:, 4 + half, P * k:P * k + P],
                                           XG[:, b, 512 * half + P * k:512 * half + P * k + P], ident)
                ins.then_inc(s_xt, 1)

            def gate_up(i, j, b):
                pe.wait_ge(s_xtd, j + 1)
                pe.wait_ge(s_xta, j + 1)
                pe.wait_ge(s_wgu[b], 32 * (i + 1))
                need(pe, s_act, j - 1)
                for k in range(KD):
                    ins = mm(PS[:, b, :], XT[:, b, k, :], WGU[b][:, k, :], start=k == 0, stop=k == KD - 1)
                ins.then_inc(s_gu, 1)

            def turn_act(j, b):
                pe.wait_ge(s_act, j + 1)
                need(pe, s_ate, j)
                for k in range(2):
                    ins = pe.transpose(PS[:, 6, P * k:P * k + P], AR[:, b, P * k:P * k + P], ident)
                ins.then_inc(s_at, 1)

            def down(i, j, b):
                pe.wait_ge(s_ate, j + 1)
                pe.wait_ge(s_wd[b], 16 * (i + 1))
                for half in range(2):
                    need(pe, s_oea if half else s_oed, j)
                    for k in range(2):
                        ins = mm(PS[:, 2 + half, :], AT[:, b, k, :], WDN[b][:, k, 512 * half:512 * half + 512],
                                 start=k == 0, stop=k == 1)
                    ins.then_inc(s_dn, 1)

            slot_rows(0, 0)
            slot_rows(1, 1)
            turn_x(0, 0, 0)
            turn_x(0, 1, 1)
            slot_rows(2, 0)
            slot_rows(3, 1)
            gate_up(0, 0, 0)
            npairs = (pe.value_load(nover[0:1, 0:1], min_val=0, max_val=31) + (E + 1)) // 2

            def blocks(i):
                gate_up(i, 2 * i + 1, 1)
                turn_act(2 * i, 0)
                turn_x(i + 1, 2 * i + 2, 0)
                slot_rows(2 * i + 4, 0)
                down(i, 2 * i, 0)
                with pe.If(i + 1 < npairs):
                    gate_up(i + 1, 2 * i + 2, 0)
                turn_act(2 * i + 1, 1)
                turn_x(i + 1, 2 * i + 3, 1)
                slot_rows(2 * i + 5, 1)
                down(i, 2 * i + 1, 1)
            blocks(0)
            with pe.Fori(1, MAXPAIRS) as i:
                with pe.If(i < npairs):
                    blocks(i)


_INS = ["x", "c", "ada_w", "ada_b", "mix_norm_g", "w_in", "b_fgate", "qn_a", "kn_a", "qn_b", "kn_b", "rel_bias",
        "w_proj_a", "w_proj_b", "w_out", "ffn_norm_g", "w_router", "router_bias", "w_gate_e", "w_up_e", "w_down_e",
        "w_gate_s", "w_up_s", "w_down_s"]


def kernel(**inputs):
    import concourse.bacc as bacc
    from concourse.bass_utils import run_bass_kernel_spmd

    nc = bacc.Bacc("TRN2", target_bir_lowering=False, num_devices=1)
    arrays, aps = {}, {}

    def give(name, array):
        arrays[name] = array
        aps[name] = nc.dram_tensor(name, array.shape, mybir.dt.from_np(array.dtype), kind="ExternalInput").ap()

    for name in _INS:
        array = np.ascontiguousarray(inputs[name])
        give(name, array if name == "c" else array.reshape(array.shape[1:]))
    for name, array in zip(("consts", "causal", "etab"), constants()):
        give(name, array)
    aps["out"] = nc.dram_tensor("out", (S, D), mybir.dt.float32, kind="ExternalOutput").ap()
    build(nc, aps)
    r = run_bass_kernel_spmd(nc, [arrays], core_ids=[0])
    return r.results[0]["out"].reshape(1, S, D)
```

```python
import contextlib

import numpy as np

import concourse.bass as bass
from concourse import mybir

P = 128
D = 1024
S = 512
DH = 64
HA = 8
NH = 16
NT = S // P
KD = D // P
E = 64
NG = 8
TOPG = 4
TOPK = 8
F = 256
EPS = 1e-6
ROUTED_SCALE = 2.5
REL = 128
NTAB = 2 * REL + 1
EXT = 640
N_ADA = 6 * D
HC = 256
SEG = 512
DA = DH + 2
NBLK = 64 + 36
NEXT = NBLK - E
MAXPAIRS = 48
NEG = -1e30
NOROW = 8192.0
NOTOK = 1024.0
T_HI, T_LO, R_HI, R_LO, W_1, W_2, W_3, NCOL = range(8)
SLN = 4

C_ID, C_TEX, C_TIN, C_ONE, C_SLOT = 0, 128, 256, 384, 512
C_TOKG, C_TOKR, C_M, C_E, C_LOW, C_SC, C_NEG1 = 640, 644, 648, 684, 685, 749, 757
C_TOK3 = 757 + 128
C_N = C_TOK3 + 12


def constants():
    c = np.zeros((P, C_N), np.float32)
    p = np.arange(P)[:, None]
    f = np.arange(P)[None, :]
    c[:, C_ID:C_ID + P] = p == f
    c[:, C_TEX:C_TEX + P] = p < f
    c[:, C_TIN:C_TIN + P] = p <= f
    c[:, C_ONE:C_ONE + P] = 1.0
    c[:, C_SLOT:C_SLOT + P] = f + 1
    token = p + P * np.arange(NT)[None]
    c[:, C_TOKR:C_TOKR + NT] = token % 8 * TOPK
    c[:, C_TOK3 + T_HI:C_TOK3 + 12:3] = token // 8 * 8 - NOTOK
    c[:, C_TOK3 + T_LO:C_TOK3 + 12:3] = token % 8
    c[:, C_TOK3 + R_HI:C_TOK3 + 12:3] = token // 8 * 8 * TOPK - NOROW
    c[:, C_M:C_M + NEXT] = np.arange(NEXT)[None]
    c[:, C_E:C_E + 1] = p
    c[:, C_LOW:C_LOW + 64] = (np.arange(8)[None, :] < np.arange(8)[:, None]).reshape(1, 64)
    c[:, C_SC:C_SC + 3] = [EPS, DH * EPS, 1.0]
    c[:, C_NEG1:C_NEG1 + P] = -1.0
    causal = np.zeros((P, S), np.float32)
    causal[:, S - P:] = np.where(f > p, NEG, 0.0)
    etab = np.zeros((1, NBLK), np.int32)
    etab[0, :E] = np.arange(E)
    return c, causal, etab


def build(nc, a):
    f32, i32, bf16 = mybir.dt.float32, mybir.dt.int32, mybir.dt.bfloat16
    ALU, ACT, AX = mybir.AluOpType, mybir.ActivationFunctionType, mybir.AxisListType

    st = contextlib.ExitStack()
    with st:
        def sb(name, shape, dt=f32):
            return st.enter_context(nc.sbuf_tensor(name, shape, dt))

        def sem(name):
            return st.enter_context(nc.semaphore(name))

        h2_dram = nc.dram_tensor("h2_rows", (S, D), f32).ap()
        routed_dram = nc.dram_tensor("routed_rows", (S * TOPK, D), f32).ap()
        ext_dram = nc.dram_tensor("bias_rows", (HA, P, EXT), f32).ap()

        cst = sb("cst", [P, C_N])
        X = sb("X", [P, NT, D])
        MOD = sb("MOD", [P, 4, D])
        R_HT = sb("R_HT", [P, 4096])
        R_Z = sb("R_Z", [P, 12288])
        R_G = sb("R_G", [P, 8192])
        R_W = sb("R_W", [P, 8192])
        R_T = sb("R_T", [P, 4608])
        R_S = sb("R_S", [P, 3616])
        R_A = sb("R_A", [P, 1024])

        HT = R_HT[:, :].rearrange("p (k s) -> p k s", k=KD)
        Z = R_Z[:, :].rearrange("p (r t n) -> p r t n", r=3, t=NT)
        G = R_G[:, :].rearrange("p (r t n) -> p r t n", r=2, t=NT)
        WR = R_W[:, :].rearrange("p (b k n) -> p b k n", b=2, k=KD)
        AD = R_T[:, 0:4096].rearrange("p (b k n) -> p b k n", b=2, k=KD)
        AF = [R_Z[:, 2048 * u:2048 * (u + 1)].rearrange("p (k n) -> p k n", k=KD) for u in range(6)]\
            + [AD[:, 0], AD[:, 1]]
        ROWS = R_A[0:32, 0:P]
        ACC = R_A[:, :].rearrange("p (b n) -> p b n", b=4)
        HROW = R_S[:, 0:2048].rearrange("p (b n) -> p b n", b=2)
        JUNK = R_S[:, 2048:3072]
        SQT = R_S[:, 0:2048].rearrange("p (t n) -> p t n", t=NT)
        GN = R_G[:, 0:1024]
        QKT = R_HT[0:DA, 0:2048].rearrange("p (b r s) -> p b r s", b=2, r=2)
        PTS = R_HT[:, 2048:3328]
        TB = R_A[:, :].rearrange("p (b s) -> p b s", b=2)
        T4 = R_T[:, :].rearrange("p (h s) -> p h s", h=9)
        PB = R_S[:, 0:2560].rearrange("p (b s) -> p b s", b=2)
        QS = R_S[:, 2560:3616].rearrange("p (b r t d) -> p b r t d", b=2, r=2, t=NT)
        YT = R_T[:, 0:4096].rearrange("p (k s) -> p k s", k=KD)
        WPA = R_W[:, 0:4096].rearrange("p (k n) -> p k n", k=4)
        WPB = R_W[:, 4096:8192].rearrange("p (k n) -> p k n", k=4)
        MT = HT
        WO = R_Z[:, 0:8192].rearrange("p (k n) -> p k n", k=KD)
        H2T = YT
        WSGU = R_W[:, 0:4096].rearrange("p (k n) -> p k n", k=KD)
        WSD = R_W[:, 4096:6144].rearrange("p (k n) -> p k n", k=2)
        WRT = R_W[:, 6144:6656].rearrange("p (k n) -> p k n", k=KD)
        SILS = R_S[:, 1024:2048].rearrange("p (t n) -> p t n", t=NT)
        ACTS = R_S[:, 2048:3072].rearrange("p (t n) -> p t n", t=NT)
        RX = R_HT[:, 0:1400].bitcast(bf16).rearrange("p (j t c) -> p j t c", j=NBLK, t=NT)
        PM = R_HT[:, 1400:1800].rearrange("p (j t) -> p j t", j=NBLK)

        def tab(at):
            return R_HT[:, at:at + 256].rearrange("p (t e) -> p t e", t=NT)
        SC, BI, MB, RP, SEL, WT, Q1, RV = (tab(1800 + 256 * n) for n in range(8))
        M8 = R_A[:, 512:768].rearrange("p (g v) -> p g v", g=32)
        GT = R_HT[:, 3336:3592].rearrange("p (t g u) -> p t g u", t=NT, g=NG)
        GE = R_HT[:, 3592:3848].rearrange("p (t g u) -> p t g u", t=NT, g=NG)
        SCT = R_A[0:E, 0:512]
        Q1T, WTT, RVT = R_A[0:E, 0:512], R_A[0:E, 512:1024], R_S[0:E, 3072:3584]
        WX = R_Z[:, :].rearrange("p (b n) -> p b n", b=2)
        WGU = [WX[:, b, 0:4096].rearrange("p (k n) -> p k n", k=KD) for b in range(2)]
        WDN = [WX[:, b, 4096:6144].rearrange("p (k n) -> p k n", k=2) for b in range(2)]
        XG = R_G[:, 0:2048].rearrange("p (b n) -> p b n", b=2)
        XT = R_G[:, 2048:4096].rearrange("p (b k s) -> p b k s", b=2, k=KD)
        SIL = R_G[:, 4096:4608].rearrange("p (b n) -> p b n", b=2)
        AR = R_G[:, 4608:5120].rearrange("p (b n) -> p b n", b=2)
        AT = R_G[:, 5120:5632].rearrange("p (b k s) -> p b k s", b=2, k=2)
        OB = R_G[:, 5632:7680].rearrange("p (b n) -> p b n", b=2)
        AH = R_S[:, 0:512].bitcast(bf16).rearrange("p (b t s) -> p b t s", b=2, t=NT)
        FB = [R_W[:, :], R_Z[:, 0:8192], R_G[:, :], R_W[:, :]]

        cact = sb("cact", [P, KD])
        gcol = sb("gcol", [P, 3, KD])
        mcol = sb("mcol", [P, 2, KD])
        ssx = sb("ssx", [P, 12])
        QKG = sb("QKG", [P, 2, 2, DH])
        RQ = sb("RQ", [P, 2, NT, NH])
        bfg = sb("bfg", [P, HA])
        rbias = sb("rbias", [P, E])
        tabr = R_G[0:HA, 4096:4096 + NTAB]
        extr = R_G[0:HA, 4608:4608 + EXT]
        WF = sb("WF", [P, KD, HA])
        FZ = sb("FZ", [P, 4, NT, HA])
        CUM = sb("CUM", [P, 2, NT, NH])
        mx = sb("mx", [P, 2, 2, NT])
        sm = sb("sm", [P, 2, 2, NT])
        gs = sb("gs", [P, 5, 32])
        ws = sb("ws", [P, 2, NT])
        V8 = sb("V8", [P, NT, 8])
        ob = sb("ob", [E, 8])
        OH = sb("OH", [E, 3, NEXT])
        etab = sb("etab_sb", [1, NBLK], i32)
        nover = sb("nover", [1, 1], i32)
        slx = sb("slx", [P, 8, 3])
        slc = sb("slc", [P, NCOL])
        wres = R_A[:, 768:1024].rearrange("p (t e) -> p t e", t=NT)
        wxr = sb("wxr", [P, NT, NEXT])
        gidx = [sb(f"gidx{b}", [P, 1], i32) for b in range(2)]
        ridx = [sb(f"ridx{b}", [P, 1], i32) for b in range(2)]
        PS = st.enter_context(nc.psum_tensor("PS", [P, 8, 512], f32))

        ident = cst[:, C_ID:C_ID + P]
        ones = cst[:, C_ONE:C_ONE + P]

        s_cst, s_rows, s_gn, s_qkg, s_small, s_tab = map(sem, (
            "cst_loaded", "rows_loaded", "gain_loaded", "qk_gains_loaded", "small_loaded", "table_loaded"))
        s_x = [sem(f"x_loaded{t}") for t in range(NT)]
        s_af = [sem(f"first_ada_loaded{u}") for u in range(8)]
        s_rx = sem("x_reciprocals_ready")
        s_rowst, s_ada1, s_mcol, s_hm = map(sem, ("rows_turned", "first_ada_done", "mod_columns_ready", "h_ready"))
        s_modb, s_wf, s_ext, s_extw, s_t4, s_t4c = map(sem, (
            "mod_bias_loaded", "wf_loaded", "ext_built", "ext_written", "bias_tiles_loaded", "causal_loaded"))
        s_ada = [sem(f"ada_loaded{b}") for b in range(2)]
        s_w = [sem(f"w_in_loaded{b}") for b in range(2)]
        s_cact, s_acc, s_ones, s_madd, s_mod2 = map(sem, (
            "c_act_ready", "ada_sums_ready", "ada_spread", "mod_added", "mod2_ready"))
        s_ssx, s_hrow, s_xpose, s_ht = map(sem, ("x_root_ready", "h_row_ready", "h_transposed", "ht_ready"))
        s_f, s_e, s_lf, s_cum, s_cumr = map(sem, ("f_done", "softplus_part", "log_f_ready", "cum_done", "cum_ready"))
        s_proj, s_zfree, s_ss, s_root, s_norm = map(sem, (
            "proj_done", "proj_evacuated", "qk_squares_ready", "qk_roots_ready", "qk_normed"))
        s_t4m, s_stage, s_tb, s_tq, s_qkev, s_s, s_sred, s_nmx, s_exp = map(sem, (
            "bias_masked", "qk_staged", "bias_staged", "qk_transposed", "qkt_ready", "scores_done",
            "scores_taken", "negmax_ready", "probs_ready"))
        s_pt, s_ptd, s_pta, s_pv, s_y = map(sem, (
            "probs_transposed", "pt_ready_dve", "pt_ready_act", "pv_done", "y_ready"))
        s_yt, s_yted, s_ytea, s_wp, s_u, s_m, s_mt, s_mte, s_wo, s_o, s_x2 = map(sem, (
            "y_transposed", "yt_ready_dve", "yt_ready_act", "w_proj_loaded", "u_done", "m_ready",
            "m_transposed", "mt_ready", "w_out_loaded", "out_done", "x2_ready"))
        s_ss2, s_h2, s_h2t, s_h2te, s_ws, s_rt, s_sct, s_sc = map(sem, (
            "x2_root_ready", "h2_row_ready", "h2_transposed", "h2t_ready", "shared_loaded",
            "router_done", "router_scores_ready", "router_scores_turned"))
        s_hb = [sem(f"h2_written{b}") for b in range(2)]
        s_sgu, s_ssil, s_sact, s_sat, s_sate, s_sdn, s_sx = map(sem, (
            "shared_gu_done", "shared_silu_ready", "shared_act_ready", "shared_at_done",
            "shared_at_ready", "shared_down_done", "shared_added"))
        s_sel, s_pos, s_q1, s_ob, s_oend, s_oh1, s_tr, s_trd, s_xm, s_tabs = map(sem, (
            "selected", "positions_done", "slots_ready", "over_counts_ready", "over_ends_done",
            "over_onehot_ready", "tables_transposed", "tables_ready_t", "ext_tables_done", "tables_ready"))
        s_etab = sem("expert_table_loaded")
        s_rxc = sem("token_columns_ready")
        s_w12 = sem("weight_parts_added")
        s_xgi = sem("gather_buffers_set")
        s_wgu = [sem(f"gate_up_loaded{b}") for b in range(2)]
        s_wd = [sem(f"down_loaded{b}") for b in range(2)]
        s_gat = [sem(f"gathered{b}") for b in range(2)]
        s_scat = [sem(f"scattered{b}") for b in range(2)]
        s_ah, s_ohd, s_sl, s_xt, s_xtd, s_xta, s_gu, s_silu, s_act, s_at, s_ate, s_dn, s_oed, s_oea, s_ri = map(sem, (
            "onehot_ready", "slots_done", "slot_rows_ready", "x_transposed", "xt_ready_dve",
            "xt_ready_act", "gu_done", "silu_ready", "act_ready", "act_transposed", "at_ready",
            "down_done", "o_ready_dve", "o_ready_act", "row_index_ready"))
        s_routed, s_fin, s_out = map(sem, ("all_scattered", "out_ready", "out_written"))
        s_fb = [sem(f"final_loaded{b}") for b in range(3)]
        s_idle = sem("idle")
        s_dch, s_ach, s_pch = map(sem, ("dve_chain", "act_chain", "pool_chain"))

        block = st.enter_context(nc.Block())

        def need(eng, s, value):
            if isinstance(value, int) and value <= 0:
                return
            eng.wait_ge(s, value)

        class Chain:
            def __init__(self, eng, s):
                self.eng, self.s, self.base, self.n = eng, s, 0, 0

            def __call__(self, ins):
                self.n += 1
                ins.then_inc(self.s, 1)
                self.eng.wait_ge(self.s, self.base + self.n)

            def enter(self, i, first, per):
                if not isinstance(i, int):
                    self.saved = self.base + self.n
                    self.base, self.n = self.saved + (i - first) * per, 0
                    self.per = per
                else:
                    self.saved = None

            def leave(self, count):
                if self.saved is not None:
                    assert self.n == self.per, self.n
                    self.base, self.n = self.saved + count * self.per, 0

        w_in, ada_w = a["w_in"], a["ada_w"]
        BY_DVE, BY_PE = (0, 2, 3, 5, 6, 7), (1, 4)
        PE_ORDER = (1, 0, 2, 3, 4, 5, 6, 7)
        ADA_COLS = ([HC * u for u in range(8)]
                    + [3 * D + HC * u for u in range(8)]
                    + [2 * D + HC * u for u in range(4)] + [5 * D + HC * u for u in range(4)])
        W_COLS = []
        for r in range(3):
            W_COLS += [(0 * 3 + r) * SEG, (1 * 3 + r) * SEG]
        W_COLS += [6 * SEG + HA + SEG * n for n in range(4)]

        def settle(eng):
            eng.sem_inc(s_idle, 1)

        def bc(ap, shape):
            return ap.to_broadcast(shape)

        @block.sync
        def _(sp):
            for row, src in ((0, a["c"]), (8, a["mix_norm_g"]), (16, a["ada_b"][0:2 * D])):
                src = src.rearrange("o (k p) -> (o k) p", p=P) if row == 0 else src.rearrange("(k p) -> k p", p=P)
                sp.dma_start(ROWS[row:row + src.shape[0], :], src).then_inc(s_rows, 16)
            sp.dma_start(cst[:, :], a["consts"]).then_inc(s_cst, 16)
            for t in range(NT):
                sp.dma_start(X[:, t, :], a["x"][P * t:P * (t + 1), :]).then_inc(s_x[t], 16)

            def ada_step(u):
                return ada_w[:, ADA_COLS[u]:ADA_COLS[u] + HC].rearrange("(k p) n -> p k n", p=P)

            def load_ada(u):
                sp.wait_ge(s_acc, u - 3)
                sp.dma_start(AD[:, u % 2], ada_step(u)).then_inc(s_ada[u % 2], 16)

            def load_w(c):
                if c >= 2:
                    sp.wait_ge(s_proj, 4 * (c - 1))
                sp.dma_start(WR[:, c % 2], w_in[:, W_COLS[c]:W_COLS[c] + SEG].rearrange(
                    "(k p) n -> p k n", p=P)).then_inc(s_w[c % 2], 16)

            for u in range(8):
                sp.dma_start(AF[u], ada_step(u)).then_inc(s_af[u], 16)
            load_w(0)
            sp.dma_start(WF[:, :, :], w_in[:, 6 * SEG:6 * SEG + HA].rearrange(
                "(k p) n -> p k n", p=P)).then_inc(s_wf, 16)
            load_ada(8)
            load_ada(9)
            load_w(1)
            for n, at in enumerate((3 * D, 4 * D, 2 * D, 5 * D)):
                sp.dma_start(MOD[:, n, :], a["ada_b"][at:at + D].rearrange("(o d) -> o d", o=1)
                             .to_broadcast([P, D])).then_inc(s_modb, 16)
            sp.dma_start(GN, a["ffn_norm_g"].rearrange("(o d) -> o d", o=1).to_broadcast([P, D])).then_inc(s_gn, 16)
            for g in range(4):
                for u in range(8 + 4 * g, 12 + 4 * g):
                    if u >= 10:
                        load_ada(u)
                load_w(2 + g)
            sp.wait_ge(s_acc, 22)
            sp.wait_ge(s_extw, 16)
            sp.dma_start(T4[:, 0:HA, :], bass.AP(ext_dram.tensor, P - 1, [[EXT - 1, P], [P * EXT, HA], [1, S]]))\
                .then_inc(s_t4, 16)
            sp.dma_start(T4[:, HA, :], a["causal"]).then_inc(s_t4c, 16)
            for c in range(6, 10):
                load_w(c)
            sp.wait_ge(s_proj, 36)
            sp.dma_start(WPA, a["w_proj_a"].rearrange("(k p) n -> p k n", p=P)).then_inc(s_wp, 16)
            sp.wait_ge(s_proj, 40)
            sp.dma_start(WPB, a["w_proj_b"].rearrange("(k p) n -> p k n", p=P)).then_inc(s_wp, 16)
            sp.wait_ge(s_yt, 8)
            sp.dma_start(WO, a["w_out"].rearrange("(k p) n -> p k n", p=P)).then_inc(s_wo, 16)
            sp.wait_ge(s_u, 8)
            sp.dma_start(WRT, a["w_router"].rearrange("(k p) n -> p k n", p=P)).then_inc(s_ws, 16)
            sp.dma_start(WSGU[:, :, 0:F], a["w_gate_s"].rearrange("(k p) n -> p k n", p=P)).then_inc(s_ws, 16)
            sp.dma_start(WSGU[:, :, F:2 * F], a["w_up_s"].rearrange("(k p) n -> p k n", p=P)).then_inc(s_ws, 16)
            sp.dma_start(WSD, a["w_down_s"].rearrange("(k p) n -> p k n", p=P)).then_inc(s_ws, 16)
            for t in range(NT):
                sp.wait_ge(s_h2, t + 1)
                sp.dma_start(h2_dram[P * t:P * (t + 1), :], HROW[:, t % 2]).then_inc(s_hb[t % 2], 16)

            def load_expert(j, b, e):
                need(sp, s_gu, j - 1)
                sp.dma_start(WGU[b][:, :, 0:F], a["w_gate_e"][bass.ds(e, 1)].rearrange(
                    "o (k p) n -> p (o k) n", p=P)).then_inc(s_wgu[b], 16)
                sp.dma_start(WGU[b][:, :, F:2 * F], a["w_up_e"][bass.ds(e, 1)].rearrange(
                    "o (k p) n -> p (o k) n", p=P)).then_inc(s_wgu[b], 16)
                need(sp, s_dn, 2 * (j - 1))
                sp.dma_start(WDN[b], a["w_down_e"][bass.ds(e, 1)].rearrange(
                    "o (k p) n -> p (o k) n", p=P)).then_inc(s_wd[b], 16)

            sp.wait_ge(s_o, 8)
            load_expert(0, 0, 0)
            load_expert(1, 1, 1)
            sp.wait_ge(s_tabs, 1)
            npairs = (sp.value_load(nover[0:1, 0:1], min_val=0, max_val=31) + (E + 1)) // 2
            with sp.Fori(1, MAXPAIRS) as i:
                with sp.If(i < npairs):
                    for b in range(2):
                        e = sp.value_load(etab[0:1, bass.ds(2 * i + b, 1)], min_val=0, max_val=E - 1)
                        load_expert(2 * i + b, b, e)
            sp.wait_ge(s_routed, 1)
            for t in range(NT):
                if t == 3:
                    sp.wait_ge(s_fin, 1)
                sp.dma_start(FB[t], routed_dram[P * TOPK * t:P * TOPK * (t + 1), :].rearrange(
                    "(p k) d -> p (k d)", k=TOPK)).then_inc(s_fb[t % 3], 16)
            for t in range(NT):
                sp.wait_ge(s_fin, t + 1)
                sp.dma_start(a["out"][P * t:P * (t + 1), :], X[:, t, :]).then_inc(s_out, 16)
            sp.wait_ge(s_out, 16 * NT)

        @block.gpsimd
        def _(pool):
            pool.memset(CUM[:, :, :, 0:HA], 0.0).then_inc(s_pch, 1)
            pool.memset(extr[:, :], 0.0).then_inc(s_pch, 1)
            pool.wait_ge(s_tab, 16)
            pool.wait_ge(s_pch, 2)
            pool.tensor_copy(extr[:, 383:383 + 2 * REL], tabr[:, NTAB - 1:0:-1]).then_inc(s_ext, 1)
            pool.tensor_copy(extr[:, 0:383], bc(tabr[:, NTAB - 1:NTAB], [HA, 383])).then_inc(s_ext, 1)
            pool.wait_ge(s_ext, 2)
            pool.wait_ge(s_hm, 8)
            pool.dma_start(ext_dram, bc(extr[:, :].unsqueeze(1), [HA, P, EXT])).then_inc(s_extw, 16)
            pool.wait_ge(s_t4, 16)
            pool.memset(T4[0:DH, 0:HA, S - DH:S], NEG).then_inc(s_t4m, 1)
            pool.wait_ge(s_t4m, 1)
            pool.wait_ge(s_t4c, 16)
            pool.wait_ge(s_ones, 16)
            pool.wait_ge(s_norm, 4)
            pool.wait_ge(s_cumr, 2)
            pool.memset(QS[:, :, 0, :, DH + 1:DA], 1.0).then_inc(s_pch, 1)
            pool.memset(QS[:, :, 1, :, DH:DH + 1], 1.0).then_inc(s_pch, 1)
            pool.wait_ge(s_pch, 4)

            def stage(i, b, mixer):
                h = 2 * i + b
                need(pool, s_tq, 2 * h - 2)
                settle(pool)
                pool.tensor_copy(QS[:, b, 0, :, 0:DH], Z[:, 0, :, bass.ds(h * DH, DH)]).then_inc(s_stage, 1)
                pool.tensor_copy(QS[:, b, 1, :, 0:DH], Z[:, 1, :, bass.ds(h * DH, DH)]).then_inc(s_stage, 1)
                pool.tensor_copy(QS[:, b, 0, :, DH:DH + 1], CUM[:, 0, :, bass.ds(h, 1)]).then_inc(s_stage, 1)
                pool.tensor_copy(QS[:, b, 1, :, DH + 1:DA], CUM[:, 1, :, bass.ds(h, 1)]).then_inc(s_stage, 1)
                need(pool, s_sred, 3 * (h - 1))
                settle(pool)
                row = bass.ds(h, 1) if mixer == 0 else bass.ds(HA, 1)
                pool.tensor_copy(TB[:, b, :], T4[:, row, :].rearrange("p o s -> p (o s)")).then_inc(s_tb, 1)

            for b in range(2):
                stage(0, b, 0)
            with pool.Fori(1, HA // 2) as i:
                for b in range(2):
                    stage(i, b, 0)
            with pool.Fori(HA // 2, NH // 2) as i:
                for b in range(2):
                    stage(i, b, 1)

            pool.wait_ge(s_o, 8)
            pool.tensor_copy(RX[:, :, :, 0:3], bc(cst[:, C_TOK3:C_TOK3 + 12].rearrange(
                "p (t c) -> p t c", t=NT).unsqueeze(1), [P, NBLK, NT, 3])).then_inc(s_rxc, 1)
            pool.wait_ge(s_mt, 8)
            pool.wait_ge(s_ss2, 4)
            pool.memset(XG[:, 0, :], 0.0).then_inc(s_xgi, 1)
            pool.memset(XG[:, 1, :], 0.0).then_inc(s_xgi, 1)
            pool.wait_ge(s_xgi, 2)
            pool.wait_ge(s_hb[0], 32)
            pool.wait_ge(s_hb[1], 32)

            def gather(j, b):
                pool.wait_ge(s_sl, SLN * (j + 1))
                need(pool, s_xt, j - 1)
                settle(pool)
                pool.indirect_dma_start(
                    out=XG[:, b, :], out_offset=None, in_=h2_dram,
                    in_offset=bass.IndirectOffsetOnAxis(ap=gidx[b][:, 0:1], axis=0),
                    bounds_check=S - 1, oob_is_err=False).then_inc(s_gat[b], 16)

            def scatter(j, b):
                pool.wait_ge(s_oed, j + 1)
                pool.wait_ge(s_oea, j + 1)
                pool.wait_ge(s_ri, j + 1)
                settle(pool)
                pool.indirect_dma_start(
                    out=routed_dram, out_offset=bass.IndirectOffsetOnAxis(ap=ridx[b][:, 0:1], axis=0),
                    in_=OB[:, b, :], in_offset=None,
                    bounds_check=S * TOPK - 1, oob_is_err=False).then_inc(s_scat[b], 16)

            for j in range(4):
                gather(j, j % 2)
            npairs = (pool.value_load(nover[0:1, 0:1], min_val=0, max_val=31) + (E + 1)) // 2
            with pool.Fori(0, MAXPAIRS) as i:
                with pool.If(i < npairs):
                    for b in range(2):
                        j = 2 * i + b
                        scatter(j, b)
                        gather(j + 4, b)
            for b in range(2):
                pool.wait_ge(s_scat[b], 16 * npairs)
            for b in range(2):
                pool.wait_ge(s_gat[b], 16 * npairs + 32)
            pool.sem_inc(s_routed, 1)

        @block.scalar
        def _(act):
            link = Chain(act, s_ach)
            act.wait_ge(s_rowst, 1)
            act.activation(cact[:, :], PS[:, 5, 0:KD], ACT.Silu).then_inc(s_cact, 1)
            act.activation(gcol[:, :, :], PS[:, 5, KD:4 * KD].rearrange("p (r k) -> p r k", r=3), ACT.Copy)\
                .then_inc(s_cact, 1)
            for t in range(NT):
                act.wait_ge(s_x[t], 16)
                link(act.activation(JUNK, X[:, t, :], ACT.Square, accum_out=ssx[:, t:t + 1]))
            act.activation(ssx[:, 4:8], ssx[:, 0:4], ACT.Sqrt, scale=1.0 / D, bias=cst[:, C_SC:C_SC + 1])\
                .then_inc(s_ssx, 1)
            act.dma_start(tabr[:, :], a["rel_bias"]).then_inc(s_tab, 16)
            for n, g in enumerate(("qn_a", "qn_b", "kn_a", "kn_b")):
                act.dma_start(QKG[:, n // 2, n % 2, :], a[g].rearrange("(o d) -> o d", o=1).to_broadcast([P, DH]))\
                    .then_inc(s_qkg, 16)
            act.dma_start(bfg[:, :], a["b_fgate"].rearrange("(o d) -> o d", o=1).to_broadcast([P, HA]))\
                .then_inc(s_small, 16)
            act.dma_start(rbias[:, :], a["router_bias"].rearrange("(o d) -> o d", o=1).to_broadcast([P, E]))\
                .then_inc(s_small, 16)
            act.dma_start(etab[:, :], a["etab"]).then_inc(s_etab, 16)
            act.wait_ge(s_rx, 1)

            def x_row(t):
                if t >= 2:
                    act.wait_ge(s_xpose, 2 * t - 2)
                act.activation(HROW[:, t % 2], X[:, t, :], ACT.Copy, scale=ssx[:, 8 + t:9 + t]).then_inc(s_hrow, 1)
            x_row(0)
            x_row(1)
            for n in range(8):
                act.wait_ge(s_xpose, n + 1)
                if n in (2, 4):
                    x_row(n // 2 + 1)
                act.activation(HT[:, 4 * (n % 2):4 * (n % 2) + 4, P * (n // 2):P * (n // 2) + P],
                               PS[:, 6 + n % 2, :].rearrange("p (k s) -> p k s", k=4), ACT.Copy).then_inc(s_ht, 1)
            act.wait_ge(s_mcol, 1)
            act.wait_ge(s_ht, 8)
            for k in range(6, KD):
                act.activation(HT[:, k, :], HT[:, k, :], ACT.Identity, scale=mcol[:, 1, k:k + 1],
                               bias=mcol[:, 0, k:k + 1]).then_inc(s_hm, 1)
            act.sem_inc(s_zfree, 4)

            def take_qkv(r, half):
                for t in range(NT):
                    act.wait_ge(s_proj, 8 * r + 4 * half + t + 1)
                    act.activation(Z[:, bass.ds(r, 1), t, SEG * half:SEG * (half + 1)].rearrange("p o n -> p (o n)"),
                                   PS[:, t, :], ACT.Copy).then_inc(s_zfree, 1)
            take_qkv(0, 0)
            act.wait_ge(s_e, 1)
            link(act.activation(FZ[:, 2], FZ[:, 1], ACT.Exp))
            act.activation(FZ[:, 3], FZ[:, 2], ACT.Ln, bias=cst[:, C_SC + 2:C_SC + 3]).then_inc(s_e, 1)
            take_qkv(0, 1)
            with act.Fori(1, 3) as r:
                for half in range(2):
                    take_qkv(r, half)
            act.wait_ge(s_ss, 4)
            act.activation(RQ[:, 0], RQ[:, 0], ACT.Sqrt, bias=cst[:, C_SC + 1:C_SC + 2]).then_inc(s_root, 1)
            act.activation(RQ[:, 1], RQ[:, 1], ACT.Sqrt, scale=1.0 / DH, bias=cst[:, C_SC:C_SC + 1]).then_inc(s_root, 1)
            act.wait_ge(s_mod2, 1)
            act.wait_ge(s_extw, 16)
            with act.Fori(0, 2) as r:
                for half in range(2):
                    for t in range(NT):
                        act.wait_ge(s_proj, 24 + 8 * r + 4 * half + t + 1)
                        act.activation(G[:, bass.ds(r, 1), t, SEG * half:SEG * (half + 1)].rearrange("p o n -> p (o n)"),
                                       PS[:, t, :], ACT.Sigmoid).then_inc(s_zfree, 1)

            def take_qkt(h, b):
                need(act, s_s, 3 * (h - 1))
                for r in range(2):
                    act.wait_ge(s_tq, 2 * h + 1 + r)
                    act.activation(QKT[:, b, r, :], PS[0:DA, 4 + r, :], ACT.Copy).then_inc(s_qkev, 1)

            def exps(h, b):
                act.wait_ge(s_nmx, h + 1)
                need(act, s_y, h - 1)
                for i in range(NT):
                    at = P * (i * (i + 1) // 2)
                    act.activation(PB[:, b, at:at + P * (i + 1)], PB[:, b, at:at + P * (i + 1)], ACT.Exp,
                                   bias=mx[:, b, 1, i:i + 1], accum_out=sm[:, b, 0, i:i + 1]).then_inc(s_exp, 1)

            def take_pt3(h):
                act.wait_ge(s_pt, 4 * h + 4)
                act.activation(PTS[:, 768:1280], PS[:, 7, :], ACT.Copy).then_inc(s_pta, 1)

            take_qkt(0, 0)
            take_qkt(1, 1)
            exps(0, 0)
            take_qkt(2, 0)
            exps(1, 1)
            take_pt3(0)

            def heads(i):
                for b in range(2):
                    h = 2 * i + 1 + b
                    take_qkt(h + 2, 1 - b)
                    exps(h + 1, b)
                    take_pt3(h)
            heads(0)
            with act.Fori(1, 6) as i:
                heads(i)
            take_qkt(15, 1)
            exps(14, 0)
            take_pt3(13)
            exps(15, 1)
            take_pt3(14)
            take_pt3(15)

            for t in range(NT):
                act.wait_ge(s_yt, 2 * t + 2)
                act.activation(YT[:, 4:8, P * t:P * t + P],
                               PS[:, 5 + 2 * (t % 2), :].rearrange("p (k s) -> p k s", k=4), ACT.Copy).then_inc(s_ytea, 1)
            for n in range(8):
                t = n // 2
                act.wait_ge(s_mt, n + 1)
                act.activation(MT[:, 4 * (n % 2):4 * (n % 2) + 4, P * t:P * t + P],
                               PS[:, 4 + n % 4, :].rearrange("p (k s) -> p k s", k=4), ACT.Copy).then_inc(s_mte, 1)

            def take_h2t(t):
                for n in range(2 * t, 2 * t + 2):
                    act.wait_ge(s_h2t, n + 1)
                    act.activation(H2T[:, 4 * (n % 2):4 * (n % 2) + 4, P * t:P * t + P],
                                   PS[:, 4 + n % 4, :].rearrange("p (k s) -> p k s", k=4), ACT.Copy).then_inc(s_h2te, 1)
            for t in range(NT):
                act.wait_ge(s_x2, 2 * t + 2)
                link(act.activation(G[:, 0, t, :], X[:, t, :], ACT.Square, accum_out=ssx[:, t:t + 1]))
                act.activation(ssx[:, 4 + t:5 + t], ssx[:, t:t + 1], ACT.Sqrt, scale=1.0 / D,
                               bias=cst[:, C_SC:C_SC + 1]).then_inc(s_ss2, 1)
                if t:
                    take_h2t(t - 1)
            take_h2t(NT - 1)
            act.wait_ge(s_rt, 1)
            act.activation(SCT, PS[0:E, 4, :], ACT.Sigmoid).then_inc(s_sct, 1)
            for b in range(2):
                act.wait_ge(s_hb[b], 32)
            for t in range(NT):
                act.wait_ge(s_sgu, t + 1)
                act.activation(SILS[:, t, :], PS[:, t, 0:F], ACT.Silu).then_inc(s_ssil, 1)
            for t in range(NT):
                act.wait_ge(s_sat, t + 1)
                need(act, s_sdn, 2 * (t - 1))
                act.activation(AT[:, t % 2], PS[:, 6, 0:F].rearrange("p (k s) -> p k s", k=2), ACT.Copy)\
                    .then_inc(s_sate, 1)

            def take_xt(j, b):
                act.wait_ge(s_xt, j + 1)
                need(act, s_gu, j - 1)
                act.activation(XT[:, b, 4:8, :], PS[:, 5, :].rearrange("p (k s) -> p k s", k=4), ACT.Copy)\
                    .then_inc(s_xta, 1)

            def silu(j, b):
                act.wait_ge(s_gu, j + 1)
                need(act, s_act, j - 1)
                act.activation(SIL[:, b, :], PS[:, b, 0:F], ACT.Silu).then_inc(s_silu, 1)

            def take_at(j, b):
                act.wait_ge(s_at, j + 1)
                need(act, s_dn, 2 * (j - 1))
                act.activation(AT[:, b], PS[:, 6, 0:F].rearrange("p (k s) -> p k s", k=2), ACT.Copy)\
                    .then_inc(s_ate, 1)

            def take_o(i, j, b):
                act.wait_ge(s_dn, 2 * j + 2)
                need(act, s_scat[b], 16 * i)
                act.activation(OB[:, b, 512:1024], PS[:, 3, :], ACT.Copy,
                               scale=slx[:, bass.ds(j % 8, 1), 2:3].rearrange("p o c -> p (o c)")).then_inc(s_oea, 1)

            take_xt(0, 0)
            take_xt(1, 1)
            silu(0, 0)
            act.wait_ge(s_tabs, 1)
            npairs = (act.value_load(nover[0:1, 0:1], min_val=0, max_val=31) + (E + 1)) // 2

            def blocks(i):
                take_at(2 * i, 0)
                silu(2 * i + 1, 1)
                take_xt(2 * i + 2, 0)
                take_o(i, 2 * i, 0)
                take_at(2 * i + 1, 1)
                with act.If(i + 1 < npairs):
                    silu(2 * i + 2, 0)
                take_xt(2 * i + 3, 1)
                take_o(i, 2 * i + 1, 1)
            blocks(0)
            with act.Fori(1, MAXPAIRS) as i:
                with act.If(i < npairs):
                    blocks(i)

        @block.vector
        def _(dve):
            link = Chain(dve, s_dch)

            def ada_sum(u):
                src = AF[u] if u < 8 else AD[:, u % 2]
                acc = ACC[:, (BY_DVE.index(u) if u < 8 else u) % 4]
                if u < 8:
                    dve.wait_ge(s_af[u], 16)
                    if BY_DVE.index(u) >= 4:
                        dve.wait_ge(s_ada1, PE_ORDER.index(BY_DVE[BY_DVE.index(u) - 4]) + 1)
                else:
                    dve.wait_ge(s_ada[u % 2], 16 * (u // 2 - 3))
                    need(dve, s_ones, u - 11)
                link(dve.tensor_scalar(acc, src[:, 0], cact[:, 0:1], None, ALU.mult))
                for k in range(1, KD):
                    ins = dve.scalar_tensor_tensor(acc, src[:, k], cact[:, k:k + 1], acc, ALU.mult, ALU.add)
                    if k < KD - 1:
                        link(ins)
                ins.then_inc(s_acc, 1)

            def mod_add(u, at):
                dve.tensor_tensor(MOD[:, at // D, at % D:at % D + HC], MOD[:, at // D, at % D:at % D + HC],
                                  PS[:, 4 + (u % 4) // 2, HC * (u % 2):HC * (u % 2) + HC], ALU.add).then_inc(s_madd, 1)

            dve.wait_ge(s_ssx, 1)
            dve.reciprocal(ssx[:, 8:12], ssx[:, 4:8]).then_inc(s_rx, 1)
            dve.wait_ge(s_cact, 2)
            for u in BY_DVE:
                ada_sum(u)
            dve.wait_ge(s_ada1, 8)
            link(dve.tensor_tensor(mcol[:, :, :], PS[:, 4, 0:2 * KD].rearrange("p (r k) -> p r k", r=2),
                                   gcol[:, 1:3, :], ALU.add))
            dve.scalar_tensor_tensor(mcol[:, 1, :], mcol[:, 1, :], 1.0, gcol[:, 0, :], ALU.add, ALU.mult)\
                .then_inc(s_mcol, 1)
            dve.wait_ge(s_mcol, 1)
            dve.wait_ge(s_ht, 8)
            for k in range(6):
                dve.tensor_scalar(HT[:, k, :], HT[:, k, :], mcol[:, 1, k:k + 1], mcol[:, 0, k:k + 1],
                                  ALU.mult, ALU.add).then_inc(s_hm, 1)

            def log_forget():
                dve.wait_ge(s_f, 1)
                dve.wait_ge(s_small, 32)
                link(dve.tensor_tensor(FZ[:, 0], PS[:, 6, 0:32].rearrange("p (t h) -> p t h", t=NT),
                                       bc(bfg[:, :].unsqueeze(1), [P, NT, HA]), ALU.add))
                link(dve.tensor_scalar(FZ[:, 1], FZ[:, 0], -1.0, None, ALU.mult))
                dve.tensor_tensor(FZ[:, 1], FZ[:, 0], FZ[:, 1], ALU.min).then_inc(s_e, 1)
                dve.wait_ge(s_e, 2)
                link(dve.tensor_scalar(FZ[:, 0], FZ[:, 0], 0.0, None, ALU.min))
                dve.tensor_tensor(FZ[:, 0], FZ[:, 0], FZ[:, 3], ALU.subtract).then_inc(s_lf, 1)

            for g in range(4):
                for u in range(8 + 4 * g, 12 + 4 * g):
                    ada_sum(u)
                if g == 0:
                    log_forget()
                else:
                    if g == 1:
                        dve.wait_ge(s_modb, 64)
                    dve.wait_ge(s_ones, 4 * g)
                    for u in range(4 + 4 * g, 8 + 4 * g):
                        mod_add(u, HC * (u - 8))
            dve.wait_ge(s_ones, 16)
            for u in range(20, 24):
                mod_add(u, HC * (u - 8))
            dve.wait_ge(s_madd, 16)
            dve.wait_ge(s_gn, 16)
            dve.scalar_tensor_tensor(MOD[:, 1, :], MOD[:, 1, :], 1.0, GN, ALU.add, ALU.mult).then_inc(s_mod2, 1)
            dve.wait_ge(s_cum, 1)
            cps = PS[:, 7, 0:32].rearrange("p (t h) -> p t h", t=NT)
            dve.tensor_copy(CUM[:, 0, :, HA:NH], cps).then_inc(s_cumr, 1)
            dve.tensor_scalar(CUM[:, 1, :, HA:NH], cps, -1.0, None, ALU.mult).then_inc(s_cumr, 1)
            dve.wait_ge(s_qkg, 64)

            def qk(r, half):
                return Z[:, r, :, SEG * half:SEG * (half + 1)].rearrange("p t (h d) -> p t h d", h=HA)
            for r in range(2):
                for half in range(2):
                    dve.wait_ge(s_zfree, 4 + 8 * r + 4 * half + 4)
                    link(dve.tensor_tensor(SQT, Z[:, r, :, SEG * half:SEG * (half + 1)],
                                           Z[:, r, :, SEG * half:SEG * (half + 1)], ALU.mult))
                    link(dve.tensor_reduce(RQ[:, r, :, HA * half:HA * (half + 1)],
                                           SQT.rearrange("p t (h d) -> p t h d", h=HA), AX.X, ALU.add))
                    dve.sem_inc(s_ss, 1)
            dve.wait_ge(s_root, 2)
            link(dve.reciprocal(RQ[:, :, :, :].rearrange("p r t h -> p (r t h)"),
                                RQ[:, :, :, :].rearrange("p r t h -> p (r t h)")))
            for r in range(2):
                for half in range(2):
                    link(dve.tensor_tensor(qk(r, half), qk(r, half), bc(
                        RQ[:, r, :, HA * half:HA * (half + 1)].unsqueeze(3), [P, NT, HA, DH]), ALU.mult))
                    dve.tensor_tensor(qk(r, half), qk(r, half), bc(
                        QKG[:, r, half, :].unsqueeze(1).unsqueeze(1), [P, NT, HA, DH]), ALU.mult).then_inc(s_norm, 1)

            def take_scores(h, b):
                dve.wait_ge(s_tb, h + 1)
                need(dve, s_pt, 4 * (h - 1))
                for g, tiles in enumerate(((0, 2), (1,), (3,))):
                    dve.wait_ge(s_s, 3 * h + g + 1)
                    settle(dve)
                    for n, i in enumerate(tiles):
                        w, at = P * (i + 1), P * (i * (i + 1) // 2)
                        src = P if i == 2 else 0
                        ins = dve.tensor_tensor_reduce(
                            out=PB[:, b, at:at + w], in0=PS[:, g, src:src + w], in1=TB[:, b, S - w:S],
                            scale=1.0, scalar=-3e38, op0=ALU.add, op1=ALU.max, accum_out=mx[:, b, 0, i:i + 1])
                    ins.then_inc(s_sred, 1)
                dve.wait_ge(s_sred, 3 * h + 3)
                dve.tensor_scalar(mx[:, b, 1, :], mx[:, b, 0, :], -1.0, None, ALU.mult).then_inc(s_nmx, 1)

            def take_pt(h, i):
                dve.wait_ge(s_pt, 4 * h + i + 1)
                at = P * (i * (i + 1) // 2)
                dve.tensor_copy(PTS[:, at:at + P * (i + 1)], PS[:, 6 + i % 2, 0:P * (i + 1)]).then_inc(s_ptd, 1)

            def take_y(h, b):
                dve.wait_ge(s_exp, 4 * h + 4)
                link(dve.reciprocal(sm[:, b, 1, :], sm[:, b, 0, :]))
                dve.wait_ge(s_pv, 4 * h + 4)
                dve.tensor_tensor(Z[:, 0, :, bass.ds(h * DH, DH)],
                                  PS[:, 3, 0:256].rearrange("p (t d) -> p t d", t=NT),
                                  bc(sm[:, b, 1, :].unsqueeze(2), [P, NT, DH]), ALU.mult).then_inc(s_y, 1)

            take_scores(0, 0)
            take_scores(1, 1)
            for n in range(3):
                take_pt(0, n)

            def heads(i, first):
                link.enter(i, first, 2)
                for b in range(2):
                    h = 2 * i + 1 + b
                    take_scores(h + 1, b)
                    for n in range(3):
                        take_pt(h, n)
                    take_y(h - 1, b)
            heads(0, 0)
            with dve.Fori(1, 7) as i:
                heads(i, 1)
            link.leave(6)
            for n in range(3):
                take_pt(15, n)
            take_y(14, 0)
            take_y(15, 1)

            for t in range(NT):
                dve.wait_ge(s_yt, 2 * t + 1)
                dve.tensor_copy(YT[:, 0:4, P * t:P * t + P],
                                PS[:, 4 + 2 * (t % 2), :].rearrange("p (k s) -> p k s", k=4)).then_inc(s_yted, 1)
            for n in range(8):
                t, cols = n // 2, slice(512 * (n % 2), 512 * (n % 2) + 512)
                dve.wait_ge(s_u, n + 1)
                for r in range(2):
                    link(dve.tensor_tensor(G[:, r, t, cols], G[:, r, t, cols], PS[:, 2 * (n % 2) + r, :], ALU.mult))
                dve.tensor_tensor(G[:, 0, t, cols], G[:, 0, t, cols], G[:, 1, t, cols], ALU.add).then_inc(s_m, 1)

            def h2_rows(t):
                dve.wait_ge(s_ss2, t + 1)
                link(dve.reciprocal(ssx[:, 8 + t:9 + t], ssx[:, 4 + t:5 + t]))
                if t >= 2:
                    dve.wait_ge(s_h2t, 2 * t - 2)
                    dve.wait_ge(s_hb[t % 2], 16)
                link(dve.scalar_tensor_tensor(HROW[:, t % 2], X[:, t, :], ssx[:, 8 + t:9 + t], MOD[:, 1, :],
                                              ALU.mult, ALU.mult))
                dve.tensor_tensor(HROW[:, t % 2], HROW[:, t % 2], MOD[:, 0, :], ALU.add).then_inc(s_h2, 1)

            for n in range(8):
                t, cols = n // 2, slice(512 * (n % 2), 512 * (n % 2) + 512)
                dve.wait_ge(s_o, n + 1)
                link(dve.tensor_tensor(G[:, 1, t, cols], PS[:, n % 4, :], MOD[:, 2, cols], ALU.mult))
                dve.tensor_tensor(X[:, t, cols], X[:, t, cols], G[:, 1, t, cols], ALU.add).then_inc(s_x2, 1)
                if n % 2 and t:
                    h2_rows(t - 1)
            h2_rows(NT - 1)

            dve.wait_ge(s_sc, 1)
            gsum, cnt, gm, ng = (gs[:, n, :].rearrange("p (t g) -> p t g", t=NT) for n in range(4))
            link(dve.tensor_copy(SC, PS[:, 5, 0:256].rearrange("p (t e) -> p t e", t=NT)))
            link(dve.tensor_tensor(BI, SC, bc(rbias[:, :].unsqueeze(1), [P, NT, E]), ALU.add))
            for t in range(NT):
                for g in range(NG):
                    ins = dve.max(M8[:, NG * t + g, :], BI[:, t, 8 * g:8 * g + 8])
            link(ins)
            link(dve.tensor_tensor(gs[:, 0, :].unsqueeze(2), M8[:, :, 0:1], M8[:, :, 1:2], ALU.add))
            mine = bc(gsum.unsqueeze(3), [P, NT, NG, NG])
            other = bc(gsum.unsqueeze(2), [P, NT, NG, NG])
            low = bc(cst[:, C_LOW:C_LOW + 64].rearrange("p (g u) -> p g u", g=NG).unsqueeze(1), [P, NT, NG, NG])
            link(dve.tensor_tensor(GE, other, mine, ALU.is_equal))
            link(dve.tensor_tensor(GE, GE, low, ALU.mult))
            link(dve.tensor_tensor(GT, other, mine, ALU.is_gt))
            link(dve.tensor_tensor(GT, GT, GE, ALU.add))
            link(dve.tensor_reduce(cnt, GT, AX.X, ALU.add))
            link(dve.tensor_scalar(gm, cnt, float(TOPG) - 0.5, None, ALU.is_lt))
            link(dve.tensor_scalar(ng, gm, -NEG, NEG, ALU.mult, ALU.add))
            for t in range(NT):
                v = MB[:, t, :].rearrange("p (g u) -> p g u", g=NG)
                link(dve.tensor_tensor(v, BI[:, t, :].rearrange("p (g u) -> p g u", g=NG),
                                       bc(gm[:, t, :].unsqueeze(2), [P, NG, 8]), ALU.mult))
                link(dve.tensor_tensor(v, v, bc(ng[:, t, :].unsqueeze(2), [P, NG, 8]), ALU.add))
                link(dve.max(V8[:, t, :], MB[:, t, :]))
                link(dve.match_replace(RP[:, t, :], V8[:, t, :], MB[:, t, :], -3e38))
            dve.tensor_scalar(SEL, RP, -2e38, None, ALU.is_lt).then_inc(s_sel, 1)
            dve.wait_ge(s_sel, 1)
            link(dve.tensor_tensor(WT, SC, SEL, ALU.mult))
            link(dve.tensor_reduce(ws[:, 0, :], WT, AX.X, ALU.add))
            link(dve.reciprocal(ws[:, 1, :], ws[:, 0, :]))
            link(dve.tensor_tensor(WT, WT, bc(ws[:, 1, :].unsqueeze(2), [P, NT, E]), ALU.mult))
            link(dve.tensor_scalar(WT, WT, ROUTED_SCALE, None, ALU.mult))
            for t in range(NT):
                link(dve.tensor_tensor_scan(RV[:, t, :], cst[:, C_ONE:C_ONE + E], SEL[:, t, :], 0.0, ALU.mult, ALU.add))
            link(dve.tensor_tensor(RV, RV, SEL, ALU.subtract))
            link(dve.tensor_tensor(RV, RV, bc(cst[:, C_TOKR:C_TOKR + NT].unsqueeze(2), [P, NT, E]), ALU.add))
            dve.wait_ge(s_pos, 1)
            link(dve.scalar_tensor_tensor(Q1, PS[:, 4, 0:256].rearrange("p (t e) -> p t e", t=NT), 1.0, SEL,
                                          ALU.add, ALU.mult))
            dve.sem_inc(s_q1, 1)
            link(dve.tensor_scalar(ob[:, 0:1], PS[0:E, 4, 256:257], float(P) + 0.5, None, ALU.is_gt))
            link(dve.tensor_scalar(ob[:, 1:2], PS[0:E, 4, 256:257], 2.0 * P + 0.5, None, ALU.is_gt))
            link(dve.tensor_scalar(ob[:, 2:3], PS[0:E, 4, 256:257], 3.0 * P + 0.5, None, ALU.is_gt))
            link(dve.tensor_tensor(ob[:, 3:4], ob[:, 0:1], ob[:, 1:2], ALU.add))
            dve.tensor_tensor(ob[:, 3:4], ob[:, 3:4], ob[:, 2:3], ALU.add).then_inc(s_ob, 1)
            perm = "p t e -> p e t"
            link(dve.tensor_copy(PM[:, 0:E, :], Q1.rearrange(perm)))
            link(dve.tensor_copy(RX[:, 0:E, :, R_LO], RV.rearrange(perm)))

            def split(lo, hi, w, left):
                link(dve.tensor_copy(RX[:, lo:hi, :, W_1], w))
                link(dve.tensor_tensor(left, w, RX[:, lo:hi, :, W_1], ALU.subtract))
                link(dve.tensor_copy(RX[:, lo:hi, :, W_2], left))
                link(dve.tensor_tensor(left, left, RX[:, lo:hi, :, W_2], ALU.subtract))
                link(dve.tensor_copy(RX[:, lo:hi, :, W_3], left))
            split(0, E, WT.rearrange(perm), wres.rearrange(perm))

            def shared_act(t):
                dve.wait_ge(s_ssil, t + 1)
                dve.tensor_tensor(ACTS[:, t, :], SILS[:, t, :], PS[:, t, F:2 * F], ALU.mult).then_inc(s_sact, 1)
            shared_act(0)
            shared_act(1)
            dve.wait_ge(s_oend, 1)
            m36 = cst[0:E, C_M:C_M + NEXT]
            link(dve.tensor_copy(ob[:, 4:5], PS[0:E, 4, 0:1]))
            link(dve.tensor_tensor(ob[:, 5:6], ob[:, 4:5], ob[:, 3:4], ALU.subtract))
            link(dve.tensor_scalar(OH[:, 0, :], m36, ob[:, 5:6], None, ALU.is_ge))
            link(dve.scalar_tensor_tensor(OH[:, 0, :], m36, ob[:, 4:5], OH[:, 0, :], ALU.is_lt, ALU.mult))
            link(dve.tensor_scalar(OH[:, 1, :], m36, ob[:, 5:6], 1.0, ALU.subtract, ALU.add))
            dve.scalar_tensor_tensor(OH[:, 1, :], OH[:, 1, :], float(P), OH[:, 0, :], ALU.mult, ALU.mult)\
                .then_inc(s_oh1, 1)
            for n, (dst, bank) in enumerate(((Q1T, 5), (WTT, 6), (RVT, 7))):
                dve.wait_ge(s_tr, n + 1)
                dve.tensor_copy(dst, PS[0:E, bank, :]).then_inc(s_trd, 1)
            shared_act(2)
            shared_act(3)
            dve.wait_ge(s_xm, 1)
            for col, dst in enumerate((PM[:, E:NBLK, :], wxr[:, :, :].rearrange("p t m -> p m t"),
                                       RX[:, E:NBLK, :, R_LO])):
                link(dve.tensor_copy(dst, PS[:, 4, 144 * col:144 * (col + 1)].rearrange("p (t m) -> p m t", t=NT)))
            split(E, NBLK, wxr[:, :, :].rearrange("p t m -> p m t"), wxr[:, :, :].rearrange("p t m -> p m t"))
            dve.wait_ge(s_rxc, 1)
            dve.wait_ge(s_etab, 16)
            link(dve.tensor_copy(nover[:, :], PS[0:1, 4, 468:469]))
            dve.tensor_copy(etab[:, E:NBLK], PS[0:1, 4, 432:468]).then_inc(s_tabs, 1)

            def shared_add(t):
                for n in range(2 * t, 2 * t + 2):
                    cols = slice(512 * (n % 2), 512 * (n % 2) + 512)
                    dve.wait_ge(s_sdn, n + 1)
                    link(dve.tensor_tensor(G[:, 1, 3, cols], PS[:, 2 + n % 2, :], MOD[:, 3, cols], ALU.mult))
                    link(dve.tensor_tensor(X[:, t, cols], X[:, t, cols], G[:, 1, 3, cols], ALU.add))
                    dve.sem_inc(s_sx, 1)

            def onehot(j, b):
                need(dve, s_ohd, j - 1)
                dve.tensor_tensor(AH[:, b], bc(cst[:, C_SLOT:C_SLOT + P].unsqueeze(1), [P, NT, P]),
                                  bc(PM[:, bass.ds(j, 1), :].rearrange("p o t -> p (o t)").unsqueeze(2), [P, NT, P]),
                                  ALU.is_equal).then_inc(s_ah, 1)

            def slots(j, b):
                def col(c):
                    return slx[:, bass.ds(j % 8, 1), c:c + 1].rearrange("p o c -> p (o c)")
                dve.wait_ge(s_ohd, j + 1)
                need(dve, s_xt, j - 1)
                dve.tensor_copy(slc[:, :], PS[:, 7, 0:NCOL]).then_inc(s_sl, 1)
                dve.wait_ge(s_sl, SLN * j + 1)
                dve.scalar_tensor_tensor(col(1), slc[:, R_HI:R_HI + 1], NOROW, slc[:, R_LO:R_LO + 1],
                                         ALU.add, ALU.add).then_inc(s_sl, 1)
                dve.tensor_tensor(col(0), slc[:, W_1:W_1 + 1], slc[:, W_2:W_2 + 1], ALU.add).then_inc(s_w12, 1)
                dve.wait_ge(s_w12, j + 1)
                dve.tensor_tensor(col(2), col(0), slc[:, W_3:W_3 + 1], ALU.add).then_inc(s_sl, 1)
                dve.scalar_tensor_tensor(gidx[b][:, :], slc[:, T_HI:T_HI + 1], NOTOK, slc[:, T_LO:T_LO + 1],
                                         ALU.add, ALU.add).then_inc(s_sl, 1)

            def take_xt(j, b):
                dve.wait_ge(s_xt, j + 1)
                need(dve, s_gu, j - 1)
                dve.tensor_copy(XT[:, b, 0:4, :], PS[:, 4, :].rearrange("p (k s) -> p k s", k=4)).then_inc(s_xtd, 1)

            def mul(j, b):
                dve.wait_ge(s_silu, j + 1)
                need(dve, s_at, j - 1)
                dve.tensor_tensor(AR[:, b, :], SIL[:, b, :], PS[:, b, F:2 * F], ALU.mult).then_inc(s_act, 1)

            def take_o(i, j, b):
                need(dve, s_scat[b], 16 * i)
                dve.wait_ge(s_sl, SLN * (j + 1))
                dve.tensor_copy(ridx[b][:, :], slx[:, bass.ds(j % 8, 1), 1:2].rearrange("p o c -> p (o c)"))\
                    .then_inc(s_ri, 1)
                dve.wait_ge(s_dn, 2 * j + 1)
                dve.tensor_scalar(OB[:, b, 0:512], PS[:, 2, :],
                                  slx[:, bass.ds(j % 8, 1), 2:3].rearrange("p o c -> p (o c)"), None,
                                  ALU.mult).then_inc(s_oed, 1)

            dve.wait_ge(s_tabs, 1)
            for b in range(2):
                dve.wait_ge(s_hb[b], 32)
            npairs = (dve.value_load(nover[0:1, 0:1], min_val=0, max_val=31) + (E + 1)) // 2
            onehot(0, 0)
            onehot(1, 1)
            shared_add(0)
            slots(0, 0)
            onehot(2, 0)
            slots(1, 1)
            onehot(3, 1)
            shared_add(1)
            shared_add(2)
            take_xt(0, 0)
            shared_add(3)
            take_xt(1, 1)
            slots(2, 0)
            slots(3, 1)
            mul(0, 0)

            def blocks(i):
                onehot(2 * i + 4, 0)
                mul(2 * i + 1, 1)
                take_xt(2 * i + 2, 0)
                slots(2 * i + 4, 0)
                take_o(i, 2 * i, 0)
                onehot(2 * i + 5, 1)
                with dve.If(i + 1 < npairs):
                    mul(2 * i + 2, 0)
                take_xt(2 * i + 3, 1)
                slots(2 * i + 5, 1)
                take_o(i, 2 * i + 1, 1)
            blocks(0)
            with dve.Fori(1, MAXPAIRS) as i:
                with dve.If(i < npairs):
                    blocks(i)

            for t in range(NT):
                dve.wait_ge(s_fb[t % 3], 16 * (t // 3 + 1))
                for w in (4 * D, 2 * D, D):
                    link(dve.tensor_tensor(FB[t][:, 0:w], FB[t][:, 0:w], FB[t][:, w:2 * w], ALU.add))
                link(dve.tensor_tensor(FB[t][:, 0:D], FB[t][:, 0:D], MOD[:, 3, :], ALU.mult))
                dve.tensor_tensor(X[:, t, :], X[:, t, :], FB[t][:, 0:D], ALU.add).then_inc(s_fin, 1)

        @block.tensor
        def _(pe):
            mm = pe.matmul

            def spread(us):
                for u in us:
                    ins = mm(PS[:, 4 + (u % 4) // 2, HC * (u % 2):HC * (u % 2) + HC], ones, ACC[:, u % 4],
                             start=True, stop=True)
                ins.then_inc(s_ones, len(us))

            pe.wait_ge(s_cst, 16)
            pe.wait_ge(s_rows, 48)
            pe.transpose(PS[:, 5, 0:32], ROWS, ident[0:32, 0:32]).then_inc(s_rowst, 1)

            def turn(dst_bank, src, ready):
                for k in range(4):
                    ins = pe.transpose(PS[:, dst_bank, P * k:P * k + P], src[:, P * k:P * k + P], ident)
                ins.then_inc(ready, 1)

            def turn_row(t):
                pe.wait_ge(s_hrow, t + 1)
                for half in range(2):
                    need(pe, s_ht, 2 * t - 1 + half)
                    turn(6 + half, HROW[:, t % 2, 512 * half:512 * half + 512], s_xpose)

            def ada_by_feature(u):
                if u in BY_PE:
                    pe.wait_ge(s_cact, 1)
                    pe.wait_ge(s_af[u], 16)
                else:
                    pe.wait_ge(s_acc, BY_DVE.index(u) + 1)
                for half in range(2):
                    out, cols = PS[:, 4, 2 * u + half:2 * u + half + 1], slice(P * half, P * half + P)
                    if u in BY_PE:
                        for k in range(KD):
                            ins = mm(out, AF[u][:, k, cols], cact[:, k:k + 1], start=k == 0, stop=k == KD - 1)
                    else:
                        ins = mm(out, ACC[:, BY_DVE.index(u) % 4, cols], ones[:, 0:1], start=True, stop=True)
                ins.then_inc(s_ada1, 1)

            turn_row(0)
            turn_row(1)
            ada_by_feature(PE_ORDER[0])
            turn_row(2)
            turn_row(3)
            for u in PE_ORDER[1:]:
                ada_by_feature(u)
            pe.wait_ge(s_hm, 8)

            def forget():
                pe.wait_ge(s_wf, 16)
                for t in range(NT):
                    for k in range(KD):
                        ins = mm(PS[:, 6, HA * t:HA * t + HA], HT[:, k, P * t:P * t + P], WF[:, k, :],
                                 start=k == 0, stop=k == KD - 1)
                ins.then_inc(s_f, 1)

            def project(i, b):
                pe.wait_ge(s_w[b], 16 * (i + 1))
                for t in range(NT):
                    pe.wait_ge(s_zfree, 8 * i + 4 * b + t + 1)
                    for k in range(KD):
                        ins = mm(PS[:, t, :], HT[:, k, P * t:P * t + P], WR[:, b, k, :],
                                 start=k == 0, stop=k == KD - 1)
                    ins.then_inc(s_proj, 1)

            for i in range(2):
                for b in range(2):
                    project(i, b)
                    if i == 0 and b == 0:
                        forget()
                    pe.wait_ge(s_acc, 10 + 4 * (2 * i + b))
                    need(pe, s_madd, 4 * (2 * i + b))
                    spread(range(8 + 4 * (2 * i + b), 12 + 4 * (2 * i + b)))
            pe.wait_ge(s_lf, 1)
            for t in range(NT):
                for j in range(t + 1):
                    ins = mm(PS[:, 7, HA * t:HA * t + HA], cst[:, C_TIN:C_TIN + P] if j == t else ones,
                             FZ[:, 0, j, :], start=j == 0, stop=j == t)
            ins.then_inc(s_cum, 1)
            with pe.Fori(2, 5) as i:
                for b in range(2):
                    project(i, b)

            def turn_qk(h, b):
                pe.wait_ge(s_stage, 4 * h + 4)
                for r in range(2):
                    need(pe, s_qkev, 2 * h - 1 + r)
                    for t in range(NT):
                        ins = pe.transpose(PS[0:DA, 4 + r, P * t:P * t + P], QS[:, b, r, t, :], ident)
                    ins.then_inc(s_tq, 1)

            def scores(h, b):
                pe.wait_ge(s_qkev, 2 * h + 2)
                for g, tiles in enumerate(((0, 2), (1,), (3,))):
                    need(pe, s_sred, 3 * h - 2 + g)
                    for i in tiles:
                        at = P if i == 2 else 0
                        ins = mm(PS[:, g, at:at + P * (i + 1)], QKT[:, b, 0, P * i:P * i + P],
                                 QKT[:, b, 1, 0:P * (i + 1)], start=True, stop=True)
                    ins.then_inc(s_s, 1)

            def turn_p(h, b, i):
                at = P * (i * (i + 1) // 2)
                pe.wait_ge(s_exp, 4 * h + i + 1)
                if i == 1:
                    need(pe, s_pta, h)
                else:
                    need(pe, s_ptd, 3 * h + (0, 0, 1, 2)[i])
                for j in range(i + 1):
                    ins = pe.transpose(PS[:, 6 + i % 2, P * j:P * j + P], PB[:, b, at + P * j:at + P * j + P], ident)
                ins.then_inc(s_pt, 1)

            def pv(h, i):
                at = P * (i * (i + 1) // 2)
                if i == 3:
                    pe.wait_ge(s_pta, h + 1)
                else:
                    pe.wait_ge(s_ptd, 3 * h + i + 1)
                if i == 0:
                    need(pe, s_y, h)
                for j in range(i + 1):
                    ins = mm(PS[:, 3, DH * i:DH * i + DH], PTS[:, at + P * j:at + P * j + P],
                             Z[:, 2, j, bass.ds(h * DH, DH)], start=j == 0, stop=j == i)
                ins.then_inc(s_pv, 1)

            pe.wait_ge(s_cumr, 2)
            pe.wait_ge(s_madd, 16)
            turn_qk(0, 0)
            pe.wait_ge(s_zfree, 44)
            turn_qk(1, 1)
            scores(0, 0)
            scores(1, 1)
            turn_qk(2, 0)
            for n in range(4):
                turn_p(0, 0, n)

            def heads(i):
                for b in range(2):
                    h = 2 * i + 1 + b
                    scores(h + 1, b)
                    turn_qk(h + 2, 1 - b)
                    for n in range(4):
                        pv(h - 1, n)
                        turn_p(h, 1 - b, n)
            for i in range(1):
                heads(i)
            with pe.Fori(1, 6) as i:
                heads(i)
            scores(14, 0)
            turn_qk(15, 1)
            for n in range(4):
                pv(12, n)
                turn_p(13, 1, n)
            scores(15, 1)
            for h in (14, 15):
                for n in range(4):
                    pv(h - 1, n)
                    turn_p(h, h % 2, n)
            for n in range(4):
                pv(15, n)

            pe.wait_ge(s_y, 16)
            pe.wait_ge(s_qkev, 32)
            pe.wait_ge(s_ptd, 48)
            pe.wait_ge(s_pta, 16)
            for t in range(NT):
                for half in range(2):
                    need(pe, s_ytea if half else s_yted, t - 1)
                    turn(4 + 2 * (t % 2) + half, Z[:, 0, t, 512 * half:512 * half + 512], s_yt)
            pe.wait_ge(s_sred, 48)
            pe.wait_ge(s_yted, 4)
            pe.wait_ge(s_ytea, 4)
            pe.wait_ge(s_wp, 32)

            def merge(t):
                for half in range(2):
                    n = 2 * t + half
                    need(pe, s_m, n - 1)
                    for r, w in enumerate((WPA, WPB)):
                        for k in range(4):
                            ins = mm(PS[:, 2 * half + r, :], YT[:, 4 * r + k, P * t:P * t + P],
                                     w[:, k, 512 * half:512 * half + 512], start=k == 0, stop=k == 3)
                    ins.then_inc(s_u, 1)

            def turn_m(t):
                pe.wait_ge(s_m, 2 * t + 2)
                for half in range(2):
                    need(pe, s_mte, 2 * t + half - 3)
                    turn(4 + (2 * t + half) % 4, G[:, 0, t, 512 * half:512 * half + 512], s_mt)
            merge(0)
            for t in range(1, NT):
                merge(t)
                turn_m(t - 1)
            turn_m(NT - 1)
            pe.wait_ge(s_mte, 8)
            pe.wait_ge(s_wo, 16)

            def turn_h2(t):
                pe.wait_ge(s_h2, t + 1)
                for half in range(2):
                    need(pe, s_h2te, 2 * t + half - 3)
                    turn(4 + (2 * t + half) % 4, HROW[:, t % 2, 512 * half:512 * half + 512], s_h2t)
            for n in range(8):
                t, half = n // 2, n % 2
                need(pe, s_x2, n - 3)
                for k in range(KD):
                    ins = mm(PS[:, n % 4, :], MT[:, k, P * t:P * t + P], WO[:, k, 512 * half:512 * half + 512],
                             start=k == 0, stop=k == KD - 1)
                ins.then_inc(s_o, 1)
                if half and t >= 2:
                    turn_h2(t - 2)
            def shared_gate_up(t):
                need(pe, s_x2, 5 + t)
                for k in range(KD):
                    ins = mm(PS[:, t, :], H2T[:, k, P * t:P * t + P], WSGU[:, k, :], start=k == 0, stop=k == KD - 1)
                ins.then_inc(s_sgu, 1)

            pe.wait_ge(s_h2te, 4)
            pe.wait_ge(s_ws, 64)
            shared_gate_up(0)
            turn_h2(2)
            turn_h2(3)
            pe.wait_ge(s_h2te, 8)
            for k in range(KD):
                ins = mm(PS[0:E, 4, :], WRT[:, k, :], H2T[:, k, :], start=k == 0, stop=k == KD - 1)
            ins.then_inc(s_rt, 1)
            pe.wait_ge(s_sct, 1)
            for t in range(NT):
                ins = pe.transpose(PS[:, 5, E * t:E * t + E], SCT[:, P * t:P * t + P], ident[0:E, 0:E])
            ins.then_inc(s_sc, 1)
            shared_gate_up(1)
            shared_gate_up(2)
            pe.wait_ge(s_sel, 1)
            for t in range(NT):
                for j in range(t + 1):
                    mm(PS[:, 4, E * t:E * t + E], cst[:, C_TEX:C_TEX + P] if j == t else ones, SEL[:, j, :],
                       start=j == 0, stop=j == t)
            for j in range(NT):
                ins = mm(PS[0:E, 4, 256:257], SEL[:, j, :], ones[:, 0:1], start=j == 0, stop=j == NT - 1)
            ins.then_inc(s_pos, 1)
            shared_gate_up(3)
            pe.wait_ge(s_ob, 1)
            mm(PS[0:E, 4, 0:1], cst[0:E, C_TIN:C_TIN + E], ob[:, 3:4], start=True, stop=True).then_inc(s_oend, 1)
            pe.wait_ge(s_q1, 1)
            for bank, src in ((5, Q1), (6, WT), (7, RV)):
                for t in range(NT):
                    ins = pe.transpose(PS[0:E, bank, P * t:P * t + P], src[:, t, :], ident)
                ins.then_inc(s_tr, 1)

            def shared_turn(t):
                pe.wait_ge(s_sact, t + 1)
                need(pe, s_sate, t)
                for k in range(2):
                    ins = pe.transpose(PS[:, 6, P * k:P * k + P], ACTS[:, t, P * k:P * k + P], ident)
                ins.then_inc(s_sat, 1)

            def shared_down(t):
                pe.wait_ge(s_sate, t + 1)
                for half in range(2):
                    need(pe, s_sx, 2 * t + half - 1)
                    for k in range(2):
                        ins = mm(PS[:, 2 + half, :], AT[:, t % 2, k, :], WSD[:, k, 512 * half:512 * half + 512],
                                 start=k == 0, stop=k == 1)
                    ins.then_inc(s_sdn, 1)

            pe.wait_ge(s_trd, 3)
            shared_turn(0)
            pe.wait_ge(s_oh1, 1)
            for t in range(NT):
                at = NEXT * t
                mm(PS[:, 4, at:at + NEXT], Q1T[:, P * t:P * t + P], OH[:, 0, :], start=True, stop=False)
                mm(PS[:, 4, at:at + NEXT], cst[0:E, C_NEG1:C_NEG1 + P], OH[:, 1, :], start=False, stop=True)
            for n, src in ((1, WTT), (2, RVT)):
                for t in range(NT):
                    at = 144 * n + NEXT * t
                    mm(PS[:, 4, at:at + NEXT], src[:, P * t:P * t + P], OH[:, 0, :], start=True, stop=True)
            mm(PS[0:1, 4, 432:468], cst[0:E, C_E:C_E + 1], OH[:, 0, :], start=True, stop=True)
            mm(PS[0:1, 4, 468:469], ob[:, 3:4], ones[0:E, 0:1], start=True, stop=True).then_inc(s_xm, 1)

            def slot_rows(j, b):
                pe.wait_ge(s_ah, j + 1)
                need(pe, s_sl, SLN * j)
                for t in range(NT):
                    ins = mm(PS[:, 7, 0:NCOL], AH[:, b, t, :], RX[:, bass.ds(j, 1), t, :].rearrange("p o c -> p (o c)"),
                             start=t == 0, stop=t == NT - 1)
                ins.then_inc(s_ohd, 1)

            def turn_x(i, j, b):
                pe.wait_ge(s_gat[b], 16 * (i + 1))
                need(pe, s_xtd, j)
                need(pe, s_xta, j)
                for half in range(2):
                    for k in range(4):
                        ins = pe.transpose(PS[:, 4 + half, P * k:P * k + P],
                                           XG[:, b, 512 * half + P * k:512 * half + P * k + P], ident)
                ins.then_inc(s_xt, 1)

            def gate_up(i, j, b):
                pe.wait_ge(s_xtd, j + 1)
                pe.wait_ge(s_xta, j + 1)
                pe.wait_ge(s_wgu[b], 32 * (i + 1))
                need(pe, s_act, j - 1)
                for k in range(KD):
                    ins = mm(PS[:, b, :], XT[:, b, k, :], WGU[b][:, k, :], start=k == 0, stop=k == KD - 1)
                ins.then_inc(s_gu, 1)

            def turn_act(j, b):
                pe.wait_ge(s_act, j + 1)
                need(pe, s_ate, j)
                for k in range(2):
                    ins = pe.transpose(PS[:, 6, P * k:P * k + P], AR[:, b, P * k:P * k + P], ident)
                ins.then_inc(s_at, 1)

            def down(i, j, b):
                pe.wait_ge(s_ate, j + 1)
                pe.wait_ge(s_wd[b], 16 * (i + 1))
                for half in range(2):
                    need(pe, s_oea if half else s_oed, j)
                    for k in range(2):
                        ins = mm(PS[:, 2 + half, :], AT[:, b, k, :], WDN[b][:, k, 512 * half:512 * half + 512],
                                 start=k == 0, stop=k == 1)
                    ins.then_inc(s_dn, 1)

            pe.wait_ge(s_sact, 4)
            shared_turn(1)
            shared_down(0)
            pe.wait_ge(s_tabs, 1)
            slot_rows(0, 0)
            slot_rows(1, 1)
            shared_turn(2)
            shared_down(1)
            shared_turn(3)
            shared_down(2)
            turn_x(0, 0, 0)
            shared_down(3)
            turn_x(0, 1, 1)
            slot_rows(2, 0)
            slot_rows(3, 1)
            gate_up(0, 0, 0)
            pe.wait_ge(s_sx, 8)
            npairs = (pe.value_load(nover[0:1, 0:1], min_val=0, max_val=31) + (E + 1)) // 2

            def blocks(i):
                gate_up(i, 2 * i + 1, 1)
                turn_act(2 * i, 0)
                turn_x(i + 1, 2 * i + 2, 0)
                slot_rows(2 * i + 4, 0)
                down(i, 2 * i, 0)
                with pe.If(i + 1 < npairs):
                    gate_up(i + 1, 2 * i + 2, 0)
                turn_act(2 * i + 1, 1)
                turn_x(i + 1, 2 * i + 3, 1)
                slot_rows(2 * i + 5, 1)
                down(i, 2 * i + 1, 1)
            blocks(0)
            with pe.Fori(1, MAXPAIRS) as i:
                with pe.If(i < npairs):
                    blocks(i)


_INS = ["x", "c", "ada_w", "ada_b", "mix_norm_g", "w_in", "b_fgate", "qn_a", "kn_a", "qn_b", "kn_b", "rel_bias",
        "w_proj_a", "w_proj_b", "w_out", "ffn_norm_g", "w_router", "router_bias", "w_gate_e", "w_up_e", "w_down_e",
        "w_gate_s", "w_up_s", "w_down_s"]


def kernel(**inputs):
    import concourse.bacc as bacc
    from concourse.bass_utils import run_bass_kernel_spmd

    nc = bacc.Bacc("TRN2", target_bir_lowering=False, num_devices=1)
    arrays, aps = {}, {}

    def give(name, array):
        arrays[name] = array
        aps[name] = nc.dram_tensor(name, array.shape, mybir.dt.from_np(array.dtype), kind="ExternalInput").ap()

    for name in _INS:
        array = np.ascontiguousarray(inputs[name])
        give(name, array if name == "c" else array.reshape(array.shape[1:]))
    for name, array in zip(("consts", "causal", "etab"), constants()):
        give(name, array)
    aps["out"] = nc.dram_tensor("out", (S, D), mybir.dt.float32, kind="ExternalOutput").ap()
    build(nc, aps)
    r = run_bass_kernel_spmd(nc, [arrays], core_ids=[0])
    return r.results[0]["out"].reshape(1, S, D)
```

```python
import contextlib

import numpy as np

import concourse.bass as bass
from concourse import mybir

P = 128
D = 1024
S = 512
DH = 64
HA = 8
NH = 16
NT = S // P
KD = D // P
E = 64
NG = 8
TOPG = 4
TOPK = 8
F = 256
EPS = 1e-6
ROUTED_SCALE = 2.5
REL = 128
NTAB = 2 * REL + 1
EXT = 640
HC = 256
SEG = 512
DA = DH + 2
NBLK = 64 + 36
NEXT = NBLK - E
PAIRS = E // 2
OVER_GROUPS, OVER_PAIRS = 4, 4
NEG = -1e30
NOTOK = 1024.0
T_HI, T_LO, W_1, W_2, W_3, NCOL = range(6)
SLN = 4

C_ID, C_TEX, C_TIN, C_ONE, C_SLOT = 0, 128, 256, 384, 512
C_TOK2, C_M, C_E, C_LOW, C_SC, C_NEG1 = 640, 648, 684, 685, 749, 757
C_N = 757 + 128


def constants():
    c = np.zeros((P, C_N), np.float32)
    p = np.arange(P)[:, None]
    f = np.arange(P)[None, :]
    c[:, C_ID:C_ID + P] = p == f
    c[:, C_TEX:C_TEX + P] = p < f
    c[:, C_TIN:C_TIN + P] = p <= f
    c[:, C_ONE:C_ONE + P] = 1.0
    c[:, C_SLOT:C_SLOT + P] = f + 1
    token = p + P * np.arange(NT)[None]
    c[:, C_TOK2 + T_HI:C_TOK2 + 8:2] = token // 8 * 8 - NOTOK
    c[:, C_TOK2 + T_LO:C_TOK2 + 8:2] = token % 8
    c[:, C_M:C_M + NEXT] = np.arange(NEXT)[None]
    c[:, C_E:C_E + 1] = p
    c[:, C_LOW:C_LOW + 64] = (np.arange(8)[None, :] < np.arange(8)[:, None]).reshape(1, 64)
    c[:, C_SC:C_SC + 3] = [EPS, DH * EPS, 1.0]
    c[:, C_NEG1:C_NEG1 + P] = -1.0
    causal = np.zeros((P, S), np.float32)
    causal[:, S - P:] = np.where(f > p, NEG, 0.0)
    etab = np.zeros((1, NBLK), np.int32)
    etab[0, :E] = np.arange(E)
    return c, causal, etab


def build(nc, a):
    f32, i32, bf16 = mybir.dt.float32, mybir.dt.int32, mybir.dt.bfloat16
    ALU, ACT, AX = mybir.AluOpType, mybir.ActivationFunctionType, mybir.AxisListType

    st = contextlib.ExitStack()
    with st:
        def sb(name, shape, dt=f32):
            return st.enter_context(nc.sbuf_tensor(name, shape, dt))

        def sem(name):
            return st.enter_context(nc.semaphore(name))

        h2_dram = nc.dram_tensor("h2_rows", (S, D), f32).ap()
        ext_dram = nc.dram_tensor("bias_rows", (HA, P, EXT), f32).ap()

        cst = sb("cst", [P, C_N])
        X = sb("X", [P, NT, D])
        MOD = sb("MOD", [P, 4, D])
        R_HT = sb("R_HT", [P, 4096])
        R_Z = sb("R_Z", [P, 12288])
        R_G = sb("R_G", [P, 8192])
        R_W = sb("R_W", [P, 8192])
        R_T = sb("R_T", [P, 4608])
        R_S = sb("R_S", [P, 3616])
        R_A = sb("R_A", [P, 1024])

        HT = R_HT[:, :].rearrange("p (k s) -> p k s", k=KD)
        Z = R_Z[:, :].rearrange("p (r t n) -> p r t n", r=3, t=NT)
        G = R_G[:, :].rearrange("p (r t n) -> p r t n", r=2, t=NT)
        WR = R_W[:, :].rearrange("p (b k n) -> p b k n", b=2, k=KD)
        AD = R_T[:, 0:4096].rearrange("p (b k n) -> p b k n", b=2, k=KD)
        AF = [R_Z[:, 2048 * u:2048 * (u + 1)].rearrange("p (k n) -> p k n", k=KD) for u in range(6)]\
            + [AD[:, 0], AD[:, 1]]
        ROWS = R_A[0:32, 0:P]
        ACC = R_A[:, :].rearrange("p (b n) -> p b n", b=4)
        HROW = R_S[:, 0:2048].rearrange("p (b n) -> p b n", b=2)
        JUNK = R_S[:, 2048:3072]
        SQT = R_S[:, 0:2048].rearrange("p (t n) -> p t n", t=NT)
        GN = R_G[:, 0:1024]
        QKT = R_HT[0:DA, 0:2048].rearrange("p (b r s) -> p b r s", b=2, r=2)
        PTS = R_HT[:, 2048:3328]
        TB = R_A[:, :].rearrange("p (b s) -> p b s", b=2)
        T4 = R_T[:, :].rearrange("p (h s) -> p h s", h=9)
        PB = R_S[:, 0:2560].rearrange("p (b s) -> p b s", b=2)
        QS = R_S[:, 2560:3616].rearrange("p (b r t d) -> p b r t d", b=2, r=2, t=NT)
        YT = R_T[:, 0:4096].rearrange("p (k s) -> p k s", k=KD)
        WPA = R_W[:, 0:4096].rearrange("p (k n) -> p k n", k=4)
        WPB = R_W[:, 4096:8192].rearrange("p (k n) -> p k n", k=4)
        MT = HT
        WO = R_Z[:, 0:8192].rearrange("p (k n) -> p k n", k=KD)
        H2T = YT
        WSGU = R_W[:, 0:4096].rearrange("p (k n) -> p k n", k=KD)
        WSD = R_W[:, 4096:6144].rearrange("p (k n) -> p k n", k=2)
        WRT = R_W[:, 6144:6656].rearrange("p (k n) -> p k n", k=KD)
        SILS = R_S[:, 1024:2048].rearrange("p (t n) -> p t n", t=NT)
        ACTS = R_S[:, 2048:3072].rearrange("p (t n) -> p t n", t=NT)
        RX = R_HT[:, 0:1000].bitcast(bf16).rearrange("p (j t c) -> p j t c", j=NBLK, t=NT)
        PM = R_HT[:, 1400:1800].rearrange("p (j t) -> p j t", j=NBLK)

        def tab(at):
            return R_HT[:, at:at + 256].rearrange("p (t e) -> p t e", t=NT)
        SC, BI, MB, RP, SEL, WT, Q1 = (tab(1800 + 256 * n) for n in range(7))
        M8 = R_A[:, 512:768].rearrange("p (g v) -> p g v", g=32)
        GT = R_HT[:, 3336:3592].rearrange("p (t g u) -> p t g u", t=NT, g=NG)
        GE = R_HT[:, 3592:3848].rearrange("p (t g u) -> p t g u", t=NT, g=NG)
        SCT = R_A[0:E, 0:512]
        Q1T, WTT = R_A[0:E, 0:512], R_A[0:E, 512:1024]
        WX = R_Z[:, :].rearrange("p (b n) -> p b n", b=2)
        WGU = [WX[:, b, 0:4096].rearrange("p (k n) -> p k n", k=KD) for b in range(2)]
        WDN = [WX[:, b, 4096:6144].rearrange("p (k n) -> p k n", k=2) for b in range(2)]
        XG = R_G[:, 0:2048].rearrange("p (b n) -> p b n", b=2)
        XT = R_G[:, 2048:4096].rearrange("p (b k s) -> p b k s", b=2, k=KD)
        SIL = R_G[:, 4096:4608].rearrange("p (b n) -> p b n", b=2)
        AR = R_G[:, 4608:5120].rearrange("p (b n) -> p b n", b=2)
        AT = R_G[:, 5120:5632].rearrange("p (b k s) -> p b k s", b=2, k=2)
        OB = R_G[:, 5632:7680].rearrange("p (b n) -> p b n", b=2)
        AH = R_S[:, 0:512].bitcast(bf16).rearrange("p (b t s) -> p b t s", b=2, t=NT)

        cact = sb("cact", [P, KD])
        gcol = sb("gcol", [P, 3, KD])
        mcol = sb("mcol", [P, 2, KD])
        ssx = sb("ssx", [P, 12])
        QKG = sb("QKG", [P, 2, 2, DH])
        RQ = sb("RQ", [P, 2, NT, NH])
        bfg = sb("bfg", [P, HA])
        rbias = sb("rbias", [P, E])
        tabr = R_G[0:HA, 4096:4096 + NTAB]
        extr = R_G[0:HA, 4608:4608 + EXT]
        WF = sb("WF", [P, KD, HA])
        FZ = sb("FZ", [P, 4, NT, HA])
        CUM = sb("CUM", [P, 2, NT, NH])
        mx = sb("mx", [P, 2, 2, NT])
        sm = sb("sm", [P, 2, 2, NT])
        gs = sb("gs", [P, 5, 32])
        ws = sb("ws", [P, 2, NT])
        V8 = sb("V8", [P, NT, TOPK])
        ob = sb("ob", [E, 8])
        OH = sb("OH", [E, 3, NEXT])
        etab = sb("etab_sb", [1, NBLK], i32)
        nover = sb("nover", [1, 1], i32)
        slx = sb("slx", [P, 8, 3])
        slc = sb("slc", [P, NCOL])
        wres = R_S[:, 3072:3328].rearrange("p (t e) -> p t e", t=NT)
        wxr = sb("wxr", [P, NT, NEXT])
        gidx = [sb(f"gidx{b}", [P, 1], i32) for b in range(2)]
        ridx = [sb(f"ridx{b}", [P, 1], i32) for b in range(2)]
        PS = st.enter_context(nc.psum_tensor("PS", [P, 8, 512], f32))

        ident = cst[:, C_ID:C_ID + P]
        ones = cst[:, C_ONE:C_ONE + P]

        s_cst, s_rows, s_gn, s_qkg, s_small, s_tab = map(sem, (
            "cst_loaded", "rows_loaded", "gain_loaded", "qk_gains_loaded", "small_loaded", "table_loaded"))
        s_x = [sem(f"x_loaded{t}") for t in range(NT)]
        s_af = [sem(f"first_ada_loaded{u}") for u in range(8)]
        s_rx = sem("x_reciprocals_ready")
        s_rowst, s_ada1, s_mcol, s_hm, s_hma = map(sem, (
            "rows_turned", "first_ada_done", "mod_columns_ready", "h_ready_dve", "h_ready_act"))
        s_modb, s_wf, s_ext, s_extw, s_t4, s_t4c = map(sem, (
            "mod_bias_loaded", "wf_loaded", "ext_built", "ext_written", "bias_tiles_loaded", "causal_loaded"))
        s_ada = [sem(f"ada_loaded{b}") for b in range(2)]
        s_w = [sem(f"w_in_loaded{b}") for b in range(2)]
        s_cact, s_acc, s_ones, s_madd, s_mod2 = map(sem, (
            "c_act_ready", "ada_sums_ready", "ada_spread", "mod_added", "mod2_ready"))
        s_ssx, s_hrow, s_xpose, s_ht = map(sem, ("x_root_ready", "h_row_ready", "h_transposed", "ht_ready"))
        s_f, s_e, s_lf, s_cum, s_cumr = map(sem, ("f_done", "softplus_part", "log_f_ready", "cum_done", "cum_ready"))
        s_proj, s_zfree, s_ss, s_root, s_norm = map(sem, (
            "proj_done", "proj_evacuated", "qk_squares_ready", "qk_roots_ready", "qk_normed"))
        s_t4m, s_stage, s_tb, s_tq, s_qkev, s_s, s_sred, s_nmx, s_exp = map(sem, (
            "bias_masked", "qk_staged", "bias_staged", "qk_transposed", "qkt_ready", "scores_done",
            "scores_taken", "negmax_ready", "probs_ready"))
        s_pt, s_ptd, s_pta, s_pv, s_y = map(sem, (
            "probs_transposed", "pt_ready_dve", "pt_ready_act", "pv_done", "y_ready"))
        s_yt, s_yted, s_ytea, s_wp, s_u, s_m, s_mt, s_mte, s_wo, s_o, s_x2 = map(sem, (
            "y_transposed", "yt_ready_dve", "yt_ready_act", "w_proj_loaded", "u_done", "m_ready",
            "m_transposed", "mt_ready", "w_out_loaded", "out_done", "x2_ready"))
        s_ss2, s_h2, s_h2t, s_h2te, s_ws, s_rt, s_sct, s_sc = map(sem, (
            "x2_root_ready", "h2_row_ready", "h2_transposed", "h2t_ready", "shared_loaded",
            "router_done", "router_scores_ready", "router_scores_turned"))
        s_hb = [sem(f"h2_written{b}") for b in range(2)]
        s_sgu, s_ssil, s_sact, s_sat, s_sate, s_sdn, s_sx = map(sem, (
            "shared_gu_done", "shared_silu_ready", "shared_act_ready", "shared_at_done",
            "shared_at_ready", "shared_down_done", "shared_added"))
        s_sel, s_pos, s_q1, s_ob, s_oend, s_oh1, s_tr, s_trd, s_xm, s_tabs = map(sem, (
            "selected", "positions_done", "slots_ready", "over_counts_ready", "over_ends_done",
            "over_onehot_ready", "tables_transposed", "tables_ready_t", "ext_tables_done", "tables_ready"))
        s_etab = sem("expert_table_loaded")
        s_rxc = sem("token_columns_ready")
        s_w12 = sem("weight_parts_added")
        s_xgi = sem("gather_buffers_set")
        s_wgu = [sem(f"gate_up_loaded{b}") for b in range(2)]
        s_wd = [sem(f"down_loaded{b}") for b in range(2)]
        s_gat = [sem(f"gathered{b}") for b in range(2)]
        s_scat = [sem(f"scattered{b}") for b in range(2)]
        s_ah, s_ohd, s_sl, s_xt, s_xtd, s_xta, s_gu, s_silu, s_act, s_at, s_ate, s_dn, s_oe, s_ri = map(sem, (
            "onehot_ready", "slots_done", "slot_rows_ready", "x_transposed", "xt_ready_dve",
            "xt_ready_act", "gu_done", "silu_ready", "act_ready", "act_transposed", "at_ready",
            "down_done", "o_ready", "row_index_ready"))
        s_out = sem("residual_written")
        s_idle = sem("idle")
        s_dch, s_ach, s_pch = map(sem, ("dve_chain", "act_chain", "pool_chain"))

        block = st.enter_context(nc.Block())

        def need(eng, s, value):
            if isinstance(value, int) and value <= 0:
                return
            eng.wait_ge(s, value)

        def overflow_blocks(eng, nblk, body):
            with eng.Fori(0, OVER_GROUPS) as g:
                with eng.If(2 * OVER_PAIRS * g + E < nblk):
                    with eng.Fori(0, OVER_PAIRS) as q:
                        for b in range(2):
                            i = OVER_PAIRS * g + q + PAIRS
                            with eng.If(2 * i + b < nblk):
                                body(i, b)

        def always(eng, j):
            return contextlib.nullcontext()

        class Chain:
            def __init__(self, eng, s):
                self.eng, self.s, self.base, self.n = eng, s, 0, 0

            def __call__(self, ins):
                self.n += 1
                ins.then_inc(self.s, 1)
                self.eng.wait_ge(self.s, self.base + self.n)

            def enter(self, i, first, per):
                if not isinstance(i, int):
                    self.saved = self.base + self.n
                    self.base, self.n = self.saved + (i - first) * per, 0
                    self.per = per
                else:
                    self.saved = None

            def leave(self, count):
                if self.saved is not None:
                    assert self.n == self.per, self.n
                    self.base, self.n = self.saved + count * self.per, 0

        w_in, ada_w = a["w_in"], a["ada_w"]
        BY_DVE, BY_PE = (0, 2, 3, 5, 6, 7), (1, 4)
        PE_ORDER = (1, 0, 2, 3, 4, 5, 6, 7)
        ADA_COLS = ([HC * u for u in range(8)]
                    + [3 * D + HC * u for u in range(8)]
                    + [2 * D + HC * u for u in range(4)] + [5 * D + HC * u for u in range(4)])
        W_COLS = []
        for r in range(3):
            W_COLS += [(0 * 3 + r) * SEG, (1 * 3 + r) * SEG]
        W_COLS += [6 * SEG + HA + SEG * n for n in range(4)]

        def settle(eng):
            eng.sem_inc(s_idle, 1)

        def bc(ap, shape):
            return ap.to_broadcast(shape)

        @block.sync
        def _(sp):
            for row, src in ((0, a["c"]), (8, a["mix_norm_g"]), (16, a["ada_b"][0:2 * D])):
                src = src.rearrange("o (k p) -> (o k) p", p=P) if row == 0 else src.rearrange("(k p) -> k p", p=P)
                sp.dma_start(ROWS[row:row + src.shape[0], :], src).then_inc(s_rows, 16)
            sp.dma_start(cst[:, :], a["consts"]).then_inc(s_cst, 16)
            for t in range(NT):
                sp.dma_start(X[:, t, :], a["x"][P * t:P * (t + 1), :]).then_inc(s_x[t], 16)

            def ada_step(u):
                return ada_w[:, ADA_COLS[u]:ADA_COLS[u] + HC].rearrange("(k p) n -> p k n", p=P)

            def load_ada(u):
                sp.wait_ge(s_acc, u - 3)
                sp.dma_start(AD[:, u % 2], ada_step(u)).then_inc(s_ada[u % 2], 16)

            def load_w(c):
                if c >= 2:
                    sp.wait_ge(s_proj, 4 * (c - 1))
                sp.dma_start(WR[:, c % 2], w_in[:, W_COLS[c]:W_COLS[c] + SEG].rearrange(
                    "(k p) n -> p k n", p=P)).then_inc(s_w[c % 2], 16)

            for u in range(8):
                sp.dma_start(AF[u], ada_step(u)).then_inc(s_af[u], 16)
            load_w(0)
            sp.dma_start(WF[:, :, :], w_in[:, 6 * SEG:6 * SEG + HA].rearrange(
                "(k p) n -> p k n", p=P)).then_inc(s_wf, 16)
            load_ada(8)
            load_ada(9)
            load_w(1)
            for n, at in enumerate((3 * D, 4 * D, 2 * D, 5 * D)):
                sp.dma_start(MOD[:, n, :], a["ada_b"][at:at + D].rearrange("(o d) -> o d", o=1)
                             .to_broadcast([P, D])).then_inc(s_modb, 16)
            sp.dma_start(GN, a["ffn_norm_g"].rearrange("(o d) -> o d", o=1).to_broadcast([P, D])).then_inc(s_gn, 16)
            for g in range(4):
                for u in range(8 + 4 * g, 12 + 4 * g):
                    if u >= 10:
                        load_ada(u)
                load_w(2 + g)
            sp.wait_ge(s_acc, 22)
            sp.wait_ge(s_extw, 16)
            sp.dma_start(T4[:, 0:HA, :], bass.AP(ext_dram.tensor, P - 1, [[EXT - 1, P], [P * EXT, HA], [1, S]]))\
                .then_inc(s_t4, 16)
            sp.dma_start(T4[:, HA, :], a["causal"]).then_inc(s_t4c, 16)
            for c in range(6, 10):
                load_w(c)
            sp.wait_ge(s_proj, 36)
            sp.dma_start(WPA, a["w_proj_a"].rearrange("(k p) n -> p k n", p=P)).then_inc(s_wp, 16)
            sp.wait_ge(s_proj, 40)
            sp.dma_start(WPB, a["w_proj_b"].rearrange("(k p) n -> p k n", p=P)).then_inc(s_wp, 16)
            sp.wait_ge(s_yt, 8)
            sp.dma_start(WO, a["w_out"].rearrange("(k p) n -> p k n", p=P)).then_inc(s_wo, 16)
            sp.wait_ge(s_u, 8)
            sp.dma_start(WRT, a["w_router"].rearrange("(k p) n -> p k n", p=P)).then_inc(s_ws, 16)
            sp.dma_start(WSGU[:, :, 0:F], a["w_gate_s"].rearrange("(k p) n -> p k n", p=P)).then_inc(s_ws, 16)
            sp.dma_start(WSGU[:, :, F:2 * F], a["w_up_s"].rearrange("(k p) n -> p k n", p=P)).then_inc(s_ws, 16)
            sp.dma_start(WSD, a["w_down_s"].rearrange("(k p) n -> p k n", p=P)).then_inc(s_ws, 16)
            for t in range(NT):
                sp.wait_ge(s_h2, t + 1)
                sp.dma_start(h2_dram[P * t:P * (t + 1), :], HROW[:, t % 2]).then_inc(s_hb[t % 2], 16)

            def load_gate_up(j, b, e):
                need(sp, s_gu, j - 1)
                sp.dma_start(WGU[b][:, :, 0:F], a["w_gate_e"][bass.ds(e, 1)].rearrange(
                    "o (k p) n -> p (o k) n", p=P)).then_inc(s_wgu[b], 16)
                sp.dma_start(WGU[b][:, :, F:2 * F], a["w_up_e"][bass.ds(e, 1)].rearrange(
                    "o (k p) n -> p (o k) n", p=P)).then_inc(s_wgu[b], 16)

            def load_down(j, b, e):
                need(sp, s_dn, 2 * (j - 1))
                sp.dma_start(WDN[b], a["w_down_e"][bass.ds(e, 1)].rearrange(
                    "o (k p) n -> p (o k) n", p=P)).then_inc(s_wd[b], 16)

            sp.wait_ge(s_o, 8)
            load_gate_up(0, 0, 0)
            load_down(0, 0, 0)
            load_gate_up(1, 1, 1)
            load_down(1, 1, 1)
            load_gate_up(2, 0, 2)
            with sp.Fori(1, PAIRS - 1) as i:
                for b in range(2):
                    load_gate_up(2 * i + b + 1, 1 - b, 2 * i + b + 1)
                    load_down(2 * i + b, b, 2 * i + b)
            load_gate_up(E - 1, 1, E - 1)
            load_down(E - 2, 0, E - 2)
            sp.wait_ge(s_tabs, 1)
            nblk = sp.value_load(nover[0:1, 0:1], min_val=0, max_val=31) + E

            def expert(j):
                return sp.value_load(etab[0:1, bass.ds(j, 1)], min_val=0, max_val=E - 1)
            with sp.If(E < nblk):
                load_gate_up(E, 0, expert(E))
            load_down(E - 1, 1, E - 1)

            def load_overflow(i, b):
                with sp.If(2 * i + b + 1 < nblk):
                    load_gate_up(2 * i + b + 1, 1 - b, expert(2 * i + b + 1))
                load_down(2 * i + b, b, expert(2 * i + b))
            overflow_blocks(sp, nblk, load_overflow)

        @block.gpsimd
        def _(pool):
            pool.memset(CUM[:, :, :, 0:HA], 0.0).then_inc(s_pch, 1)
            pool.memset(extr[:, :], 0.0).then_inc(s_pch, 1)
            pool.wait_ge(s_tab, 16)
            pool.wait_ge(s_pch, 2)
            pool.tensor_copy(extr[:, 383:383 + 2 * REL], tabr[:, NTAB - 1:0:-1]).then_inc(s_ext, 1)
            pool.tensor_copy(extr[:, 0:383], bc(tabr[:, NTAB - 1:NTAB], [HA, 383])).then_inc(s_ext, 1)
            pool.wait_ge(s_ext, 2)
            pool.wait_ge(s_hm, 6)
            pool.dma_start(ext_dram, bc(extr[:, :].unsqueeze(1), [HA, P, EXT])).then_inc(s_extw, 16)
            pool.wait_ge(s_t4, 16)
            pool.memset(T4[0:DH, 0:HA, S - DH:S], NEG).then_inc(s_t4m, 1)
            pool.wait_ge(s_t4m, 1)
            pool.wait_ge(s_t4c, 16)
            pool.wait_ge(s_ones, 16)
            pool.wait_ge(s_norm, 4)
            pool.wait_ge(s_cumr, 2)
            pool.memset(QS[:, :, 0, :, DH + 1:DA], 1.0).then_inc(s_pch, 1)
            pool.memset(QS[:, :, 1, :, DH:DH + 1], 1.0).then_inc(s_pch, 1)
            pool.wait_ge(s_pch, 4)

            def stage(i, b, mixer):
                h = 2 * i + b
                need(pool, s_tq, 2 * h - 2)
                settle(pool)
                pool.tensor_copy(QS[:, b, 0, :, 0:DH], Z[:, 0, :, bass.ds(h * DH, DH)]).then_inc(s_stage, 1)
                pool.tensor_copy(QS[:, b, 1, :, 0:DH], Z[:, 1, :, bass.ds(h * DH, DH)]).then_inc(s_stage, 1)
                pool.tensor_copy(QS[:, b, 0, :, DH:DH + 1], CUM[:, 0, :, bass.ds(h, 1)]).then_inc(s_stage, 1)
                pool.tensor_copy(QS[:, b, 1, :, DH + 1:DA], CUM[:, 1, :, bass.ds(h, 1)]).then_inc(s_stage, 1)
                need(pool, s_sred, 3 * (h - 1))
                settle(pool)
                row = bass.ds(h, 1) if mixer == 0 else bass.ds(HA, 1)
                pool.tensor_copy(TB[:, b, :], T4[:, row, :].rearrange("p o s -> p (o s)")).then_inc(s_tb, 1)

            for b in range(2):
                stage(0, b, 0)
            with pool.Fori(1, HA // 2) as i:
                for b in range(2):
                    stage(i, b, 0)
            with pool.Fori(HA // 2, NH // 2) as i:
                for b in range(2):
                    stage(i, b, 1)

            pool.wait_ge(s_o, 8)
            pool.tensor_copy(RX[:, :, :, 0:2], bc(cst[:, C_TOK2:C_TOK2 + 8].rearrange(
                "p (t c) -> p t c", t=NT).unsqueeze(1), [P, NBLK, NT, 2])).then_inc(s_rxc, 1)
            pool.wait_ge(s_mt, 8)
            pool.wait_ge(s_ss2, 4)
            pool.memset(XG[:, 0, :], 0.0).then_inc(s_xgi, 1)
            pool.memset(XG[:, 1, :], 0.0).then_inc(s_xgi, 1)
            pool.wait_ge(s_xgi, 2)
            pool.wait_ge(s_hb[0], 32)
            pool.wait_ge(s_hb[1], 32)

            def gather(j, b):
                pool.wait_ge(s_sl, SLN * (j + 1))
                need(pool, s_xt, j - 1)
                settle(pool)
                pool.indirect_dma_start(
                    out=XG[:, b, :], out_offset=None, in_=h2_dram,
                    in_offset=bass.IndirectOffsetOnAxis(ap=gidx[b][:, 0:1], axis=0),
                    bounds_check=S - 1, oob_is_err=False).then_inc(s_gat[b], 16)

            def scatter(i, b):
                j = 2 * i + b
                pool.wait_ge(s_oe, 2 * j + 2)
                pool.wait_ge(s_ri, j + 1)
                need(pool, s_scat[1 - b], 16 * (i + b))
                settle(pool)
                pool.indirect_dma_start(
                    out=a["out"], out_offset=bass.IndirectOffsetOnAxis(ap=ridx[b][:, 0:1], axis=0),
                    in_=OB[:, b, :], in_offset=None, compute_op=ALU.add,
                    bounds_check=S - 1, oob_is_err=False).then_inc(s_scat[b], 16)

            for j in range(4):
                gather(j, j % 2)
            nblk = pool.value_load(nover[0:1, 0:1], min_val=0, max_val=31) + E
            pool.wait_ge(s_out, 16 * NT)

            def move_pair(i):
                for b in range(2):
                    scatter(i, b)
                    gather(2 * i + b + 4, b)
            move_pair(0)
            with pool.Fori(1, PAIRS) as i:
                move_pair(i)

            def move_overflow(i, b):
                scatter(i, b)
                gather(2 * i + b + 4, b)
            overflow_blocks(pool, nblk, move_overflow)
            for b in range(2):
                pool.wait_ge(s_scat[b], 16 * ((nblk + (1 - b)) // 2))
            for b in range(2):
                pool.wait_ge(s_gat[b], 16 * ((nblk + (1 - b)) // 2) + 32)

        @block.scalar
        def _(act):
            link = Chain(act, s_ach)
            act.wait_ge(s_rowst, 1)
            act.activation(cact[:, :], PS[:, 5, 0:KD], ACT.Silu).then_inc(s_cact, 1)
            act.activation(gcol[:, :, :], PS[:, 5, KD:4 * KD].rearrange("p (r k) -> p r k", r=3), ACT.Copy)\
                .then_inc(s_cact, 1)
            for t in range(NT):
                act.wait_ge(s_x[t], 16)
                link(act.activation(JUNK, X[:, t, :], ACT.Square, accum_out=ssx[:, t:t + 1]))
            act.activation(ssx[:, 4:8], ssx[:, 0:4], ACT.Sqrt, scale=1.0 / D, bias=cst[:, C_SC:C_SC + 1])\
                .then_inc(s_ssx, 1)
            act.dma_start(tabr[:, :], a["rel_bias"]).then_inc(s_tab, 16)
            for n, g in enumerate(("qn_a", "qn_b", "kn_a", "kn_b")):
                act.dma_start(QKG[:, n // 2, n % 2, :], a[g].rearrange("(o d) -> o d", o=1).to_broadcast([P, DH]))\
                    .then_inc(s_qkg, 16)
            act.dma_start(bfg[:, :], a["b_fgate"].rearrange("(o d) -> o d", o=1).to_broadcast([P, HA]))\
                .then_inc(s_small, 16)
            act.dma_start(rbias[:, :], a["router_bias"].rearrange("(o d) -> o d", o=1).to_broadcast([P, E]))\
                .then_inc(s_small, 16)
            act.dma_start(etab[:, :], a["etab"]).then_inc(s_etab, 16)
            act.wait_ge(s_rx, 1)

            def x_row(t):
                if t >= 2:
                    act.wait_ge(s_xpose, 2 * t - 2)
                act.activation(HROW[:, t % 2], X[:, t, :], ACT.Copy, scale=ssx[:, 8 + t:9 + t]).then_inc(s_hrow, 1)
            x_row(0)
            x_row(1)
            for n in range(8):
                act.wait_ge(s_xpose, n + 1)
                if n in (2, 4):
                    x_row(n // 2 + 1)
                act.activation(HT[:, 4 * (n % 2):4 * (n % 2) + 4, P * (n // 2):P * (n // 2) + P],
                               PS[:, 6 + n % 2, :].rearrange("p (k s) -> p k s", k=4), ACT.Copy).then_inc(s_ht, 1)
            act.sem_inc(s_zfree, 4)
            act.wait_ge(s_mcol, 1)
            act.wait_ge(s_ht, 8)
            for k in range(6, KD):
                act.activation(HT[:, k, :], HT[:, k, :], ACT.Identity, scale=mcol[:, 1, k:k + 1],
                               bias=mcol[:, 0, k:k + 1]).then_inc(s_hma, 1)

            def take_qkv(r, half):
                for t in range(NT):
                    act.wait_ge(s_proj, 8 * r + 4 * half + t + 1)
                    act.activation(Z[:, bass.ds(r, 1), t, SEG * half:SEG * (half + 1)].rearrange("p o n -> p (o n)"),
                                   PS[:, t, :], ACT.Copy).then_inc(s_zfree, 1)
            take_qkv(0, 0)
            act.wait_ge(s_e, 1)
            link(act.activation(FZ[:, 2], FZ[:, 1], ACT.Exp))
            act.activation(FZ[:, 3], FZ[:, 2], ACT.Ln, bias=cst[:, C_SC + 2:C_SC + 3]).then_inc(s_e, 1)
            take_qkv(0, 1)
            with act.Fori(1, 3) as r:
                for half in range(2):
                    take_qkv(r, half)
            act.wait_ge(s_ss, 4)
            act.activation(RQ[:, 0], RQ[:, 0], ACT.Sqrt, bias=cst[:, C_SC + 1:C_SC + 2]).then_inc(s_root, 1)
            act.activation(RQ[:, 1], RQ[:, 1], ACT.Sqrt, scale=1.0 / DH, bias=cst[:, C_SC:C_SC + 1]).then_inc(s_root, 1)
            act.wait_ge(s_mod2, 1)
            act.wait_ge(s_extw, 16)
            with act.Fori(0, 2) as r:
                for half in range(2):
                    for t in range(NT):
                        act.wait_ge(s_proj, 24 + 8 * r + 4 * half + t + 1)
                        act.activation(G[:, bass.ds(r, 1), t, SEG * half:SEG * (half + 1)].rearrange("p o n -> p (o n)"),
                                       PS[:, t, :], ACT.Sigmoid).then_inc(s_zfree, 1)

            def take_qkt(h, b):
                need(act, s_s, 3 * (h - 1))
                for r in range(2):
                    act.wait_ge(s_tq, 2 * h + 1 + r)
                    act.activation(QKT[:, b, r, :], PS[0:DA, 4 + r, :], ACT.Copy).then_inc(s_qkev, 1)

            def exps(h, b):
                act.wait_ge(s_nmx, h + 1)
                need(act, s_y, h - 1)
                for i in range(NT):
                    at = P * (i * (i + 1) // 2)
                    act.activation(PB[:, b, at:at + P * (i + 1)], PB[:, b, at:at + P * (i + 1)], ACT.Exp,
                                   bias=mx[:, b, 1, i:i + 1], accum_out=sm[:, b, 0, i:i + 1]).then_inc(s_exp, 1)

            def take_pt3(h):
                act.wait_ge(s_pt, 4 * h + 4)
                act.activation(PTS[:, 768:1280], PS[:, 7, :], ACT.Copy).then_inc(s_pta, 1)

            take_qkt(0, 0)
            take_qkt(1, 1)
            exps(0, 0)
            take_qkt(2, 0)
            exps(1, 1)
            take_pt3(0)

            def heads(i):
                for b in range(2):
                    h = 2 * i + 1 + b
                    take_qkt(h + 2, 1 - b)
                    exps(h + 1, b)
                    take_pt3(h)
            heads(0)
            with act.Fori(1, 6) as i:
                heads(i)
            take_qkt(15, 1)
            exps(14, 0)
            take_pt3(13)
            exps(15, 1)
            take_pt3(14)
            take_pt3(15)

            for t in range(NT):
                act.wait_ge(s_yt, NT + t + 1)
                act.activation(YT[:, 4:8, P * t:P * t + P],
                               PS[:, (5, 7, 4, 6)[t], :].rearrange("p (k s) -> p k s", k=4), ACT.Copy).then_inc(s_ytea, 1)
            for n in range(8):
                t = n // 2
                act.wait_ge(s_mt, n + 1)
                act.activation(MT[:, 4 * (n % 2):4 * (n % 2) + 4, P * t:P * t + P],
                               PS[:, 4 + n % 4, :].rearrange("p (k s) -> p k s", k=4), ACT.Copy).then_inc(s_mte, 1)

            def take_h2t(t):
                for n in range(2 * t, 2 * t + 2):
                    act.wait_ge(s_h2t, n + 1)
                    act.activation(H2T[:, 4 * (n % 2):4 * (n % 2) + 4, P * t:P * t + P],
                                   PS[:, 4 + n % 4, :].rearrange("p (k s) -> p k s", k=4), ACT.Copy).then_inc(s_h2te, 1)
            for t in range(NT):
                act.wait_ge(s_x2, 2 * t + 2)
                link(act.activation(G[:, 0, t, :], X[:, t, :], ACT.Square, accum_out=ssx[:, t:t + 1]))
                act.activation(ssx[:, 4 + t:5 + t], ssx[:, t:t + 1], ACT.Sqrt, scale=1.0 / D,
                               bias=cst[:, C_SC:C_SC + 1]).then_inc(s_ss2, 1)
                if t:
                    take_h2t(t - 1)
            take_h2t(NT - 1)
            act.wait_ge(s_rt, 1)
            act.activation(SCT, PS[0:E, 4, :], ACT.Sigmoid).then_inc(s_sct, 1)
            for b in range(2):
                act.wait_ge(s_hb[b], 32)
            for t in range(NT):
                act.wait_ge(s_sgu, t + 1)
                act.activation(SILS[:, t, :], PS[:, t, 0:F], ACT.Silu).then_inc(s_ssil, 1)

            def shared_at(t):
                act.wait_ge(s_sat, t + 1)
                need(act, s_sdn, 2 * (t - 1))
                act.activation(AT[:, t % 2], PS[:, 6, 0:F].rearrange("p (k s) -> p k s", k=2), ACT.Copy)\
                    .then_inc(s_sate, 1)

            def take_xt(j, b):
                act.wait_ge(s_xt, j + 1)
                need(act, s_gu, j - 1)
                act.activation(XT[:, b, 4:8, :], PS[:, 5, :].rearrange("p (k s) -> p k s", k=4), ACT.Copy)\
                    .then_inc(s_xta, 1)

            def silu(j, b):
                act.wait_ge(s_gu, j + 1)
                need(act, s_act, j - 1)
                act.activation(SIL[:, b, :], PS[:, b, 0:F], ACT.Silu).then_inc(s_silu, 1)

            def take_at(j, b):
                act.wait_ge(s_at, j + 1)
                need(act, s_dn, 2 * (j - 1))
                act.activation(AT[:, b], PS[:, 6, 0:F].rearrange("p (k s) -> p k s", k=2), ACT.Copy)\
                    .then_inc(s_ate, 1)

            for t in range(3):
                shared_at(t)
            take_xt(0, 0)
            take_xt(1, 1)
            silu(0, 0)
            shared_at(3)
            for t in range(NT):
                act.wait_ge(s_sx, max(4, 2 * t + 2))
                act.dma_start(a["out"][P * t:P * (t + 1), :], X[:, t, :]).then_inc(s_out, 16)
            act.wait_ge(s_tabs, 1)
            nblk = act.value_load(nover[0:1, 0:1], min_val=0, max_val=31) + E

            def step(i, b, more):
                j = 2 * i + b
                take_at(j, b)
                with more(act, j + 1):
                    silu(j + 1, 1 - b)
                take_xt(j + 2, b)

            def pair(i):
                for b in range(2):
                    step(i, b, always)
            pair(0)
            with act.Fori(1, PAIRS - 1) as i:
                pair(i)

            def if_block(eng, j):
                return eng.If(j < nblk)
            step(PAIRS - 1, 0, always)
            step(PAIRS - 1, 1, if_block)
            overflow_blocks(act, nblk, lambda i, b: step(i, b, if_block))

        @block.vector
        def _(dve):
            link = Chain(dve, s_dch)

            def ada_sum(u):
                src = AF[u] if u < 8 else AD[:, u % 2]
                acc = ACC[:, (BY_DVE.index(u) if u < 8 else u) % 4]
                if u < 8:
                    dve.wait_ge(s_af[u], 16)
                    if BY_DVE.index(u) >= 4:
                        dve.wait_ge(s_ada1, PE_ORDER.index(BY_DVE[BY_DVE.index(u) - 4]) + 1)
                else:
                    dve.wait_ge(s_ada[u % 2], 16 * (u // 2 - 3))
                    need(dve, s_ones, u - 11)
                link(dve.tensor_scalar(acc, src[:, 0], cact[:, 0:1], None, ALU.mult))
                for k in range(1, KD):
                    ins = dve.scalar_tensor_tensor(acc, src[:, k], cact[:, k:k + 1], acc, ALU.mult, ALU.add)
                    if k < KD - 1:
                        link(ins)
                ins.then_inc(s_acc, 1)

            def mod_add(u, at):
                dve.tensor_tensor(MOD[:, at // D, at % D:at % D + HC], MOD[:, at // D, at % D:at % D + HC],
                                  PS[:, 4 + (u % 4) // 2, HC * (u % 2):HC * (u % 2) + HC], ALU.add).then_inc(s_madd, 1)

            dve.wait_ge(s_ssx, 1)
            dve.reciprocal(ssx[:, 8:12], ssx[:, 4:8]).then_inc(s_rx, 1)
            dve.wait_ge(s_cact, 2)
            for u in BY_DVE:
                ada_sum(u)
            dve.wait_ge(s_ada1, 8)
            link(dve.tensor_tensor(mcol[:, :, :], PS[:, 4, 0:2 * KD].rearrange("p (r k) -> p r k", r=2),
                                   gcol[:, 1:3, :], ALU.add))
            dve.scalar_tensor_tensor(mcol[:, 1, :], mcol[:, 1, :], 1.0, gcol[:, 0, :], ALU.add, ALU.mult)\
                .then_inc(s_mcol, 1)
            dve.wait_ge(s_mcol, 1)
            dve.wait_ge(s_ht, 8)
            for k in range(6):
                dve.tensor_scalar(HT[:, k, :], HT[:, k, :], mcol[:, 1, k:k + 1], mcol[:, 0, k:k + 1],
                                  ALU.mult, ALU.add).then_inc(s_hm, 1)

            def log_forget():
                dve.wait_ge(s_f, 1)
                dve.wait_ge(s_small, 32)
                link(dve.tensor_tensor(FZ[:, 0], PS[:, 6, 0:32].rearrange("p (t h) -> p t h", t=NT),
                                       bc(bfg[:, :].unsqueeze(1), [P, NT, HA]), ALU.add))
                link(dve.tensor_scalar(FZ[:, 1], FZ[:, 0], -1.0, None, ALU.mult))
                dve.tensor_tensor(FZ[:, 1], FZ[:, 0], FZ[:, 1], ALU.min).then_inc(s_e, 1)
                dve.wait_ge(s_e, 2)
                link(dve.tensor_scalar(FZ[:, 0], FZ[:, 0], 0.0, None, ALU.min))
                dve.tensor_tensor(FZ[:, 0], FZ[:, 0], FZ[:, 3], ALU.subtract).then_inc(s_lf, 1)

            for g in range(4):
                for u in range(8 + 4 * g, 12 + 4 * g):
                    ada_sum(u)
                if g == 0:
                    log_forget()
                else:
                    if g == 1:
                        dve.wait_ge(s_modb, 64)
                    dve.wait_ge(s_ones, 4 * g)
                    for u in range(4 + 4 * g, 8 + 4 * g):
                        mod_add(u, HC * (u - 8))
            dve.wait_ge(s_ones, 16)
            for u in range(20, 24):
                mod_add(u, HC * (u - 8))
            dve.wait_ge(s_madd, 16)
            dve.wait_ge(s_gn, 16)
            dve.scalar_tensor_tensor(MOD[:, 1, :], MOD[:, 1, :], 1.0, GN, ALU.add, ALU.mult).then_inc(s_mod2, 1)
            dve.wait_ge(s_cum, 1)
            cps = PS[:, 7, 0:32].rearrange("p (t h) -> p t h", t=NT)
            dve.tensor_copy(CUM[:, 0, :, HA:NH], cps).then_inc(s_cumr, 1)
            dve.tensor_scalar(CUM[:, 1, :, HA:NH], cps, -1.0, None, ALU.mult).then_inc(s_cumr, 1)
            dve.wait_ge(s_qkg, 64)

            def qk(r, half):
                return Z[:, r, :, SEG * half:SEG * (half + 1)].rearrange("p t (h d) -> p t h d", h=HA)
            for r in range(2):
                for half in range(2):
                    dve.wait_ge(s_zfree, 4 + 8 * r + 4 * half + 4)
                    link(dve.tensor_tensor(SQT, Z[:, r, :, SEG * half:SEG * (half + 1)],
                                           Z[:, r, :, SEG * half:SEG * (half + 1)], ALU.mult))
                    link(dve.tensor_reduce(RQ[:, r, :, HA * half:HA * (half + 1)],
                                           SQT.rearrange("p t (h d) -> p t h d", h=HA), AX.X, ALU.add))
                    dve.sem_inc(s_ss, 1)
            dve.wait_ge(s_root, 2)
            link(dve.reciprocal(RQ[:, :, :, :].rearrange("p r t h -> p (r t h)"),
                                RQ[:, :, :, :].rearrange("p r t h -> p (r t h)")))
            for r in range(2):
                for half in range(2):
                    link(dve.tensor_tensor(qk(r, half), qk(r, half), bc(
                        RQ[:, r, :, HA * half:HA * (half + 1)].unsqueeze(3), [P, NT, HA, DH]), ALU.mult))
                    dve.tensor_tensor(qk(r, half), qk(r, half), bc(
                        QKG[:, r, half, :].unsqueeze(1).unsqueeze(1), [P, NT, HA, DH]), ALU.mult).then_inc(s_norm, 1)

            def take_scores(h, b):
                dve.wait_ge(s_tb, h + 1)
                need(dve, s_pt, 4 * (h - 1))
                for g, tiles in enumerate(((0, 2), (1,), (3,))):
                    dve.wait_ge(s_s, 3 * h + g + 1)
                    settle(dve)
                    for n, i in enumerate(tiles):
                        w, at = P * (i + 1), P * (i * (i + 1) // 2)
                        src = P if i == 2 else 0
                        ins = dve.tensor_tensor_reduce(
                            out=PB[:, b, at:at + w], in0=PS[:, g, src:src + w], in1=TB[:, b, S - w:S],
                            scale=1.0, scalar=-3e38, op0=ALU.add, op1=ALU.max, accum_out=mx[:, b, 0, i:i + 1])
                    ins.then_inc(s_sred, 1)
                dve.wait_ge(s_sred, 3 * h + 3)
                dve.tensor_scalar(mx[:, b, 1, :], mx[:, b, 0, :], -1.0, None, ALU.mult).then_inc(s_nmx, 1)

            def take_pt(h, i):
                dve.wait_ge(s_pt, 4 * h + i + 1)
                at = P * (i * (i + 1) // 2)
                dve.tensor_copy(PTS[:, at:at + P * (i + 1)], PS[:, 6 + i % 2, 0:P * (i + 1)]).then_inc(s_ptd, 1)

            def take_y(h, b):
                dve.wait_ge(s_exp, 4 * h + 4)
                link(dve.reciprocal(sm[:, b, 1, :], sm[:, b, 0, :]))
                dve.wait_ge(s_pv, 4 * h + 4)
                dve.tensor_tensor(Z[:, 0, :, bass.ds(h * DH, DH)],
                                  PS[:, 3, 0:256].rearrange("p (t d) -> p t d", t=NT),
                                  bc(sm[:, b, 1, :].unsqueeze(2), [P, NT, DH]), ALU.mult).then_inc(s_y, 1)

            take_scores(0, 0)
            take_scores(1, 1)
            for n in range(3):
                take_pt(0, n)

            def heads(i, first):
                link.enter(i, first, 2)
                for b in range(2):
                    h = 2 * i + 1 + b
                    take_scores(h + 1, b)
                    for n in range(3):
                        take_pt(h, n)
                    take_y(h - 1, b)
            heads(0, 0)
            with dve.Fori(1, 7) as i:
                heads(i, 1)
            link.leave(6)
            dve.wait_ge(s_tb, NH)
            for t in range(NT):
                dve.wait_ge(s_yt, t + 1)
                dve.tensor_copy(YT[:, 0:4, P * t:P * t + P],
                                PS[:, 4 + t % 2, :].rearrange("p (k s) -> p k s", k=4)).then_inc(s_yted, 1)
            for n in range(3):
                take_pt(15, n)
            take_y(14, 0)
            take_y(15, 1)

            for n in range(8):
                t, cols = n // 2, slice(512 * (n % 2), 512 * (n % 2) + 512)
                dve.wait_ge(s_u, n + 1)
                for r in range(2):
                    link(dve.tensor_tensor(G[:, r, t, cols], G[:, r, t, cols], PS[:, 2 * (n % 2) + r, :], ALU.mult))
                dve.tensor_tensor(G[:, 0, t, cols], G[:, 0, t, cols], G[:, 1, t, cols], ALU.add).then_inc(s_m, 1)

            def h2_rows(t):
                dve.wait_ge(s_ss2, t + 1)
                link(dve.reciprocal(ssx[:, 8 + t:9 + t], ssx[:, 4 + t:5 + t]))
                if t >= 2:
                    dve.wait_ge(s_h2t, 2 * t - 2)
                    dve.wait_ge(s_hb[t % 2], 16)
                link(dve.scalar_tensor_tensor(HROW[:, t % 2], X[:, t, :], ssx[:, 8 + t:9 + t], MOD[:, 1, :],
                                              ALU.mult, ALU.mult))
                dve.tensor_tensor(HROW[:, t % 2], HROW[:, t % 2], MOD[:, 0, :], ALU.add).then_inc(s_h2, 1)

            for n in range(8):
                t, cols = n // 2, slice(512 * (n % 2), 512 * (n % 2) + 512)
                dve.wait_ge(s_o, n + 1)
                link(dve.tensor_tensor(G[:, 1, t, cols], PS[:, n % 4, :], MOD[:, 2, cols], ALU.mult))
                dve.tensor_tensor(X[:, t, cols], X[:, t, cols], G[:, 1, t, cols], ALU.add).then_inc(s_x2, 1)
                if n % 2 and t:
                    h2_rows(t - 1)
            h2_rows(NT - 1)

            dve.wait_ge(s_sc, 1)
            gsum, cnt, gm, ng = (gs[:, n, :].rearrange("p (t g) -> p t g", t=NT) for n in range(4))
            link(dve.tensor_copy(SC, PS[:, 5, 0:256].rearrange("p (t e) -> p t e", t=NT)))
            link(dve.tensor_tensor(BI, SC, bc(rbias[:, :].unsqueeze(1), [P, NT, E]), ALU.add))
            for t in range(NT):
                for g in range(NG):
                    ins = dve.max(M8[:, NG * t + g, :], BI[:, t, 8 * g:8 * g + 8])
            link(ins)
            link(dve.tensor_tensor(gs[:, 0, :].unsqueeze(2), M8[:, :, 0:1], M8[:, :, 1:2], ALU.add))
            mine = bc(gsum.unsqueeze(3), [P, NT, NG, NG])
            other = bc(gsum.unsqueeze(2), [P, NT, NG, NG])
            low = bc(cst[:, C_LOW:C_LOW + 64].rearrange("p (g u) -> p g u", g=NG).unsqueeze(1), [P, NT, NG, NG])
            link(dve.tensor_tensor(GE, other, mine, ALU.is_equal))
            link(dve.tensor_tensor(GE, GE, low, ALU.mult))
            link(dve.tensor_tensor(GT, other, mine, ALU.is_gt))
            link(dve.tensor_tensor(GT, GT, GE, ALU.add))
            link(dve.tensor_reduce(cnt, GT, AX.X, ALU.add))
            link(dve.tensor_scalar(gm, cnt, float(TOPG) - 0.5, None, ALU.is_lt))
            link(dve.tensor_scalar(ng, gm, -NEG, NEG, ALU.mult, ALU.add))
            for t in range(NT):
                v = MB[:, t, :].rearrange("p (g u) -> p g u", g=NG)
                link(dve.tensor_tensor(v, BI[:, t, :].rearrange("p (g u) -> p g u", g=NG),
                                       bc(gm[:, t, :].unsqueeze(2), [P, NG, 8]), ALU.mult))
                link(dve.tensor_tensor(v, v, bc(ng[:, t, :].unsqueeze(2), [P, NG, 8]), ALU.add))
                link(dve.max(V8[:, t, :], MB[:, t, :]))
                link(dve.match_replace(RP[:, t, :], V8[:, t, :], MB[:, t, :], -3e38))
            dve.tensor_scalar(SEL, RP, -2e38, None, ALU.is_lt).then_inc(s_sel, 1)
            dve.wait_ge(s_sel, 1)
            link(dve.tensor_tensor(WT, SC, SEL, ALU.mult))
            link(dve.tensor_reduce(ws[:, 0, :], WT, AX.X, ALU.add))
            link(dve.reciprocal(ws[:, 1, :], ws[:, 0, :]))
            link(dve.tensor_tensor(WT, WT, bc(ws[:, 1, :].unsqueeze(2), [P, NT, E]), ALU.mult))
            link(dve.tensor_scalar(WT, WT, ROUTED_SCALE, None, ALU.mult))
            dve.wait_ge(s_pos, 1)
            link(dve.tensor_scalar(ob[:, 0:1], PS[0:E, 4, 256:257], float(P) + 0.5, None, ALU.is_gt))
            link(dve.tensor_scalar(ob[:, 1:2], PS[0:E, 4, 256:257], 2.0 * P + 0.5, None, ALU.is_gt))
            link(dve.tensor_scalar(ob[:, 2:3], PS[0:E, 4, 256:257], 3.0 * P + 0.5, None, ALU.is_gt))
            link(dve.tensor_tensor(ob[:, 3:4], ob[:, 0:1], ob[:, 1:2], ALU.add))
            dve.tensor_tensor(ob[:, 3:4], ob[:, 3:4], ob[:, 2:3], ALU.add).then_inc(s_ob, 1)
            link(dve.scalar_tensor_tensor(Q1, PS[:, 4, 0:256].rearrange("p (t e) -> p t e", t=NT), 1.0, SEL,
                                          ALU.add, ALU.mult))
            dve.sem_inc(s_q1, 1)
            dve.wait_ge(s_oend, 1)
            m36 = cst[0:E, C_M:C_M + NEXT]
            link(dve.tensor_copy(ob[:, 4:5], PS[0:E, 7, 0:1]))
            link(dve.tensor_tensor(ob[:, 5:6], ob[:, 4:5], ob[:, 3:4], ALU.subtract))
            link(dve.tensor_scalar(OH[:, 0, :], m36, ob[:, 5:6], None, ALU.is_ge))
            link(dve.scalar_tensor_tensor(OH[:, 0, :], m36, ob[:, 4:5], OH[:, 0, :], ALU.is_lt, ALU.mult))
            link(dve.tensor_scalar(OH[:, 1, :], m36, ob[:, 5:6], 1.0, ALU.subtract, ALU.add))
            dve.scalar_tensor_tensor(OH[:, 1, :], OH[:, 1, :], float(P), OH[:, 0, :], ALU.mult, ALU.mult)\
                .then_inc(s_oh1, 1)
            for n, (dst, bank) in enumerate(((Q1T, 5), (WTT, 6))):
                dve.wait_ge(s_tr, n + 1)
                dve.tensor_copy(dst, PS[0:E, bank, :]).then_inc(s_trd, 1)
            perm = "p t e -> p e t"
            link(dve.tensor_copy(PM[:, 0:E, :], Q1.rearrange(perm)))

            def split(lo, hi, w, left):
                link(dve.tensor_copy(RX[:, lo:hi, :, W_1], w))
                link(dve.tensor_tensor(left, w, RX[:, lo:hi, :, W_1], ALU.subtract))
                link(dve.tensor_copy(RX[:, lo:hi, :, W_2], left))
                link(dve.tensor_tensor(left, left, RX[:, lo:hi, :, W_2], ALU.subtract))
                link(dve.tensor_copy(RX[:, lo:hi, :, W_3], left))
            split(0, E, WT.rearrange(perm), wres.rearrange(perm))

            def shared_act(t):
                dve.wait_ge(s_ssil, t + 1)
                dve.tensor_tensor(ACTS[:, t, :], SILS[:, t, :], PS[:, t, F:2 * F], ALU.mult).then_inc(s_sact, 1)
            shared_act(0)
            shared_act(1)
            shared_act(2)
            shared_act(3)
            dve.wait_ge(s_xm, 1)
            for col, dst in enumerate((PM[:, E:NBLK, :], wxr[:, :, :].rearrange("p t m -> p m t"))):
                link(dve.tensor_copy(dst, PS[:, 4, 144 * col:144 * (col + 1)].rearrange("p (t m) -> p m t", t=NT)))
            split(E, NBLK, wxr[:, :, :].rearrange("p t m -> p m t"), wxr[:, :, :].rearrange("p t m -> p m t"))
            dve.wait_ge(s_rxc, 1)
            dve.wait_ge(s_etab, 16)
            link(dve.tensor_copy(nover[:, :], PS[0:1, 4, 468:469]))
            dve.tensor_copy(etab[:, E:NBLK], PS[0:1, 4, 432:468]).then_inc(s_tabs, 1)

            def shared_add(t):
                for n in range(2 * t, 2 * t + 2):
                    cols = slice(512 * (n % 2), 512 * (n % 2) + 512)
                    dve.wait_ge(s_sdn, n + 1)
                    link(dve.tensor_tensor(G[:, 1, 3, cols], PS[:, (0 if t == 1 else 2) + n % 2, :], MOD[:, 3, cols], ALU.mult))
                    link(dve.tensor_tensor(X[:, t, cols], X[:, t, cols], G[:, 1, 3, cols], ALU.add))
                    dve.sem_inc(s_sx, 1)

            def onehot(j, b):
                need(dve, s_ohd, j - 1)
                dve.tensor_tensor(AH[:, b], bc(cst[:, C_SLOT:C_SLOT + P].unsqueeze(1), [P, NT, P]),
                                  bc(PM[:, bass.ds(j, 1), :].rearrange("p o t -> p (o t)").unsqueeze(2), [P, NT, P]),
                                  ALU.is_equal).then_inc(s_ah, 1)

            def slots(j, b):
                def col(c):
                    return slx[:, bass.ds(j % 8, 1), c:c + 1].rearrange("p o c -> p (o c)")
                dve.wait_ge(s_ohd, j + 1)
                need(dve, s_xt, j - 1)
                dve.tensor_copy(slc[:, :], PS[:, 7, 0:NCOL]).then_inc(s_sl, 1)
                dve.wait_ge(s_sl, SLN * j + 1)
                dve.scalar_tensor_tensor(col(1), slc[:, T_HI:T_HI + 1], NOTOK, slc[:, T_LO:T_LO + 1],
                                         ALU.add, ALU.add).then_inc(s_sl, 1)
                dve.tensor_tensor(col(0), slc[:, W_1:W_1 + 1], slc[:, W_2:W_2 + 1], ALU.add).then_inc(s_w12, 1)
                dve.wait_ge(s_w12, j + 1)
                dve.tensor_tensor(col(2), col(0), slc[:, W_3:W_3 + 1], ALU.add).then_inc(s_sl, 1)
                dve.scalar_tensor_tensor(gidx[b][:, :], slc[:, T_HI:T_HI + 1], NOTOK, slc[:, T_LO:T_LO + 1],
                                         ALU.add, ALU.add).then_inc(s_sl, 1)

            def take_xt(j, b):
                dve.wait_ge(s_xt, j + 1)
                need(dve, s_gu, j - 1)
                dve.tensor_copy(XT[:, b, 0:4, :], PS[:, 4, :].rearrange("p (k s) -> p k s", k=4)).then_inc(s_xtd, 1)

            def mul(j, b):
                dve.wait_ge(s_silu, j + 1)
                need(dve, s_at, j - 1)
                dve.tensor_tensor(AR[:, b, :], SIL[:, b, :], PS[:, b, F:2 * F], ALU.mult).then_inc(s_act, 1)

            def take_o(i, j, b):
                need(dve, s_scat[b], 16 * i)
                dve.wait_ge(s_sl, SLN * (j + 1))
                dve.tensor_copy(ridx[b][:, :], slx[:, bass.ds(j % 8, 1), 1:2].rearrange("p o c -> p (o c)"))\
                    .then_inc(s_ri, 1)
                for half in range(2):
                    dve.wait_ge(s_dn, 2 * j + 1 + half)
                    dve.scalar_tensor_tensor(OB[:, b, 512 * half:512 * half + 512], PS[:, 2 + half, :],
                                             slx[:, bass.ds(j % 8, 1), 2:3].rearrange("p o c -> p (o c)"),
                                             MOD[:, 3, 512 * half:512 * half + 512], ALU.mult, ALU.mult)\
                        .then_inc(s_oe, 1)

            dve.wait_ge(s_tabs, 1)
            for b in range(2):
                dve.wait_ge(s_hb[b], 32)
            nblk = dve.value_load(nover[0:1, 0:1], min_val=0, max_val=31) + E
            onehot(0, 0)
            onehot(1, 1)
            slots(0, 0)
            slots(1, 1)
            shared_add(1)
            take_xt(0, 0)
            take_xt(1, 1)
            shared_add(0)
            onehot(2, 0)
            onehot(3, 1)
            mul(0, 0)
            slots(2, 0)
            shared_add(2)
            slots(3, 1)
            shared_add(3)

            def step(i, b, more):
                j = 2 * i + b
                onehot(j + 4, b)
                with more(dve, j + 1):
                    mul(j + 1, 1 - b)
                take_xt(j + 2, b)
                slots(j + 4, b)
                take_o(i, j, b)

            def pair(i):
                for b in range(2):
                    step(i, b, always)
            pair(0)
            with dve.Fori(1, PAIRS - 1) as i:
                pair(i)

            def if_block(eng, j):
                return eng.If(j < nblk)
            step(PAIRS - 1, 0, always)
            step(PAIRS - 1, 1, if_block)
            overflow_blocks(dve, nblk, lambda i, b: step(i, b, if_block))

        @block.tensor
        def _(pe):
            mm = pe.matmul

            def spread(us):
                for u in us:
                    ins = mm(PS[:, 4 + (u % 4) // 2, HC * (u % 2):HC * (u % 2) + HC], ones, ACC[:, u % 4],
                             start=True, stop=True)
                ins.then_inc(s_ones, len(us))

            pe.wait_ge(s_cst, 16)
            pe.wait_ge(s_rows, 48)
            pe.transpose(PS[:, 5, 0:32], ROWS, ident[0:32, 0:32]).then_inc(s_rowst, 1)

            def turn(dst_bank, src, ready):
                for k in range(4):
                    ins = pe.transpose(PS[:, dst_bank, P * k:P * k + P], src[:, P * k:P * k + P], ident)
                ins.then_inc(ready, 1)

            def turn_row(t):
                pe.wait_ge(s_hrow, t + 1)
                for half in range(2):
                    need(pe, s_ht, 2 * t - 1 + half)
                    turn(6 + half, HROW[:, t % 2, 512 * half:512 * half + 512], s_xpose)

            def ada_by_feature(u):
                if u in BY_PE:
                    pe.wait_ge(s_cact, 1)
                    pe.wait_ge(s_af[u], 16)
                else:
                    pe.wait_ge(s_acc, BY_DVE.index(u) + 1)
                for half in range(2):
                    out, cols = PS[:, 4, 2 * u + half:2 * u + half + 1], slice(P * half, P * half + P)
                    if u in BY_PE:
                        for k in range(KD):
                            ins = mm(out, AF[u][:, k, cols], cact[:, k:k + 1], start=k == 0, stop=k == KD - 1)
                    else:
                        ins = mm(out, ACC[:, BY_DVE.index(u) % 4, cols], ones[:, 0:1], start=True, stop=True)
                ins.then_inc(s_ada1, 1)

            turn_row(0)
            turn_row(1)
            ada_by_feature(PE_ORDER[0])
            turn_row(2)
            turn_row(3)
            for u in PE_ORDER[1:]:
                ada_by_feature(u)

            def forget():
                pe.wait_ge(s_wf, 16)
                for t in range(NT):
                    for k in range(KD):
                        ins = mm(PS[:, 6, HA * t:HA * t + HA], HT[:, k, P * t:P * t + P], WF[:, k, :],
                                 start=k == 0, stop=k == KD - 1)
                ins.then_inc(s_f, 1)

            def project(i, b):
                pe.wait_ge(s_w[b], 16 * (i + 1))
                for t in range(NT):
                    pe.wait_ge(s_zfree, 8 * i + 4 * b + t + 1)
                    for k in range(KD):
                        if isinstance(i, int) and i + b + t == 0:
                            pe.wait_ge(s_hm if k < 6 else s_hma, k + 1 if k < 6 else k - 5)
                        ins = mm(PS[:, t, :], HT[:, k, P * t:P * t + P], WR[:, b, k, :],
                                 start=k == 0, stop=k == KD - 1)
                    ins.then_inc(s_proj, 1)

            for i in range(2):
                for b in range(2):
                    project(i, b)
                    if i == 0 and b == 0:
                        forget()
                    pe.wait_ge(s_acc, 10 + 4 * (2 * i + b))
                    need(pe, s_madd, 4 * (2 * i + b))
                    spread(range(8 + 4 * (2 * i + b), 12 + 4 * (2 * i + b)))
            pe.wait_ge(s_lf, 1)
            for t in range(NT):
                for j in range(t + 1):
                    ins = mm(PS[:, 7, HA * t:HA * t + HA], cst[:, C_TIN:C_TIN + P] if j == t else ones,
                             FZ[:, 0, j, :], start=j == 0, stop=j == t)
            ins.then_inc(s_cum, 1)
            with pe.Fori(2, 5) as i:
                for b in range(2):
                    project(i, b)

            def turn_qk(h, b):
                pe.wait_ge(s_stage, 4 * h + 4)
                for r in range(2):
                    need(pe, s_qkev, 2 * h - 1 + r)
                    for t in range(NT):
                        ins = pe.transpose(PS[0:DA, 4 + r, P * t:P * t + P], QS[:, b, r, t, :], ident)
                    ins.then_inc(s_tq, 1)

            def scores(h, b):
                pe.wait_ge(s_qkev, 2 * h + 2)
                for g, tiles in enumerate(((0, 2), (1,), (3,))):
                    need(pe, s_sred, 3 * h - 2 + g)
                    for i in tiles:
                        at = P if i == 2 else 0
                        ins = mm(PS[:, g, at:at + P * (i + 1)], QKT[:, b, 0, P * i:P * i + P],
                                 QKT[:, b, 1, 0:P * (i + 1)], start=True, stop=True)
                    ins.then_inc(s_s, 1)

            def turn_p(h, b, i):
                at = P * (i * (i + 1) // 2)
                pe.wait_ge(s_exp, 4 * h + i + 1)
                if i == 1:
                    need(pe, s_pta, h)
                else:
                    need(pe, s_ptd, 3 * h + (0, 0, 1, 2)[i])
                for j in range(i + 1):
                    ins = pe.transpose(PS[:, 6 + i % 2, P * j:P * j + P], PB[:, b, at + P * j:at + P * j + P], ident)
                ins.then_inc(s_pt, 1)

            def pv(h, i):
                at = P * (i * (i + 1) // 2)
                if i == 3:
                    pe.wait_ge(s_pta, h + 1)
                else:
                    pe.wait_ge(s_ptd, 3 * h + i + 1)
                if i == 0:
                    need(pe, s_y, h)
                for j in range(i + 1):
                    ins = mm(PS[:, 3, DH * i:DH * i + DH], PTS[:, at + P * j:at + P * j + P],
                             Z[:, 2, j, bass.ds(h * DH, DH)], start=j == 0, stop=j == i)
                ins.then_inc(s_pv, 1)

            pe.wait_ge(s_cumr, 2)
            pe.wait_ge(s_madd, 16)
            turn_qk(0, 0)
            pe.wait_ge(s_zfree, 44)
            turn_qk(1, 1)
            scores(0, 0)
            scores(1, 1)
            turn_qk(2, 0)
            for n in range(4):
                turn_p(0, 0, n)

            def heads(i):
                for b in range(2):
                    h = 2 * i + 1 + b
                    scores(h + 1, b)
                    turn_qk(h + 2, 1 - b)
                    for n in range(4):
                        pv(h - 1, n)
                        turn_p(h, 1 - b, n)
            heads(0)
            with pe.Fori(1, 6) as i:
                heads(i)
            scores(14, 0)
            turn_qk(15, 1)
            for n in range(4):
                pv(12, n)
                turn_p(13, 1, n)
            scores(15, 1)
            for n in range(4):
                pv(13, n)
                turn_p(14, 0, n)
            pe.wait_ge(s_y, HA)
            pe.wait_ge(s_qkev, 32)
            for t in range(NT):
                need(pe, s_yted, t - 1)
                turn(4 + t % 2, Z[:, 0, t, 0:512], s_yt)
            for n in range(4):
                pv(14, n)
                turn_p(15, 1, n)
            for n in range(4):
                pv(15, n)

            pe.wait_ge(s_y, 16)
            pe.wait_ge(s_ptd, 48)
            pe.wait_ge(s_pta, 16)
            pe.wait_ge(s_yted, 4)
            for t in range(NT):
                turn((5, 7, 4, 6)[t], Z[:, 0, t, 512:1024], s_yt)
            pe.wait_ge(s_sred, 48)
            pe.wait_ge(s_wp, 32)

            def merge(t):
                pe.wait_ge(s_ytea, t + 1)
                for half in range(2):
                    n = 2 * t + half
                    need(pe, s_m, n - 1)
                    for r, w in enumerate((WPA, WPB)):
                        for k in range(4):
                            ins = mm(PS[:, 2 * half + r, :], YT[:, 4 * r + k, P * t:P * t + P],
                                     w[:, k, 512 * half:512 * half + 512], start=k == 0, stop=k == 3)
                    ins.then_inc(s_u, 1)

            def turn_m(t):
                if t == 0:
                    pe.wait_ge(s_ytea, 4)
                pe.wait_ge(s_m, 2 * t + 2)
                for half in range(2):
                    need(pe, s_mte, 2 * t + half - 3)
                    turn(4 + (2 * t + half) % 4, G[:, 0, t, 512 * half:512 * half + 512], s_mt)
            merge(0)
            for t in range(1, NT):
                merge(t)
                turn_m(t - 1)
            pe.wait_ge(s_wo, 16)

            def turn_h2(t):
                pe.wait_ge(s_h2, t + 1)
                for half in range(2):
                    need(pe, s_h2te, 2 * t + half - 3)
                    turn(4 + (2 * t + half) % 4, HROW[:, t % 2, 512 * half:512 * half + 512], s_h2t)
            for n in range(8):
                t, half = n // 2, n % 2
                if half == 0:
                    pe.wait_ge(s_mte, 2 * t + 2)
                pe.wait_ge(s_m, 7 if n < 2 else 8)
                need(pe, s_x2, n - 3)
                for k in range(KD):
                    ins = mm(PS[:, n % 4, :], MT[:, k, P * t:P * t + P], WO[:, k, 512 * half:512 * half + 512],
                             start=k == 0, stop=k == KD - 1)
                ins.then_inc(s_o, 1)
                if n == 0:
                    turn_m(NT - 1)
                if half and t >= 2:
                    turn_h2(t - 2)
            def shared_gate_up(t):
                need(pe, s_x2, 5 + t)
                for k in range(KD):
                    ins = mm(PS[:, t, :], H2T[:, k, P * t:P * t + P], WSGU[:, k, :], start=k == 0, stop=k == KD - 1)
                ins.then_inc(s_sgu, 1)

            pe.wait_ge(s_h2te, 4)
            pe.wait_ge(s_ws, 64)
            shared_gate_up(0)
            turn_h2(2)
            turn_h2(3)
            pe.wait_ge(s_h2te, 8)
            for k in range(KD):
                ins = mm(PS[0:E, 4, :], WRT[:, k, :], H2T[:, k, :], start=k == 0, stop=k == KD - 1)
            ins.then_inc(s_rt, 1)
            pe.wait_ge(s_sct, 1)
            for t in range(NT):
                ins = pe.transpose(PS[:, 5, E * t:E * t + E], SCT[:, P * t:P * t + P], ident[0:E, 0:E])
            ins.then_inc(s_sc, 1)
            shared_gate_up(1)
            shared_gate_up(2)
            pe.wait_ge(s_sel, 1)
            for t in range(NT):
                for j in range(t + 1):
                    mm(PS[:, 4, E * t:E * t + E], cst[:, C_TEX:C_TEX + P] if j == t else ones, SEL[:, j, :],
                       start=j == 0, stop=j == t)
            for j in range(NT):
                ins = mm(PS[0:E, 4, 256:257], SEL[:, j, :], ones[:, 0:1], start=j == 0, stop=j == NT - 1)
            ins.then_inc(s_pos, 1)
            pe.wait_ge(s_ob, 1)
            mm(PS[0:E, 7, 0:1], cst[0:E, C_TIN:C_TIN + E], ob[:, 3:4], start=True, stop=True).then_inc(s_oend, 1)
            pe.wait_ge(s_q1, 1)
            for bank, src in ((5, Q1), (6, WT)):
                for t in range(NT):
                    ins = pe.transpose(PS[0:E, bank, P * t:P * t + P], src[:, t, :], ident)
                ins.then_inc(s_tr, 1)
            shared_gate_up(3)

            def shared_turn(t):
                pe.wait_ge(s_sact, t + 1)
                need(pe, s_sate, t)
                for k in range(2):
                    ins = pe.transpose(PS[:, 6, P * k:P * k + P], ACTS[:, t, P * k:P * k + P], ident)
                ins.then_inc(s_sat, 1)

            def shared_down(t):
                pe.wait_ge(s_sate, t + 1)
                for half in range(2):
                    if t > 1:
                        pe.wait_ge(s_sx, (3, 5)[t - 2] + half)
                    for k in range(2):
                        ins = mm(PS[:, (0 if t == 1 else 2) + half, :], AT[:, t % 2, k, :], WSD[:, k, 512 * half:512 * half + 512],
                                 start=k == 0, stop=k == 1)
                    ins.then_inc(s_sdn, 1)

            pe.wait_ge(s_trd, 2)
            shared_turn(0)
            pe.wait_ge(s_oh1, 1)
            for t in range(NT):
                at = NEXT * t
                mm(PS[:, 4, at:at + NEXT], Q1T[:, P * t:P * t + P], OH[:, 0, :], start=True, stop=False)
                mm(PS[:, 4, at:at + NEXT], cst[0:E, C_NEG1:C_NEG1 + P], OH[:, 1, :], start=False, stop=True)
                mm(PS[:, 4, 144 + at:144 + at + NEXT], WTT[:, P * t:P * t + P], OH[:, 0, :], start=True, stop=True)
            mm(PS[0:1, 4, 432:468], cst[0:E, C_E:C_E + 1], OH[:, 0, :], start=True, stop=True)
            mm(PS[0:1, 4, 468:469], ob[:, 3:4], ones[0:E, 0:1], start=True, stop=True).then_inc(s_xm, 1)

            def slot_rows(j, b):
                pe.wait_ge(s_ah, j + 1)
                need(pe, s_sl, SLN * j)
                for t in range(NT):
                    ins = mm(PS[:, 7, 0:NCOL], AH[:, b, t, :], RX[:, bass.ds(j, 1), t, :].rearrange("p o c -> p (o c)"),
                             start=t == 0, stop=t == NT - 1)
                ins.then_inc(s_ohd, 1)

            def turn_x(i, j, b):
                pe.wait_ge(s_gat[b], 16 * (i + 1))
                need(pe, s_xtd, j)
                need(pe, s_xta, j)
                for half in range(2):
                    for k in range(4):
                        ins = pe.transpose(PS[:, 4 + half, P * k:P * k + P],
                                           XG[:, b, 512 * half + P * k:512 * half + P * k + P], ident)
                ins.then_inc(s_xt, 1)

            def gate_up(i, j, b):
                pe.wait_ge(s_xtd, j + 1)
                pe.wait_ge(s_xta, j + 1)
                pe.wait_ge(s_wgu[b], 32 * (i + 1))
                need(pe, s_act, j - 1)
                for k in range(KD):
                    ins = mm(PS[:, b, :], XT[:, b, k, :], WGU[b][:, k, :], start=k == 0, stop=k == KD - 1)
                ins.then_inc(s_gu, 1)

            def turn_act(j, b):
                pe.wait_ge(s_act, j + 1)
                need(pe, s_ate, j)
                for k in range(2):
                    ins = pe.transpose(PS[:, 6, P * k:P * k + P], AR[:, b, P * k:P * k + P], ident)
                ins.then_inc(s_at, 1)

            def down(i, j, b):
                pe.wait_ge(s_ate, j + 1)
                pe.wait_ge(s_wd[b], 16 * (i + 1))
                for half in range(2):
                    need(pe, s_oe, 2 * j - 1 + half)
                    for k in range(2):
                        ins = mm(PS[:, 2 + half, :], AT[:, b, k, :], WDN[b][:, k, 512 * half:512 * half + 512],
                                 start=k == 0, stop=k == 1)
                    ins.then_inc(s_dn, 1)

            pe.wait_ge(s_sact, 4)
            shared_turn(1)
            shared_down(0)
            pe.wait_ge(s_tabs, 1)
            slot_rows(0, 0)
            shared_turn(2)
            slot_rows(1, 1)
            shared_down(1)
            turn_x(0, 0, 0)
            turn_x(0, 1, 1)
            pe.wait_ge(s_sx, 2)
            gate_up(0, 0, 0)
            shared_turn(3)
            slot_rows(2, 0)
            nblk = pe.value_load(nover[0:1, 0:1], min_val=0, max_val=31) + E

            def step(i, b, more):
                j = 2 * i + b
                with more(pe, j + 1):
                    gate_up(i + b, j + 1, 1 - b)
                if isinstance(j, int) and j == 0:
                    shared_down(2)
                    slot_rows(3, 1)
                    shared_down(3)
                turn_act(j, b)
                turn_x(i + 1, j + 2, b)
                slot_rows(j + 4, b)
                if isinstance(j, int) and j == 0:
                    pe.wait_ge(s_sx, 8)
                down(i, j, b)

            def pair(i):
                for b in range(2):
                    step(i, b, always)
            pair(0)
            with pe.Fori(1, PAIRS - 1) as i:
                pair(i)

            def if_block(eng, j):
                return eng.If(j < nblk)
            step(PAIRS - 1, 0, always)
            step(PAIRS - 1, 1, if_block)
            overflow_blocks(pe, nblk, lambda i, b: step(i, b, if_block))


_INS = ["x", "c", "ada_w", "ada_b", "mix_norm_g", "w_in", "b_fgate", "qn_a", "kn_a", "qn_b", "kn_b", "rel_bias",
        "w_proj_a", "w_proj_b", "w_out", "ffn_norm_g", "w_router", "router_bias", "w_gate_e", "w_up_e", "w_down_e",
        "w_gate_s", "w_up_s", "w_down_s"]


def kernel(**inputs):
    import concourse.bacc as bacc
    from concourse.bass_utils import run_bass_kernel_spmd

    nc = bacc.Bacc("TRN2", target_bir_lowering=False, num_devices=1)
    arrays, aps = {}, {}

    def give(name, array):
        arrays[name] = array
        aps[name] = nc.dram_tensor(name, array.shape, mybir.dt.from_np(array.dtype), kind="ExternalInput").ap()

    for name in _INS:
        array = np.ascontiguousarray(inputs[name])
        give(name, array if name == "c" else array.reshape(array.shape[1:]))
    for name, array in zip(("consts", "causal", "etab"), constants()):
        give(name, array)
    aps["out"] = nc.dram_tensor("out", (S, D), mybir.dt.float32, kind="ExternalOutput").ap()
    build(nc, aps)
    r = run_bass_kernel_spmd(nc, [arrays], core_ids=[0])
    return r.results[0]["out"].reshape(1, S, D)
```
